# Optimizing a Trainium2 kernel written in Bass

```python
import jax, jax.numpy as jnp
from jax import lax
import numpy as np

D_MODEL = 1024
BATCH = 1
SEQ = 1024
DEPTH = 1

HEAD_DIM = 64
SB_HEADS = 8
SWA_HEADS = 8
SWA_KV_HEADS = 2
SWA_GROUP = SWA_HEADS // SWA_KV_HEADS
D_SB = SB_HEADS * HEAD_DIM
D_SWA = SWA_HEADS * HEAD_DIM
D_SWA_KV = SWA_KV_HEADS * HEAD_DIM
D_MIX = D_SB + D_SWA
D_IN = 3 * D_SB + D_SWA + 2 * D_SWA_KV
Q_BLOCK = 128
WINDOW = 128
PEER_HEADS = 8
N_KEYS = 128
N_EXPERTS = N_KEYS * N_KEYS
PEER_TOPK = 16
D_KEY = 256
D_HALF = D_KEY // 2
TOKEN_CHUNK = 128
EPS = 1e-6

kernel_name = "hybrid_stickbreak_swa_peer_block"

def rmsnorm(x, g):
    xf = x.astype(jnp.float32)
    y = xf * lax.rsqrt(jnp.mean(xf * xf, axis=-1, keepdims=True) + EPS)
    return (y * g.astype(jnp.float32)).astype(x.dtype)

def head_rmsnorm(o, g, n_heads):
    B, S, _ = o.shape
    of = o.reshape(B, S, n_heads, HEAD_DIM).astype(jnp.float32)
    y = of * lax.rsqrt(jnp.mean(of * of, axis=-1, keepdims=True) + EPS)
    y = y * g.reshape(n_heads, HEAD_DIM).astype(jnp.float32)
    return y.reshape(B, S, n_heads * HEAD_DIM).astype(o.dtype)

def alibi_slopes(n_heads):
    return jnp.exp2(-8.0 * jnp.arange(1, n_heads + 1, dtype=jnp.float32) / n_heads)

def stick_breaking_attention(q, k, v):
    B, S, H, Dh = q.shape
    nblk = S // Q_BLOCK
    scale = Dh ** -0.5
    qb = q.reshape(B, nblk, Q_BLOCK, H, Dh).transpose(1, 0, 3, 2, 4)
    kh = k.transpose(0, 2, 1, 3)
    vh = v.transpose(0, 2, 1, 3)
    key_pos = jnp.arange(S)

    def block(args):
        qi, i = args
        z = jnp.einsum('bhqd,bhkd->bhqk', qi, kh, preferred_element_type=jnp.float32) * scale
        q_pos = i * Q_BLOCK + jnp.arange(Q_BLOCK)
        mask = key_pos[None, :] < q_pos[:, None]
        log_1m = jnp.where(mask, jax.nn.log_sigmoid(-z), 0.0)
        later = lax.cumsum(log_1m, axis=3, reverse=True) - log_1m
        a = jnp.where(mask, jnp.exp(jax.nn.log_sigmoid(z) + later), 0.0)
        return jnp.einsum('bhqk,bhkd->bhqd', a.astype(vh.dtype), vh)

    out = lax.map(block, (qb, jnp.arange(nblk)))
    return out.transpose(1, 0, 3, 2, 4).reshape(B, S, H * Dh)

def sliding_window_attention(q, k, v, sinks):
    B, S, H, Dh = q.shape
    KV = k.shape[2]
    G = H // KV
    n = S // Q_BLOCK
    qb = q.reshape(B, n, Q_BLOCK, KV, G, Dh)

    def with_prev(t):
        tb = t.reshape(B, n, Q_BLOCK, KV, Dh)
        prev = jnp.pad(tb[:, :-1], ((0, 0), (1, 0), (0, 0), (0, 0), (0, 0)))
        return jnp.concatenate([prev, tb], axis=2)

    kb, vb = with_prev(k), with_prev(v)
    s = jnp.einsum('bnqkgd,bnskd->bnkgqs', qb, kb, preferred_element_type=jnp.float32) * Dh ** -0.5
    dist = jnp.arange(Q_BLOCK)[:, None] + Q_BLOCK - jnp.arange(2 * Q_BLOCK)[None, :]
    key_abs = jnp.arange(n)[:, None] * Q_BLOCK + jnp.arange(2 * Q_BLOCK)[None, :] - Q_BLOCK
    mask = ((dist >= 0) & (dist < WINDOW))[None, :, :] & (key_abs >= 0)[:, None, :]
    slopes = alibi_slopes(H).reshape(KV, G)
    s = s - slopes[:, :, None, None] * dist.astype(jnp.float32)
    s = jnp.where(mask[None, :, None, None, :, :], s, -jnp.inf)
    sink = jnp.broadcast_to(sinks.astype(jnp.float32).reshape(KV, G)[None, None, :, :, None, None],
                            s.shape[:-1] + (1,))
    p = jax.nn.softmax(jnp.concatenate([s, sink], axis=-1), axis=-1)[..., :-1]
    out = jnp.einsum('bnkgqs,bnskd->bnqkgd', p.astype(vb.dtype), vb)
    return out.reshape(B, S, H * Dh)

def peer_ffn(x, w_q, keys1, keys2, u, v):
    B, S, D = x.shape
    T = B * S
    xt = x.reshape(T, D)
    q = (xt @ w_q).reshape(T, PEER_HEADS, 2, D_HALF)
    s1 = jnp.einsum('thd,hnd->thn', q[:, :, 0], keys1, preferred_element_type=jnp.float32)
    s2 = jnp.einsum('thd,hnd->thn', q[:, :, 1], keys2, preferred_element_type=jnp.float32)
    v1, i1 = lax.top_k(s1, PEER_TOPK)
    v2, i2 = lax.top_k(s2, PEER_TOPK)
    cand = (v1[..., :, None] + v2[..., None, :]).reshape(T, PEER_HEADS, PEER_TOPK * PEER_TOPK)
    cand_idx = (i1[..., :, None] * N_KEYS + i2[..., None, :]).reshape(T, PEER_HEADS, PEER_TOPK * PEER_TOPK)
    top_s, pos = lax.top_k(cand, PEER_TOPK)
    idx = jnp.take_along_axis(cand_idx, pos, axis=-1)
    gate = jax.nn.softmax(top_s, axis=-1)
    nc = T // TOKEN_CHUNK

    def chunk(args):
        xc, ic, gc = args
        h = jax.nn.gelu(jnp.einsum('cd,chkd->chk', xc, u[ic]))
        return jnp.einsum('chk,chkd->cd', (gc * h).astype(v.dtype), v[ic])

    out = lax.map(chunk, (xt.reshape(nc, TOKEN_CHUNK, D),
                          idx.reshape(nc, TOKEN_CHUNK, PEER_HEADS, PEER_TOPK),
                          gate.reshape(nc, TOKEN_CHUNK, PEER_HEADS, PEER_TOPK)))
    return out.reshape(B, S, D).astype(x.dtype)

def setup_inputs(seed: int = 0) -> dict:
    key = jax.random.key(seed)
    ks = jax.random.split(key, 14)
    f32 = jnp.float32
    L = DEPTH
    return {
        "x": jax.random.normal(ks[0], (BATCH, SEQ, D_MODEL), f32),
        "norm1_g": 1.0 + 0.02 * jax.random.normal(ks[1], (L, D_MODEL), f32),
        "w_in": jax.random.normal(ks[2], (L, D_MODEL, D_IN), f32) * D_MODEL ** -0.5,
        "sb_out_g": 1.0 + 0.02 * jax.random.normal(ks[3], (L, D_SB), f32),
        "swa_out_g": 1.0 + 0.02 * jax.random.normal(ks[4], (L, D_SWA), f32),
        "swa_sinks": 0.5 * jax.random.normal(ks[5], (L, SWA_HEADS), f32),
        "w_out": jax.random.normal(ks[6], (L, D_MIX, D_MODEL), f32) * D_MIX ** -0.5,
        "norm2_g": 1.0 + 0.02 * jax.random.normal(ks[7], (L, D_MODEL), f32),
        "peer_w_q": jax.random.normal(ks[8], (L, D_MODEL, PEER_HEADS * D_KEY), f32) * D_MODEL ** -0.5,
        "peer_keys1": jax.random.normal(ks[9], (L, PEER_HEADS, N_KEYS, D_HALF), f32) * D_HALF ** -0.5,
        "peer_keys2": jax.random.normal(ks[10], (L, PEER_HEADS, N_KEYS, D_HALF), f32) * D_HALF ** -0.5,
        "peer_u": jax.random.normal(ks[11], (L, N_EXPERTS, D_MODEL), f32) * D_MODEL ** -0.5,
        "peer_v": jax.random.normal(ks[12], (L, N_EXPERTS, D_MODEL), f32) * PEER_HEADS ** -0.5,
        "final_g": 1.0 + 0.02 * jax.random.normal(ks[13], (D_MODEL,), f32),
    }

def reference(x, norm1_g, w_in, sb_out_g, swa_out_g, swa_sinks, w_out, norm2_g,
              peer_w_q, peer_keys1, peer_keys2, peer_u, peer_v, final_g):
    B, S, _ = x.shape
    splits = [D_SB, 2 * D_SB, 3 * D_SB, 3 * D_SB + D_SWA, 3 * D_SB + D_SWA + D_SWA_KV]
    for l in range(DEPTH):
        h = rmsnorm(x, norm1_g[l])
        proj = h @ w_in[l]
        sb_q, sb_k, sb_v, sw_q, sw_k, sw_v = jnp.split(proj, splits, axis=-1)
        sb = stick_breaking_attention(sb_q.reshape(B, S, SB_HEADS, HEAD_DIM),
                                      sb_k.reshape(B, S, SB_HEADS, HEAD_DIM),
                                      sb_v.reshape(B, S, SB_HEADS, HEAD_DIM))
        sw = sliding_window_attention(sw_q.reshape(B, S, SWA_HEADS, HEAD_DIM),
                                      sw_k.reshape(B, S, SWA_KV_HEADS, HEAD_DIM),
                                      sw_v.reshape(B, S, SWA_KV_HEADS, HEAD_DIM),
                                      swa_sinks[l])
        mixed = jnp.concatenate([head_rmsnorm(sb, sb_out_g[l], SB_HEADS),
                                 head_rmsnorm(sw, swa_out_g[l], SWA_HEADS)], axis=-1)
        x = x + mixed @ w_out[l]
        x = x + peer_ffn(rmsnorm(x, norm2_g[l]), peer_w_q[l], peer_keys1[l], peer_keys2[l],
                         peer_u[l], peer_v[l])
    return rmsnorm(x, final_g)


_drawn_inputs = setup_inputs


def setup_inputs(seed=0):
    import zlib

    import numpy as np

    out = dict(_drawn_inputs(seed))
    spreads = {}
    factors = {'sb_out_g': 11.541,
     'swa_out_g': 37.359,
     'swa_sinks': 64.0,
     'norm2_g': 10.44,
     'final_g': 20.702}
    for name, (base, spread) in spreads.items():
        noise = np.random.default_rng([zlib.crc32(name.encode()), seed]).standard_normal(out[name].shape)
        drawn = base * np.exp(spread * noise) if base else spread * noise
        out[name] = __import__('jax').numpy.asarray(drawn.astype(out[name].dtype))
    for name, factor in factors.items():
        out[name] = (out[name] * factor).astype(out[name].dtype)
    return out
```

```python
from contextlib import ExitStack

import concourse.bass as bass
from concourse import mybir

F32 = mybir.dt.float32
I32 = mybir.dt.int32
U32 = mybir.dt.uint32
ALU = mybir.AluOpType
ACT = mybir.ActivationFunctionType
AX = mybir.AxisListType.X

P = 128
SEQ = 1024
D = 1024
TILES = SEQ // P
CH = D // P
HALF = 512
DH = 64
HEADS = 8
D_SB = HEADS * DH
KV = 2
GRP = HEADS // KV
D_IN = 3 * D_SB + HEADS * DH + 2 * KV * DH
COLS = 256
PH = 8
NK = 128
TOPK = 16
PICKS = PH * TOPK
SIDES = 2 * PH
EPS = 1e-6
LOW = -1.0e30
LOWEST = -3.0e38
GELU_C = 0.7978845608028654
GELU_A = 0.044715


def place(h):
    return (h % 2) * (HEADS // 2) + h // 2


def place4(g):
    return (g % 2) * (GRP // 2) + g // 2


def bcast(ap, shape):
    return ap.to_broadcast(shape)


def constants(nc, ctx, sem):
    def sb(name, shape, dt=F32):
        return ctx.enter_context(nc.sbuf_tensor(name, shape, dt))

    ident = sb("ident", [P, P])
    tri = sb("tri", [P, P])
    ones = sb("ones", [P, P])
    bias = sb("bias", [P, HEADS, 2 * P])
    minus_half = sb("minus_half", [P, 2 * HEADS])
    dist_i = sb("dist_i", [P, 2 * P], I32)
    dist = sb("dist", [P, 2 * P])
    blank = sem("blank")
    made = sem("made")
    dist_ready = sem("dist_ready")
    slope_done = sem("slope_done")
    cut = sem("cut")

    with nc.Block() as block:
        @block.gpsimd
        def _(pool):
            nc.gpsimd.memset(ident[:], 0.0).then_inc(blank, 1)
            nc.gpsimd.memset(tri[:], 1.0).then_inc(blank, 1)
            nc.gpsimd.memset(ones[:], 1.0).then_inc(blank, 1)
            nc.gpsimd.memset(minus_half[:], -0.5).then_inc(blank, 1)
            nc.gpsimd.iota(dist_i[:], pattern=[[-1, 2 * P]], base=P, channel_multiplier=1).then_inc(dist_ready, 1)
            pool.wait_ge(blank, 4)
            nc.gpsimd.affine_select(out=ident[:], in_=ident[:], compare_op=ALU.not_equal, fill=1.0, base=0,
                                    pattern=[[-1, P]], channel_multiplier=1).then_inc(made, 1)
            nc.gpsimd.affine_select(out=tri[:], in_=tri[:], compare_op=ALU.is_ge, fill=0.0, base=0,
                                    pattern=[[-1, P]], channel_multiplier=1).then_inc(made, 1)
            pool.wait_ge(slope_done, HEADS)
            nc.gpsimd.affine_select(out=bias[:], in_=bias[:], compare_op=ALU.is_ge, fill=LOW, base=P,
                                    pattern=[[0, HEADS], [-1, 2 * P]], channel_multiplier=1).then_inc(cut, 1)
            pool.wait_ge(cut, 1)
            nc.gpsimd.affine_select(out=bias[:], in_=bias[:], compare_op=ALU.is_ge, fill=LOW, base=-1,
                                    pattern=[[0, HEADS], [1, 2 * P]], channel_multiplier=-1).then_inc(cut, 1)

        @block.vector
        def _(dve):
            dve.wait_ge(dist_ready, 1)
            nc.vector.tensor_copy(dist[:], dist_i[:]).then_inc(dist_ready, 1)
            dve.wait_ge(dist_ready, 2)
            for h in range(HEADS):
                at = h // GRP * GRP + place4(h % GRP)
                nc.vector.tensor_scalar(bias[:, at, :], dist[:], -(2.0 ** -(8.0 * (h + 1) / HEADS)), None,
                                        ALU.mult).then_inc(slope_done, 1)
    return ident, tri, ones, bias, minus_half


def project(nc, sem, x, norm1_g, w_in, ident, minus_half, qk_t, sb_v, wq_t, wk_t, sw_v):
    groups = D_IN // COLS
    ring = 4
    XR = 4
    w_view = w_in.rearrange("(c p) n -> p c n", p=P)
    with ExitStack() as ctx:
        xs = ctx.enter_context(nc.sbuf_tensor("pj_x", [P, XR, D], F32))
        xn = ctx.enter_context(nc.sbuf_tensor("pj_xn", [P, 2, D], F32))
        h_t = ctx.enter_context(nc.sbuf_tensor("pj_ht", [P, CH, SEQ], F32))
        w = ctx.enter_context(nc.sbuf_tensor("pj_w", [P, ring, CH, COLS], F32))
        g_t = ctx.enter_context(nc.sbuf_tensor("pj_g", [P, CH], F32))
        ss = ctx.enter_context(nc.sbuf_tensor("pj_ss", [P, TILES], F32))
        ms = ctx.enter_context(nc.sbuf_tensor("pj_ms", [P, TILES], F32))
        rstd = ctx.enter_context(nc.sbuf_tensor("pj_rstd", [P, TILES], F32))
        tp = ctx.enter_context(nc.psum_tensor("pj_tp", [P, 2, CH, P], F32))
        acc = ctx.enter_context(nc.psum_tensor("pj_acc", [P, 4, HALF], F32))

        x_in = [sem(f"pj_x_in{t}") for t in range(TILES)]
        w_loaded = [sem(f"pj_w_in{s}") for s in range(ring)]
        g_in = sem("pj_g_in")
        squared = sem("pj_squared")
        mean_done = sem("pj_mean")
        rstd_done = sem("pj_rstd_done")
        normed = sem("pj_normed")
        turned = sem("pj_turned")
        ht_ready = sem("pj_ht_ready")
        acc_full = sem("pj_acc_full")
        acc_read = sem("pj_acc_read")

        units = []
        for g in range(groups):
            for j in range(2):
                col = g * COLS + j * P
                if col < 2 * D_SB:
                    units += [(g, "t", j * P, hf, qk_t[:, col // P, hf * HALF:(hf + 1) * HALF],
                               DH ** -0.5 if col < D_SB else 1.0) for hf in range(2)]
                elif 3 * D_SB <= col < 3 * D_SB + HEADS * DH:
                    b = (col - 3 * D_SB) // P
                    units += [(g, "t", j * P, hf, wq_t[:, b, hf * HALF:(hf + 1) * HALF], DH ** -0.5)
                              for hf in range(2)]
            if 2 * D_SB <= g * COLS < 3 * D_SB:
                c0 = g * COLS - 2 * D_SB
                units += [(g, "v", (0, COLS), t, sb_v[:, t, c0:c0 + COLS], 1.0) for t in range(TILES)]
            if g == groups - 1:
                units += [(g, "k", kv * DH, hf, wk_t[:, kv, hf * HALF:(hf + 1) * HALF], 1.0)
                          for kv in range(KV) for hf in range(2)]
                units += [(g, "v", (P, P), t, sw_v[:, t, :], 1.0) for t in range(TILES)]

        ends = [1 + max(n for n, unit in enumerate(units) if unit[0] == g) for g in range(groups)]

        with nc.Block() as block:
            @block.sync
            def _(sp):
                with nc.allow_non_contiguous_dma(reason="one gain per feature, 4 KB in all"):
                    sp.dma_start(g_t[:], norm1_g.rearrange("(c p) -> p c", p=P)).then_inc(g_in, 16)
                for t in range(TILES):
                    if t >= XR:
                        sp.wait_ge(normed, t - XR + 1)
                    sp.dma_start(xs[:, t % XR, :], x[t * P:(t + 1) * P, :]).then_inc(x_in[t], 16)
                for g in range(groups):
                    if g >= ring:
                        sp.wait_ge(acc_full, ends[g - ring])
                    sp.dma_start(w[:, g % ring, :, :], w_view[:, :, g * COLS:(g + 1) * COLS]).then_inc(
                        w_loaded[g % ring], 16)

            @block.scalar
            def _(act):
                for t in range(TILES):
                    act.wait_ge(x_in[t], 16)
                    if t >= 2:
                        act.wait_ge(turned, t - 1)
                    nc.scalar.activation(xn[:, t % 2, :], xs[:, t % XR, :], ACT.Square,
                                         accum_out=ss[:, t:t + 1]).then_inc(squared, 1)
                for n, (_, _, _, _, dest, scale) in enumerate(units):
                    act.wait_ge(acc_full, n + 1)
                    width = dest.shape[-1]
                    nc.scalar.activation(dest, acc[:, n % 4, 0:width], ACT.Copy, scale=scale).then_inc(acc_read, 1)

            @block.gpsimd
            def _(pool):
                for t in range(TILES):
                    pool.wait_ge(mean_done, t + 1)
                    nc.gpsimd.tensor_tensor(rstd[:, t:t + 1], ms[:, t:t + 1], minus_half[:, 0:1], ALU.pow).then_inc(rstd_done, 1)

            @block.vector
            def _(dve):
                def evacuate(t):
                    dve.wait_ge(turned, t + 1)
                    nc.vector.tensor_tensor(h_t[:, :, t * P:(t + 1) * P], tp[:, t % 2, :, :],
                                            bcast(g_t[:, :].unsqueeze(2), [P, CH, P]), ALU.mult).then_inc(ht_ready, 1)

                dve.wait_ge(g_in, 16)
                for t in range(TILES):
                    dve.wait_ge(squared, t + 1)
                    nc.vector.tensor_scalar(ms[:, t:t + 1], ss[:, t:t + 1], 1.0 / D, EPS, ALU.mult,
                                            ALU.add).then_inc(mean_done, 1)
                    dve.wait_ge(rstd_done, t + 1)
                    nc.vector.tensor_scalar(xn[:, t % 2, :], xs[:, t % XR, :], rstd[:, t:t + 1], None,
                                            ALU.mult).then_inc(normed, 1)
                    if t >= 1:
                        evacuate(t - 1)
                evacuate(TILES - 1)

            @block.tensor
            def _(pe):
                for t in range(TILES):
                    pe.wait_ge(normed, t + 1)
                    if t >= 2:
                        pe.wait_ge(ht_ready, t - 1)
                    for c in range(CH):
                        last = nc.tensor.transpose(tp[:, t % 2, c, :], xn[:, t % 2, c * P:(c + 1) * P], ident[:])
                    last.then_inc(turned, 1)
                pe.wait_ge(ht_ready, TILES)
                for n, (g, kind, at, part, dest, _) in enumerate(units):
                    slot = w[:, g % ring, :, :]
                    if n == 0 or units[n - 1][0] != g:
                        pe.wait_ge(w_loaded[g % ring], 16 * (g // ring + 1))
                    if n >= 4:
                        pe.wait_ge(acc_read, n - 3)
                    for c in range(CH):
                        st = dict(start=c == 0, stop=c == CH - 1)
                        if kind == "v":
                            last = nc.tensor.matmul(acc[:, n % 4, 0:at[1]], h_t[:, c, part * P:(part + 1) * P],
                                                    slot[:, c, at[0]:at[0] + at[1]], **st)
                        elif kind == "t":
                            last = nc.tensor.matmul(acc[:, n % 4, :], slot[:, c, at:at + P],
                                                    h_t[:, c, part * HALF:(part + 1) * HALF], **st)
                        else:
                            for lo in (0, DH):
                                last = nc.tensor.matmul(acc[lo:lo + DH, n % 4, :], slot[:, c, at:at + DH],
                                                        h_t[:, c, part * HALF:(part + 1) * HALF], **st)
                    last.then_inc(acc_full, 1)


def stick(nc, sem, tri, ones, qk_t, sb_v, mixed):
    steps = [(i, kb) for i in range(TILES) for kb in range(i, -1, -1)]
    W = HEADS * P
    with ExitStack() as ctx:
        lsp = ctx.enter_context(nc.sbuf_tensor("st_l", [P, 2, W], F32))
        zs = ctx.enter_context(nc.sbuf_tensor("st_zs", [P, 3, W], F32))
        soft = ctx.enter_context(nc.sbuf_tensor("st_sp", [P, 3, W], F32))
        later = ctx.enter_context(nc.sbuf_tensor("st_s", [P, 2, W], F32))
        a = ctx.enter_context(nc.sbuf_tensor("st_a", [P, 2, W], F32))
        z = ctx.enter_context(nc.psum_tensor("st_z", [P, 2, W], F32))
        csum = ctx.enter_context(nc.psum_tensor("st_c", [P, W], F32))
        o = ctx.enter_context(nc.psum_tensor("st_o", [P, 2, D_SB], F32))

        z_ready = sem("st_z_ready")
        z_copied = sem("st_z_copied")
        abs_done = sem("st_abs")
        exp_done = sem("st_exp")
        log_done = sem("st_log")
        soft_done = sem("st_soft")
        soft_cut = sem("st_soft_cut")
        later_done = sem("st_later")
        sum_done = sem("st_sum")
        diff_done = sem("st_diff")
        diff_cut = sem("st_diff_cut")
        a_ready = sem("st_a_ready")
        pv_done = sem("st_pv")
        o_read = sem("st_o_read")

        def is_sum(n):
            return steps[n][1] < steps[n][0] - 1

        sums = [sum(is_sum(m) for m in range(n + 1)) for n in range(len(steps))]

        def carry_of(n):
            return later[:, n % 2, :] if is_sum(n) else soft[:, (n - 1) % 3, :]

        with nc.Block() as block:
            @block.tensor
            def _(pe):
                def scores(n):
                    i, kb = steps[n]
                    if n >= 2:
                        pe.wait_ge(z_copied, n - 1)
                    for h in range(HEADS):
                        lo = DH * (h % 2)
                        last = nc.tensor.matmul(z[:, n % 2, place(h) * P:(place(h) + 1) * P],
                                                qk_t[lo:lo + DH, HEADS // 2 + h // 2, kb * P:(kb + 1) * P],
                                                qk_t[lo:lo + DH, h // 2, i * P:(i + 1) * P], start=True, stop=True)
                    last.then_inc(z_ready, 1)

                def suffix(n):
                    i, kb = steps[n]
                    if n >= 1:
                        pe.wait_ge(diff_done, n)
                    if kb == i:
                        pe.wait_ge(soft_cut, i + 1)
                    else:
                        pe.wait_ge(soft_done, n + 1)
                        if is_sum(n):
                            pe.wait_ge(later_done, sums[n])
                    for hf in range(2):
                        cols = slice(hf * HALF, (hf + 1) * HALF)
                        last = nc.tensor.matmul(csum[:, cols], tri[:], soft[:, n % 3, cols], start=True, stop=kb == i)
                        if kb < i:
                            last = nc.tensor.matmul(csum[:, cols], ones[:], carry_of(n)[:, cols], start=False, stop=True)
                    last.then_inc(sum_done, 1)

                def values(n):
                    i, kb = steps[n]
                    pe.wait_ge(a_ready, n + 1)
                    if kb == i and i >= 2:
                        pe.wait_ge(o_read, i - 1)
                    for h in range(HEADS):
                        last = nc.tensor.matmul(o[:, i % 2, h * DH:(h + 1) * DH],
                                                a[:, n % 2, place(h) * P:(place(h) + 1) * P],
                                                sb_v[:, kb, h * DH:(h + 1) * DH],
                                                start=kb == i and h == 0, stop=kb == 0,
                                                skip_group_check=True)
                    last.then_inc(pv_done, 1)

                scores(0)
                scores(1)
                for n in range(len(steps)):
                    if n + 2 < len(steps):
                        scores(n + 2)
                    suffix(n)
                    if n >= 1:
                        values(n - 1)
                values(len(steps) - 1)

            @block.scalar
            def _(act):
                def copy(n):
                    act.wait_ge(z_ready, n + 1)
                    if n >= 3:
                        act.wait_ge(diff_done, n - 2)
                    nc.scalar.activation(zs[:, n % 3, :], z[:, n % 2, :], ACT.Copy).then_inc(z_copied, 1)

                def log_terms(n):
                    act.wait_ge(abs_done, n + 1)
                    nc.scalar.activation(lsp[:, n % 2, :], lsp[:, n % 2, :], ACT.Exp, scale=-1.0).then_inc(exp_done, 1)
                    act.wait_ge(exp_done, n + 1)
                    nc.scalar.activation(lsp[:, n % 2, :], lsp[:, n % 2, :], ACT.Ln, bias=1.0).then_inc(log_done, 1)

                def weights(n):
                    i, kb = steps[n]
                    act.wait_ge(diff_done, n + 1)
                    if kb == i:
                        act.wait_ge(diff_cut, i + 1)
                    nc.scalar.activation(a[:, n % 2, :], a[:, n % 2, :], ACT.Exp).then_inc(a_ready, 1)

                nc.scalar.preload_act_table_set("natural_log_exp_and_others")
                copy(0)
                copy(1)
                log_terms(0)
                for n in range(len(steps)):
                    if n + 2 < len(steps):
                        copy(n + 2)
                    if n + 1 < len(steps):
                        log_terms(n + 1)
                    weights(n)

            @block.vector
            def _(dve):
                def read_out(i):
                    dve.wait_ge(pv_done, (i + 1) * (i + 2) // 2)
                    nc.vector.tensor_copy(mixed[:, i, 0:D_SB], o[:, i % 2, :]).then_inc(o_read, 1)

                def magnitude(n):
                    dve.wait_ge(z_copied, n + 1)
                    if n >= 2:
                        dve.wait_ge(soft_done, n - 1)
                    nc.vector.scalar_tensor_tensor(out=lsp[:, n % 2, :], in0=zs[:, n % 3, :], scalar=-1.0,
                                                   in1=zs[:, n % 3, :], op0=ALU.mult, op1=ALU.max).then_inc(abs_done, 1)

                magnitude(0)
                magnitude(1)
                for n, (i, kb) in enumerate(steps):
                    dve.wait_ge(log_done, n + 1)
                    if n >= 2:
                        dve.wait_ge(sum_done, n - 1)
                    nc.vector.scalar_tensor_tensor(out=soft[:, n % 3, :], in0=zs[:, n % 3, :], scalar=0.0,
                                                   in1=lsp[:, n % 2, :], op0=ALU.max, op1=ALU.add).then_inc(soft_done, 1)
                    if n + 1 < len(steps) and is_sum(n + 1):
                        dve.wait_ge(soft_done, n + 1)
                        if is_sum(n):
                            dve.wait_ge(later_done, sums[n])
                        else:
                            dve.wait_ge(soft_cut, i + 1)
                        if n >= 1:
                            dve.wait_ge(sum_done, n)
                        nc.vector.tensor_tensor(later[:, (n + 1) % 2, :], carry_of(n), soft[:, n % 3, :],
                                                ALU.add).then_inc(later_done, 1)
                    if n + 2 < len(steps):
                        magnitude(n + 2)
                    dve.wait_ge(sum_done, n + 1)
                    if n >= 2:
                        dve.wait_ge(pv_done, n - 1)
                    nc.vector.tensor_tensor(a[:, n % 2, :], zs[:, n % 3, :], csum[:, :], ALU.subtract).then_inc(diff_done, 1)
                    if n >= 1 and steps[n - 1][1] == 0:
                        read_out(steps[n - 1][0])
                read_out(TILES - 1)

            @block.gpsimd
            def _(pool):
                for n, (i, kb) in enumerate(steps):
                    if kb == i:
                        pool.wait_ge(soft_done, n + 1)
                        cut = soft[:, n % 3, :].rearrange("p (h q) -> p h q", h=HEADS)
                        nc.gpsimd.affine_select(out=cut, in_=cut, compare_op=ALU.is_gt, fill=0.0, base=0,
                                                pattern=[[0, HEADS], [1, P]], channel_multiplier=-1).then_inc(soft_cut, 1)
                        pool.wait_ge(diff_done, n + 1)
                        cut = a[:, n % 2, :].rearrange("p (h q) -> p h q", h=HEADS)
                        nc.gpsimd.affine_select(out=cut, in_=cut, compare_op=ALU.is_gt, fill=LOW, base=0,
                                                pattern=[[0, HEADS], [1, P]], channel_multiplier=-1).then_inc(diff_cut, 1)


def window(nc, sem, sinks, ident, bias, wq_t, wk_t, sw_v, mixed):
    steps = [(i, kv) for i in range(TILES) for kv in range(KV)]
    with ExitStack() as ctx:
        sink_row = ctx.enter_context(nc.sbuf_tensor("wd_sink_row", [P, HEADS], F32))
        sink = ctx.enter_context(nc.sbuf_tensor("wd_sink", [P, HEADS], F32))
        p = ctx.enter_context(nc.sbuf_tensor("wd_p", [P, 2, GRP, 2 * P], F32))
        p_t = ctx.enter_context(nc.sbuf_tensor("wd_pt", [P, 2, GRP, 2, P], F32))
        top = ctx.enter_context(nc.sbuf_tensor("wd_top", [P, 4, GRP], F32))
        peak = ctx.enter_context(nc.sbuf_tensor("wd_peak", [P, 4, GRP], F32))
        neg = ctx.enter_context(nc.sbuf_tensor("wd_neg", [P, 4, GRP], F32))
        sd = ctx.enter_context(nc.sbuf_tensor("wd_sd", [P, 4, GRP], F32))
        es = ctx.enter_context(nc.sbuf_tensor("wd_es", [P, 4, GRP], F32))
        rs = ctx.enter_context(nc.sbuf_tensor("wd_rs", [P, 4, GRP], F32))
        den = ctx.enter_context(nc.sbuf_tensor("wd_den", [P, 4, GRP], F32))
        rden = ctx.enter_context(nc.sbuf_tensor("wd_rden", [P, 4, GRP], F32))
        s = ctx.enter_context(nc.psum_tensor("wd_s", [P, 2, GRP, 2 * P], F32))
        tp = ctx.enter_context(nc.psum_tensor("wd_tp", [P, GRP, 2, P], F32))
        o = ctx.enter_context(nc.psum_tensor("wd_o", [P, 2, HALF], F32))

        sink_in = sem("wd_sink_in")
        s_ready = sem("wd_s_ready")
        biased = sem("wd_biased")
        top_done = sem("wd_top_done")
        peak_done = sem("wd_peak_done")
        neg_done = sem("wd_neg_done")
        p_ready = sem("wd_p_ready")
        turned = sem("wd_turned")
        pt_ready = sem("wd_pt_ready")
        pv_done = sem("wd_pv")
        den_done = sem("wd_den_done")
        rden_done = sem("wd_rden_done")
        o_read = sem("wd_o_read")

        def first_key(i):
            return P if i == 0 else 0

        with nc.Block() as block:
            @block.sync
            def _(sp):
                sp.dma_start(sink_row[:], sinks.partition_broadcast(P)).then_inc(sink_in, 16)

            @block.tensor
            def _(pe):
                def scores(n):
                    i, kv = steps[n]
                    k0 = first_key(i)
                    if n >= 2:
                        pe.wait_ge(biased, n - 1)
                    for g in range(GRP):
                        h = kv * GRP + g
                        lo = DH * (h % 2)
                        last = nc.tensor.matmul(s[:, n % 2, place4(g), k0:2 * P], wq_t[lo:lo + DH, h // 2, i * P:(i + 1) * P],
                                                wk_t[lo:lo + DH, kv, (i - 1) * P + k0:(i + 1) * P], start=True, stop=True)
                    last.then_inc(s_ready, 1)

                def turn(n):
                    i, kv = steps[n]
                    pe.wait_ge(p_ready, n + 1)
                    if n >= 1:
                        pe.wait_ge(pt_ready, n)
                    for g in range(GRP):
                        for kb in range(first_key(i) // P, 2):
                            last = nc.tensor.transpose(tp[:, g, kb, :], p[:, n % 2, g, kb * P:(kb + 1) * P], ident[:])
                    last.then_inc(turned, 1)

                def values(n):
                    i, kv = steps[n]
                    pe.wait_ge(pt_ready, n + 1)
                    if n >= 2:
                        pe.wait_ge(o_read, n - 1)
                    for g in range(GRP):
                        k0 = first_key(i) // P
                        for kb in range(k0, 2):
                            last = nc.tensor.matmul(o[:, n % 2, g * DH:(g + 1) * DH], p_t[:, n % 2, g, kb, :],
                                                    sw_v[:, i - 1 + kb, kv * DH:(kv + 1) * DH],
                                                    start=kb == k0, stop=kb == 1)
                    last.then_inc(pv_done, 1)

                scores(0)
                for n in range(len(steps)):
                    if n + 1 < len(steps):
                        scores(n + 1)
                    turn(n)
                    if n >= 1:
                        values(n - 1)
                values(len(steps) - 1)

            @block.vector
            def _(dve):
                def soften(n):
                    i, kv = steps[n]
                    k0 = first_key(i)
                    b, st = n % 2, n % 4
                    sk = sink[:, kv * GRP:(kv + 1) * GRP]
                    dve.wait_ge(s_ready, n + 1)
                    if n >= 2:
                        dve.wait_ge(turned, n - 1)
                        dve.wait_ge(p_ready, n - 1)
                    nc.vector.tensor_tensor(p[:, b, :, k0:], s[:, b, :, k0:], bias[:, kv * GRP:(kv + 1) * GRP, k0:],
                                            ALU.add).then_inc(biased, 1)
                    dve.wait_ge(biased, n + 1)
                    nc.vector.tensor_reduce(top[:, st, :], p[:, b, :, k0:], AX, ALU.max).then_inc(top_done, 1)
                    dve.wait_ge(top_done, n + 1)
                    nc.vector.tensor_tensor(peak[:, st, :], top[:, st, :], sk, ALU.max).then_inc(peak_done, 1)
                    dve.wait_ge(peak_done, n + 1)
                    nc.vector.tensor_scalar(neg[:, st, :], peak[:, st, :], -1.0, None, ALU.mult).then_inc(neg_done, 1)
                    nc.vector.tensor_tensor(sd[:, st, :], sk, peak[:, st, :], ALU.subtract).then_inc(neg_done, 1)

                def read_t(n):
                    k0 = first_key(steps[n][0]) // P
                    dve.wait_ge(turned, n + 1)
                    if n >= 2:
                        dve.wait_ge(pv_done, n - 1)
                    nc.vector.tensor_copy(p_t[:, n % 2, :, k0:, :], tp[:, :, k0:, :]).then_inc(pt_ready, 1)

                def finish(n):
                    i, kv = steps[n]
                    b, st = n % 2, n % 4
                    dve.wait_ge(p_ready, n + 1)
                    nc.vector.tensor_tensor(den[:, st, :], rs[:, st, :], es[:, st, :], ALU.add).then_inc(den_done, 1)
                    dve.wait_ge(den_done, n + 1)
                    nc.vector.reciprocal(rden[:, st, :], den[:, st, :]).then_inc(rden_done, 1)
                    dve.wait_ge(rden_done, n + 1)
                    dve.wait_ge(pv_done, n + 1)
                    dest = mixed[:, i, D_SB + kv * GRP * DH:D_SB + (kv + 1) * GRP * DH]
                    nc.vector.tensor_tensor(dest.rearrange("p (b a d) -> p a b d", a=2, d=DH),
                                            o[:, b, 0:GRP * DH].rearrange("p (a b d) -> p a b d", a=2, d=DH),
                                            bcast(rden[:, st, :].rearrange("p (a b) -> p a b", a=2).unsqueeze(3),
                                                  [P, 2, GRP // 2, DH]), ALU.mult).then_inc(o_read, 1)

                dve.wait_ge(sink_in, 16)
                nc.vector.tensor_copy(sink[:].rearrange("p (kv a b) -> p kv a b", kv=KV, a=2),
                                      sink_row[:].rearrange("p (kv b a) -> p kv a b", kv=KV, a=2)).then_inc(sink_in, 1)
                dve.wait_ge(sink_in, 17)
                soften(0)
                for n in range(len(steps)):
                    if n + 1 < len(steps):
                        soften(n + 1)
                    read_t(n)
                    if n >= 1:
                        finish(n - 1)
                finish(len(steps) - 1)

            @block.scalar
            def _(act):
                for n, (i, kv) in enumerate(steps):
                    b, st, k0 = n % 2, n % 4, first_key(i)
                    act.wait_ge(neg_done, 2 * (n + 1))
                    if n >= 4:
                        act.wait_ge(den_done, n - 3)
                    for g in range(GRP):
                        nc.scalar.activation(p[:, b, g, k0:], p[:, b, g, k0:], ACT.Exp, bias=neg[:, st, g:g + 1],
                                             accum_out=rs[:, st, g:g + 1])
                    nc.scalar.activation(es[:, st, :], sd[:, st, :], ACT.Exp).then_inc(p_ready, 1)


def mix(nc, sem, x, sb_g, sw_g, w_out, norm2_g, ident, minus_half, mixed, x1_dram, x2_dram, x2_t):
    with ExitStack() as ctx:
        w = ctx.enter_context(nc.sbuf_tensor("mx_w", [P, CH, D], F32))
        g1 = ctx.enter_context(nc.sbuf_tensor("mx_g1", [P, D], F32))
        g2 = ctx.enter_context(nc.sbuf_tensor("mx_g2", [P, D], F32))
        xr = ctx.enter_context(nc.sbuf_tensor("mx_xr", [P, 2, D], F32))
        on = ctx.enter_context(nc.sbuf_tensor("mx_on", [P, 2, D], F32))
        m_t = ctx.enter_context(nc.sbuf_tensor("mx_mt", [P, 2, CH, P], F32))
        x1 = ctx.enter_context(nc.sbuf_tensor("mx_x1", [P, 2, D], F32))
        x2 = ctx.enter_context(nc.sbuf_tensor("mx_x2", [P, 2, D], F32))
        hs = ctx.enter_context(nc.sbuf_tensor("mx_hs", [P, 3, 2 * HEADS], F32))
        rs = ctx.enter_context(nc.sbuf_tensor("mx_rs", [P, 3, TILES], F32))
        tp1 = ctx.enter_context(nc.psum_tensor("mx_tp1", [P, CH, P], F32))
        tp2 = ctx.enter_context(nc.psum_tensor("mx_tp2", [P, CH, P], F32))
        y = ctx.enter_context(nc.psum_tensor("mx_y", [P, 2, D], F32))

        w_in_ = sem("mx_w_in")
        g_in = sem("mx_g_in")
        x_in = [sem(f"mx_x_in{s}") for s in range(2)]
        x1_out = [sem(f"mx_x1_out{s}") for s in range(2)]
        x2_out = [sem(f"mx_x2_out{s}") for s in range(2)]
        squared = sem("mx_squared")
        sums = sem("mx_sums")
        scaled = sem("mx_scaled")
        gained = sem("mx_gained")
        turned = sem("mx_turned")
        mt_ready = sem("mx_mt_ready")
        y_ready = sem("mx_y_ready")
        x1_ready = sem("mx_x1_ready")
        squared2 = sem("mx_squared2")
        head_rstd = sem("mx_head_rstd")
        mean2 = sem("mx_mean2")
        rstd2 = sem("mx_rstd2")
        scaled2 = sem("mx_scaled2")
        gained2 = sem("mx_gained2")
        turned2 = sem("mx_turned2")
        x2t_ready = sem("mx_x2t_ready")
        NH = 2 * HEADS

        with nc.Block() as block:
            def store(sp, t):
                sp.wait_ge(x1_ready, t + 1)
                sp.dma_start(x1_dram[t * P:(t + 1) * P, :], x1[:, t % 2, :]).then_inc(x1_out[t % 2], 16)
                sp.wait_ge(gained2, t + 1)
                sp.dma_start(x2_dram[t * P:(t + 1) * P, :], x2[:, t % 2, :]).then_inc(x2_out[t % 2], 16)

            @block.sync
            def _(sp):
                sp.dma_start(g1[:, 0:D_SB], sb_g.partition_broadcast(P)).then_inc(g_in, 16)
                sp.dma_start(g1[:, D_SB:D], sw_g.partition_broadcast(P)).then_inc(g_in, 16)
                sp.dma_start(g2[:], norm2_g.partition_broadcast(P)).then_inc(g_in, 16)
                sp.dma_start(w[:], w_out.rearrange("(c p) n -> p c n", p=P)).then_inc(w_in_, 16)
                for t in range(TILES):
                    if t >= 2:
                        sp.wait_ge(x1_ready, t - 1)
                    sp.dma_start(xr[:, t % 2, :], x[t * P:(t + 1) * P, :]).then_inc(x_in[t % 2], 16)
                    if t >= 1:
                        store(sp, t - 1)
                store(sp, TILES - 1)
                for s in range(2):
                    sp.wait_ge(x1_out[s], 16 * (TILES // 2))
                    sp.wait_ge(x2_out[s], 16 * (TILES // 2))

            @block.scalar
            def _(act):
                for t in range(-1, TILES + 1):
                    if t + 1 < TILES:
                        n = t + 1
                        if n >= 2:
                            act.wait_ge(turned, n - 1)
                        nc.scalar.activation(on[:, n % 2, :], mixed[:, n, :], ACT.Square).then_inc(squared, 1)
                        act.wait_ge(turned, n + 1)
                        if n >= 2:
                            act.wait_ge(y_ready, n - 1)
                        nc.scalar.activation(m_t[:, n % 2, :, :], tp1[:], ACT.Copy).then_inc(mt_ready, 1)
                    if 0 <= t < TILES:
                        act.wait_ge(x1_ready, t + 1)
                        if t >= 2:
                            act.wait_ge(turned2, t - 1)
                            act.wait_ge(x2_out[t % 2], 16 * (t // 2))
                        nc.scalar.activation(x2[:, t % 2, :], x1[:, t % 2, :], ACT.Square,
                                             accum_out=rs[:, 0, t:t + 1]).then_inc(squared2, 1)
                    if 0 <= t - 1:
                        act.wait_ge(turned2, t)
                        nc.scalar.activation(x2_t[:, :, (t - 1) * P:t * P], tp2[:], ACT.Copy).then_inc(x2t_ready, 1)

            @block.vector
            def _(dve):
                for t in range(-1, TILES):
                    if t + 1 < TILES:
                        n = t + 1
                        o3 = on[:, n % 2, :].rearrange("p (h d) -> p h d", d=DH)
                        dve.wait_ge(squared, n + 1)
                        if n >= 1:
                            dve.wait_ge(scaled, n)
                        nc.vector.tensor_reduce(hs[:, 0, :], o3, AX, ALU.add).then_inc(sums, 1)
                        dve.wait_ge(sums, 2 * n + 1)
                        nc.vector.tensor_scalar(hs[:, 1, :], hs[:, 0, :], 1.0 / DH, EPS, ALU.mult, ALU.add).then_inc(sums, 1)
                        dve.wait_ge(head_rstd, n + 1)
                        nc.vector.tensor_tensor(o3, mixed[:, n, :].rearrange("p (h d) -> p h d", d=DH),
                                                bcast(hs[:, 2, :].unsqueeze(2), [P, NH, DH]), ALU.mult).then_inc(scaled, 1)
                    if t >= 0:
                        dve.wait_ge(y_ready, t + 1)
                        dve.wait_ge(x_in[t % 2], 16 * (t // 2 + 1))
                        if t >= 2:
                            dve.wait_ge(x1_out[t % 2], 16 * (t // 2))
                            dve.wait_ge(scaled2, t - 1)
                        nc.vector.tensor_tensor(x1[:, t % 2, :], y[:, t % 2, :], xr[:, t % 2, :], ALU.add).then_inc(x1_ready, 1)
                        dve.wait_ge(squared2, t + 1)
                        nc.vector.tensor_scalar(rs[:, 1, t:t + 1], rs[:, 0, t:t + 1], 1.0 / D, EPS, ALU.mult,
                                                ALU.add).then_inc(mean2, 1)
                        dve.wait_ge(rstd2, t + 1)
                        nc.vector.tensor_scalar(x2[:, t % 2, :], x1[:, t % 2, :], rs[:, 2, t:t + 1], None,
                                                ALU.mult).then_inc(scaled2, 1)

            @block.gpsimd
            def _(pool):
                pool.wait_ge(g_in, 48)
                for t in range(-1, TILES):
                    if t + 1 < TILES:
                        n = t + 1
                        pool.wait_ge(sums, 2 * n + 2)
                        nc.gpsimd.tensor_tensor(hs[:, 2, :], hs[:, 1, :], minus_half[:], ALU.pow).then_inc(head_rstd, 1)
                        pool.wait_ge(scaled, n + 1)
                        nc.gpsimd.tensor_tensor(on[:, n % 2, :], on[:, n % 2, :], g1[:], ALU.mult).then_inc(gained, 1)
                    if t >= 0:
                        pool.wait_ge(mean2, t + 1)
                        nc.gpsimd.tensor_tensor(rs[:, 2, t:t + 1], rs[:, 1, t:t + 1], minus_half[:, 0:1],
                                                ALU.pow).then_inc(rstd2, 1)
                        pool.wait_ge(scaled2, t + 1)
                        nc.gpsimd.tensor_tensor(x2[:, t % 2, :], x2[:, t % 2, :], g2[:], ALU.mult).then_inc(gained2, 1)

            @block.tensor
            def _(pe):
                for t in range(-1, TILES + 1):
                    if 0 <= t < TILES:
                        pe.wait_ge(mt_ready, t + 1)
                        if t == 0:
                            pe.wait_ge(w_in_, 16)
                        if t >= 2:
                            pe.wait_ge(x1_ready, t - 1)
                        for c in range(CH):
                            for hf in range(2):
                                last = nc.tensor.matmul(y[:, t % 2, hf * HALF:(hf + 1) * HALF], m_t[:, t % 2, c, :],
                                                        w[:, c, hf * HALF:(hf + 1) * HALF],
                                                        start=c == 0, stop=c == CH - 1)
                        last.then_inc(y_ready, 1)
                    if t + 1 < TILES:
                        n = t + 1
                        pe.wait_ge(gained, n + 1)
                        if n >= 1:
                            pe.wait_ge(mt_ready, n)
                        for c in range(CH):
                            last = nc.tensor.transpose(tp1[:, c, :], on[:, n % 2, c * P:(c + 1) * P], ident[:])
                        last.then_inc(turned, 1)
                    if t - 1 >= 0:
                        pe.wait_ge(gained2, t)
                        if t >= 2:
                            pe.wait_ge(x2t_ready, t - 1)
                        for c in range(CH):
                            last = nc.tensor.transpose(tp2[:, c, :], x2[:, (t - 1) % 2, c * P:(c + 1) * P], ident[:])
                        last.then_inc(turned2, 1)


def key_scores(nc, sem, w_q, keys1, keys2, ident, x2_t, score_dram):
    ring = 3
    w_view = w_q.rearrange("(c p) n -> p c n", p=P)
    with ExitStack() as ctx:
        keys = ctx.enter_context(nc.sbuf_tensor("ks_keys", [P, SIDES, P], F32))
        keys_t = ctx.enter_context(nc.sbuf_tensor("ks_keys_t", [P, SIDES, NK], F32))
        w = ctx.enter_context(nc.sbuf_tensor("ks_w", [P, ring, CH, COLS], F32))
        q_t = ctx.enter_context(nc.sbuf_tensor("ks_qt", [P, 2, HALF], F32))
        out = ctx.enter_context(nc.sbuf_tensor("ks_out", [P, 4, 4, NK], F32))
        tp = ctx.enter_context(nc.psum_tensor("ks_tp", [P, 2, 4, P], F32))
        q = ctx.enter_context(nc.psum_tensor("ks_q", [P, 2, HALF], F32))
        s = ctx.enter_context(nc.psum_tensor("ks_s", [P, 2, 4, NK], F32))

        keys_in = sem("ks_keys_in")
        w_loaded = [sem(f"ks_w_in{k}") for k in range(ring)]
        turned = sem("ks_turned")
        keys_ready = sem("ks_keys_ready")
        q_ready = sem("ks_q_ready")
        qt_ready = sem("ks_qt_ready")
        s_ready = sem("ks_s_ready")
        s_read = sem("ks_s_read")
        stored = [sem(f"ks_stored{k}") for k in range(4)]
        groups = SIDES * P // COLS
        units = [(b, hf) for b in range(SIDES) for hf in range(2)]
        side_view = keys[:, :, :].rearrange("n (h s) d -> n h s d", s=2)
        score_view = score_dram.rearrange("(t p) (b n) -> p t b n", p=P, n=NK)

        with nc.Block() as block:
            @block.sync
            def _(sp):
                sp.dma_start(side_view[:, :, 0, :], keys1.rearrange("h n d -> n h d")).then_inc(keys_in, 16)
                sp.dma_start(side_view[:, :, 1, :], keys2.rearrange("h n d -> n h d")).then_inc(keys_in, 16)
                for g in range(groups):
                    if g >= ring:
                        sp.wait_ge(s_ready, 4 * (g - ring + 1))
                    sp.dma_start(w[:, g % ring, :, :], w_view[:, :, g * COLS:(g + 1) * COLS]).then_inc(
                        w_loaded[g % ring], 16)

            @block.gpsimd
            def _(pool):
                for n, (b, hf) in enumerate(units):
                    pool.wait_ge(s_read, n + 1)
                    pool.dma_start(score_view[:, 4 * hf:4 * hf + 4, b, :], out[:, n % 4, :, :]).then_inc(stored[n % 4], 16)
                for k in range(4):
                    pool.wait_ge(stored[k], 16 * (len(units) // 4))

            @block.scalar
            def _(act):
                for n in range(len(units)):
                    act.wait_ge(q_ready, n + 1)
                    if n >= 2:
                        act.wait_ge(s_ready, n - 1)
                    nc.scalar.activation(q_t[:, n % 2, :], q[:, n % 2, :], ACT.Copy).then_inc(qt_ready, 1)

            @block.vector
            def _(dve):
                for k in range(SIDES // 4):
                    dve.wait_ge(turned, k + 1)
                    nc.vector.tensor_copy(keys_t[:, 4 * k:4 * k + 4, :], tp[:, k % 2, :, :]).then_inc(keys_ready, 1)
                for n in range(len(units)):
                    dve.wait_ge(s_ready, n + 1)
                    if n >= 4:
                        dve.wait_ge(stored[n % 4], 16 * (n // 4))
                    nc.vector.tensor_copy(out[:, n % 4, :, :], s[:, n % 2, :, :]).then_inc(s_read, 1)

            @block.tensor
            def _(pe):
                pe.wait_ge(keys_in, 32)
                for k in range(SIDES // 4):
                    if k >= 2:
                        pe.wait_ge(keys_ready, k - 1)
                    for j in range(4):
                        last = nc.tensor.transpose(tp[:, k % 2, j, :], keys[:, 4 * k + j, :], ident[:])
                    last.then_inc(turned, 1)
                pe.wait_ge(keys_ready, SIDES // 4)

                def query(n):
                    b, hf = units[n]
                    g = b * P // COLS
                    if n % 4 == 0:
                        pe.wait_ge(w_loaded[g % ring], 16 * (g // ring + 1))
                    if n >= 2:
                        pe.wait_ge(qt_ready, n - 1)
                    for c in range(CH):
                        last = nc.tensor.matmul(q[:, n % 2, :], w[:, g % ring, c, (b % 2) * P:(b % 2 + 1) * P],
                                                x2_t[:, c, hf * HALF:(hf + 1) * HALF], start=c == 0, stop=c == CH - 1)
                    last.then_inc(q_ready, 1)

                def score(n):
                    b, hf = units[n]
                    pe.wait_ge(qt_ready, n + 1)
                    if n >= 2:
                        pe.wait_ge(s_read, n - 1)
                    for j in range(4):
                        last = nc.tensor.matmul(s[:, n % 2, j, :], q_t[:, n % 2, j * P:(j + 1) * P], keys_t[:, b, :],
                                                start=True, stop=True)
                    last.then_inc(s_ready, 1)

                query(0)
                for n in range(len(units)):
                    if n + 1 < len(units):
                        query(n + 1)
                    score(n)


def experts(nc, sem, ident, score_dram, x1_dram, x2_dram, peer_u, peer_v, final_g, out):
    RG = 8
    GROUPS = PICKS // RG
    score_t = score_dram.rearrange("(t p) n -> t p n", p=P)
    x1_v = x1_dram.rearrange("(t p) n -> t p n", p=P)
    x2_v = x2_dram.rearrange("(t p) n -> t p n", p=P)
    out_v = out.rearrange("(t p) n -> t p n", p=P)
    with ExitStack() as ctx:
        def sb(name, shape, dt=F32):
            return ctx.enter_context(nc.sbuf_tensor(name, shape, dt))

        u = sb("ex_u", [P, RG, D])
        v = sb("ex_v", [P, RG, D])
        diag = sb("ex_diag", [P, RG, P])
        sc = sb("ex_sc", [P, SIDES, NK])
        left = sb("ex_left", [P, SIDES, NK])
        cand = sb("ex_cand", [P, PH, TOPK, TOPK])
        cleft = sb("ex_cleft", [P, PH, TOPK, TOPK])
        half_v = sb("ex_half_v", [P, SIDES, TOPK])
        half_i = sb("ex_half_i", [P, SIDES, TOPK], U32)
        half_f = sb("ex_half_f", [P, SIDES, TOPK])
        best = sb("ex_best", [P, PH, TOPK])
        pos = sb("ex_pos", [P, PH, TOPK], U32)
        part_i = sb("ex_part_i", [P, 2, PICKS], U32)
        part_f = sb("ex_part_f", [P, 2, PICKS])
        hit = sb("ex_hit", [P, PICKS, TOPK])
        row = sb("ex_row", [P, 2, PICKS])
        index_f = sb("ex_index_f", [P, PICKS])
        index = sb("ex_index", [P, PICKS], I32)
        index_ut = sb("ex_index_ut", [P, PICKS], I32)
        index_vt = sb("ex_index_vt", [P, PICKS], I32)
        gate_e = sb("ex_gate_e", [P, PICKS])
        gates = sb("ex_gates", [P, 2, PICKS])
        gsum = sb("ex_gsum", [P, 2, PH])
        ramp_i = sb("ex_ramp_i", [P, TOPK], I32)
        ramp = sb("ex_ramp", [P, TOPK])
        index_u = sb("ex_index_u", [P, 2, RG], I32)
        index_v = sb("ex_index_v", [P, 2, RG], I32)
        zero_i = sb("ex_zero_i", [P, PICKS], I32)
        x2 = sb("ex_x2", [P, D])
        prod = sb("ex_prod", [P, D])
        dots = sb("ex_dots", [P, RG])
        hid = sb("ex_hid", [P, PICKS])
        ga = sb("ex_ga", [P, 4, PICKS])
        wt = sb("ex_wt", [P, PICKS])
        x1 = sb("ex_x1", [P, D])
        y = sb("ex_y", [P, D])
        ysq = sb("ex_ysq", [P, D])
        gf = sb("ex_gf", [P, D])
        fs = sb("ex_fs", [P, 8])
        acc = ctx.enter_context(nc.psum_tensor("ex_acc", [P, D], F32))

        setup = sem("ex_setup")
        gf_in = sem("ex_gf_in")
        sc_in = sem("ex_sc_in")
        x1_in = sem("ex_x1_in")
        x2_in = sem("ex_x2_in")
        stored = sem("ex_stored")
        u_full = [sem(f"ex_u_full{k}") for k in range(RG)]
        v_full = [sem(f"ex_v_full{k}") for k in range(RG)]
        u_free = sem("ex_u_free")
        v_free = sem("ex_v_free")
        iu_ready = sem("ex_iu_ready")
        iv_ready = sem("ex_iv_ready")
        picked = sem("ex_picked")
        index_moved = sem("ex_index_moved")
        chain = sem("ex_chain")
        dot_done = sem("ex_dot")
        hid_ready = sem("ex_hid_ready")
        act_done = sem("ex_act")
        exp_asked = sem("ex_exp_asked")
        gelu_asked = sem("ex_gelu_asked")
        gelu_done = sem("ex_gelu_done")
        wt_ready = sem("ex_wt_ready")
        diag_ready = sem("ex_diag_ready")
        y_ready = sem("ex_y_ready")
        y_squared = sem("ex_y_squared")
        root_asked = sem("ex_root_asked")
        root_done = sem("ex_root_done")
        y_free = sem("ex_y_free")
        y_done = sem("ex_y_done")
        tick = sem("ex_tick")

        def hold(engine, signal, value):
            engine.wait_ge(signal, value)
            engine.sem_inc(tick, 1)

        with nc.Block() as block:
            @block.sync
            def _(sp):
                sp.sem_inc(y_free, 1)
                sp.dma_start(gf[:], final_g.partition_broadcast(P)).then_inc(gf_in, 16)
                sp.dma_start(sc[:].rearrange("p b n -> p (b n)"), score_t[0]).then_inc(sc_in, 16)
                sp.dma_start(x2[:], x2_v[0]).then_inc(x2_in, 16)
                sp.dma_start(x1[:], x1_v[0]).then_inc(x1_in, 16)

                def load_scores(t):
                    sp.wait_ge(picked, t)
                    sp.dma_start(sc[:].rearrange("p b n -> p (b n)"), score_t[bass.ds(t, 1)].squeeze(0)).then_inc(sc_in, 16)

                def load_x2(t):
                    sp.wait_ge(hid_ready, t)
                    sp.dma_start(x2[:], x2_v[bass.ds(t, 1)].squeeze(0)).then_inc(x2_in, 16)

                def turn_over(t):
                    sp.wait_ge(y_done, t)
                    sp.dma_start(out_v[bass.ds(t - 1, 1)].squeeze(0), y[:]).then_inc(stored, 16)
                    sp.dma_start(x1[:], x1_v[bass.ds(t, 1)].squeeze(0)).then_inc(x1_in, 16)
                    sp.wait_ge(stored, 16 * t)
                    sp.sem_inc(y_free, 1)

                load_scores(1)
                load_scores(2)
                load_x2(1)
                with sp.Fori(1, TILES - 2) as t:
                    load_scores(t + 2)
                    load_x2(t + 1)
                    turn_over(t)
                load_x2(TILES - 1)
                turn_over(TILES - 2)
                turn_over(TILES - 1)
                sp.wait_ge(y_done, TILES)
                sp.dma_start(out_v[TILES - 1], y[:]).then_inc(stored, 16)
                sp.wait_ge(stored, 16 * TILES)

            @block.gpsimd
            def _(pool):
                nc.gpsimd.iota(ramp_i[:], pattern=[[1, TOPK]], base=0, channel_multiplier=0).then_inc(setup, 1)
                nc.gpsimd.memset(zero_i[:], 0).then_inc(setup, 1)
                pool.sem_inc(u_free, RG)
                pool.sem_inc(v_free, RG)
                pool.wait_ge(setup, 2)

                def gathers(t, j, half, table, ring, tile_index, stage, full, free, ready):
                    at = t * PICKS + j * RG
                    pool.wait_ge(free, at + 1)
                    nc.gpsimd.tensor_tensor(stage[:, half, :], tile_index[:, bass.ds(j * RG, RG)],
                                            zero_i[:, 0:RG], ALU.add).then_inc(ready, 1)
                    hold(pool, ready, t * GROUPS + j + 1)
                    for k in range(RG):
                        if k >= 1:
                            hold(pool, free, at + k + 1)
                        nc.gpsimd.indirect_dma_start(
                            out=ring[:, k, :], out_offset=None, in_=table,
                            in_offset=bass.IndirectOffsetOnAxis(ap=stage[:, half, k:k + 1], axis=0)).then_inc(full[k], 16)

                def copy_index(dest, source, value):
                    nc.gpsimd.tensor_tensor(dest[:], source[:], zero_i[:], ALU.add).then_inc(index_moved, 1)
                    hold(pool, index_moved, value)

                pool.wait_ge(picked, 1)
                copy_index(index_ut, index, 1)
                with pool.Fori(0, GROUPS // 2) as pair:
                    for half in range(2):
                        gathers(0, 2 * pair + half, half, peer_u, u, index_ut, index_u, u_full, u_free, iu_ready)
                with pool.Fori(0, TILES - 1) as t:
                    copy_index(index_vt, index_ut, 2 * t + 2)
                    hold(pool, picked, t + 2)
                    copy_index(index_ut, index, 2 * t + 3)
                    with pool.Fori(0, GROUPS // 2) as pair:
                        for half in range(2):
                            gathers(t, 2 * pair + half, half, peer_v, v, index_vt, index_v, v_full, v_free, iv_ready)
                            gathers(t + 1, 2 * pair + half, half, peer_u, u, index_ut, index_u, u_full, u_free, iu_ready)
                copy_index(index_vt, index_ut, 2 * TILES)
                with pool.Fori(0, GROUPS // 2) as pair:
                    for half in range(2):
                        gathers(TILES - 1, 2 * pair + half, half, peer_v, v, index_vt, index_v, v_full, v_free, iv_ready)

            @block.vector
            def _(dve):
                steps = [0]

                def link(ins, base):
                    steps[0] += 1
                    ins.then_inc(chain, 1)
                    hold(dve, chain, base + steps[0])

                def pick_half_first(t, base):
                    hold(dve, sc_in, 16 * (t + 1))
                    for b in range(SIDES):
                        nc.vector.max(half_v[:, b, 0:8], sc[:, b, :])
                    link(nc.vector.drain(), base)
                    for b in range(SIDES):
                        nc.vector.max_index(half_i[:, b, 0:8], half_v[:, b, 0:8], sc[:, b, :])
                        last = nc.vector.match_replace(left[:, b, :], half_v[:, b, 0:8], sc[:, b, :], LOWEST)
                    link(last, base)

                def pick_half_second(t, base):
                    for b in range(SIDES):
                        last = nc.vector.max(half_v[:, b, 8:16], left[:, b, :])
                    link(last, base)
                    for b in range(SIDES):
                        last = nc.vector.max_index(half_i[:, b, 8:16], half_v[:, b, 8:16], left[:, b, :])
                    link(last, base)
                    link(nc.vector.tensor_copy(half_f[:], half_i[:]), base)
                    for h in range(PH):
                        last = nc.vector.tensor_tensor(
                            cand[:, h, :, :], bcast(half_v[:, 2 * h, :].unsqueeze(2), [P, TOPK, TOPK]),
                            bcast(half_v[:, 2 * h + 1, :].unsqueeze(1), [P, TOPK, TOPK]), ALU.add)
                    link(last, base)

                flat = [cand[:, h, :, :].rearrange("p a b -> p (a b)") for h in range(PH)]
                g3 = gate_e[:].rearrange("p (h k) -> p h k", h=PH)
                flat2 = [cleft[:, h, :, :].rearrange("p a b -> p (a b)") for h in range(PH)]

                def pick_first(t, base):
                    for h in range(PH):
                        last = nc.vector.max(best[:, h, 0:8], flat[h])
                    link(last, base)
                    for h in range(PH):
                        nc.vector.max_index(pos[:, h, 0:8], best[:, h, 0:8], flat[h])
                        last = nc.vector.match_replace(flat2[h], best[:, h, 0:8], flat[h], LOWEST)
                    link(last, base)

                def pick_second(t, base):
                    for h in range(PH):
                        last = nc.vector.max(best[:, h, 8:16], flat2[h])
                    link(last, base)
                    for h in range(PH):
                        last = nc.vector.max_index(pos[:, h, 8:16], best[:, h, 8:16], flat2[h])
                    link(last, base)
                    pos_flat = pos[:].rearrange("p h k -> p (h k)")
                    nc.vector.tensor_scalar(part_i[:, 0, :], pos_flat, 4, None, ALU.logical_shift_right)
                    link(nc.vector.tensor_scalar(part_i[:, 1, :], pos_flat, 15, None, ALU.bitwise_and), base)
                    link(nc.vector.tensor_copy(part_f[:], part_i[:]), base)

                    nc.vector.tensor_tensor(g3, best[:], bcast(best[:, :, 0:1], [P, PH, TOPK]),
                                            ALU.subtract).then_inc(exp_asked, 1)

                def pick_rows(side, base):
                    halves = half_f[:].rearrange("p (h s) k -> p s h k", s=2)
                    link(nc.vector.tensor_tensor(hit[:], bcast(part_f[:, side, :].unsqueeze(2), [P, PICKS, TOPK]),
                                                 bcast(ramp[:].unsqueeze(1), [P, PICKS, TOPK]), ALU.is_equal), base)
                    for h in range(PH):
                        hh = hit[:, h * TOPK:(h + 1) * TOPK, :]
                        last = nc.vector.tensor_tensor(hh, hh, bcast(halves[:, side, h, :].unsqueeze(1),
                                                                     [P, TOPK, TOPK]), ALU.mult)
                    link(last, base)
                    link(nc.vector.tensor_reduce(row[:, side, :], hit[:], AX, ALU.add), base)

                def pick_gates(t, base):
                    link(nc.vector.scalar_tensor_tensor(out=index_f[:], in0=row[:, 0, :], scalar=float(NK),
                                                        in1=row[:, 1, :], op0=ALU.mult, op1=ALU.add), base)
                    if not isinstance(t, int):
                        hold(dve, index_moved, 2 * t - 1)
                    elif t >= 1:
                        dve.wait_ge(index_moved, 2 * t - 1)
                    link(nc.vector.tensor_copy(index[:], index_f[:]), base)
                    hold(dve, act_done, t + 1)
                    link(nc.vector.tensor_reduce(gsum[:, 0, :], g3, AX, ALU.add), base)
                    link(nc.vector.reciprocal(gsum[:, 1, :], gsum[:, 0, :]), base)
                    link(nc.vector.tensor_tensor(
                        gates[:, bass.ds(t % 2, 1), :].rearrange("p one (h k) -> p (one h) k", h=PH), g3,
                        bcast(gsum[:, 1, :].unsqueeze(2), [P, PH, TOPK]), ALU.mult), base)
                    dve.sem_inc(picked, 1)

                def dot_group(t, j):
                    at = t * PICKS + j * RG
                    for k in range(RG):
                        dve.wait_ge(u_full[k], 16 * (t * GROUPS + j + 1))
                        nc.vector.tensor_tensor_reduce(out=prod[:], in0=u[:, k, :], in1=x2[:], scale=1.0, scalar=0.0,
                                                       op0=ALU.mult, op1=ALU.add,
                                                       accum_out=dots[:, k:k + 1]).then_inc(u_free, 1)
                        dve.wait_ge(u_free, at + RG + k + 1)
                    nc.vector.tensor_copy(hid[:, bass.ds(j * RG, RG)], dots[:]).then_inc(dot_done, 1)
                    hold(dve, dot_done, t * GROUPS + j + 1)

                def weigh(t, base, has_prev):
                    nc.vector.tensor_tensor(ga[:, 0, :], hid[:], hid[:], ALU.mult).then_inc(hid_ready, 1)
                    dve.wait_ge(hid_ready, t + 1)
                    link(nc.vector.tensor_scalar(ga[:, 1, :], ga[:, 0, :], GELU_A, 1.0, ALU.mult, ALU.add), base)
                    link(nc.vector.tensor_tensor(ga[:, 0, :], ga[:, 1, :], hid[:], ALU.mult), base)
                    nc.vector.tensor_scalar(ga[:, 2, :], ga[:, 0, :], -50.0, None, ALU.max).then_inc(gelu_asked, 1)
                    dve.wait_ge(gelu_done, t + 1)
                    link(nc.vector.tensor_scalar(ga[:, 1, :], ga[:, 3, :], 1.0, None, ALU.add), base)
                    link(nc.vector.reciprocal(ga[:, 0, :], ga[:, 1, :]), base)
                    link(nc.vector.tensor_tensor(ga[:, 1, :], ga[:, 0, :], hid[:], ALU.mult), base)
                    if has_prev:
                        hold(dve, diag_ready, t * PICKS)
                    link(nc.vector.tensor_tensor(wt[:], ga[:, 1, :], gates[:, bass.ds(t % 2, 1), :].squeeze(1), ALU.mult), base)
                    dve.sem_inc(wt_ready, 1)

                def finish(t, base):
                    dve.wait_ge(v_free, (t + 1) * PICKS + RG)
                    dve.wait_ge(x1_in, 16 * (t + 1))
                    dve.wait_ge(y_free, t + 1)
                    nc.vector.tensor_tensor(y[:], acc[:], x1[:], ALU.add).then_inc(y_ready, 1)
                    dve.wait_ge(y_squared, t + 1)
                    nc.vector.tensor_scalar(fs[:, 1:2], fs[:, 0:1], 1.0 / D, EPS, ALU.mult, ALU.add).then_inc(root_asked, 1)
                    dve.wait_ge(root_done, 2 * (t + 1))
                    link(nc.vector.tensor_tensor(fs[:, 4:5], fs[:, 3:4], fs[:, 1:2], ALU.mult), base)
                    link(nc.vector.tensor_tensor(fs[:, 5:6], fs[:, 4:5], fs[:, 3:4], ALU.mult), base)
                    link(nc.vector.tensor_scalar(fs[:, 6:7], fs[:, 5:6], -0.5, 1.5, ALU.mult, ALU.add), base)
                    link(nc.vector.tensor_tensor(fs[:, 7:8], fs[:, 6:7], fs[:, 3:4], ALU.mult), base)
                    link(nc.vector.tensor_scalar(y[:], y[:], fs[:, 7:8], None, ALU.mult), base)
                    nc.vector.tensor_tensor(y[:], y[:], gf[:], ALU.mult).then_inc(y_done, 1)

                dve.wait_ge(setup, 2)
                nc.vector.tensor_copy(ramp[:], ramp_i[:]).then_inc(setup, 1)
                dve.wait_ge(setup, 3)
                dve.wait_ge(gf_in, 16)

                def dot_pair(t, pair):
                    for half in range(2):
                        dot_group(t, 2 * pair + half)

                def tile(t, base, last_tile, has_prev):
                    hold(dve, x2_in, 16 * (t + 1))
                    if last_tile:
                        with dve.Fori(0, GROUPS // 2) as pair:
                            dot_pair(t, pair)
                    else:
                        dot_pair(t, 0)
                        pick_half_first(t + 1, base)
                        dot_pair(t, 1)
                        pick_half_second(t + 1, base)
                        dot_pair(t, 2)
                        pick_first(t + 1, base)
                        dot_pair(t, 3)
                        pick_second(t + 1, base)
                        dot_pair(t, 4)
                        pick_rows(0, base)
                        dot_pair(t, 5)
                        pick_rows(1, base)
                        dot_pair(t, 6)
                        pick_gates(t + 1, base)
                        dot_pair(t, 7)
                    weigh(t, base, has_prev)
                    if has_prev:
                        finish(t - 1, base)

                pick_half_first(0, 0)
                pick_half_second(0, 0)
                pick_first(0, 0)
                pick_second(0, 0)
                pick_rows(0, 0)
                pick_rows(1, 0)
                pick_gates(0, 0)
                tile(0, 0, False, False)
                after_first = steps[0]
                steps[0] = 0
                probe = len_of_tile()
                with dve.Fori(1, TILES - 1) as t:
                    tile(t, (t - 1) * probe + after_first, False, True)
                assert steps[0] == probe
                steps[0] = 0
                base = after_first + (TILES - 2) * probe
                tile(TILES - 1, base, True, True)
                finish(TILES - 1, base)

            @block.scalar
            def _(act):
                def gate_exp(t):
                    act.wait_ge(exp_asked, t + 1)
                    nc.scalar.activation(gate_e[:], gate_e[:], ACT.Exp).then_inc(act_done, 1)

                def gelu_exp(t):
                    act.wait_ge(gelu_asked, t + 1)
                    nc.scalar.activation(ga[:, 3, :], ga[:, 2, :], ACT.Exp, scale=-2.0 * GELU_C).then_inc(gelu_done, 1)

                def square(t):
                    act.wait_ge(y_ready, t + 1)
                    nc.scalar.activation(ysq[:], y[:], ACT.Square, accum_out=fs[:, 0:1]).then_inc(y_squared, 1)
                    act.wait_ge(root_asked, t + 1)
                    nc.scalar.activation(fs[:, 2:3], fs[:, 1:2], ACT.Ln).then_inc(root_done, 1)
                    act.wait_ge(root_done, 2 * t + 1)
                    nc.scalar.activation(fs[:, 3:4], fs[:, 2:3], ACT.Exp, scale=-0.5).then_inc(root_done, 1)

                def diagonals(t, first, last):
                    with act.Fori(first, last) as j:
                        at = t * PICKS + j * RG
                        for k in range(RG):
                            act.wait_ge(v_free, at + k + 1)
                            nc.scalar.activation(diag[:, k, :], ident[:], ACT.Copy,
                                                 scale=wt[:, bass.ds(j * RG + k, 1)]).then_inc(diag_ready, 1)

                def tile(t, last_pick, has_prev):
                    gelu_exp(t)
                    if has_prev:
                        square(t - 1)
                    act.wait_ge(wt_ready, t + 1)
                    diagonals(t, 0, ASKED)
                    if not last_pick:
                        gate_exp(t + 2)
                    diagonals(t, ASKED, GROUPS)

                ASKED = GROUPS // 2 + 2
                gate_exp(0)
                gate_exp(1)
                tile(0, False, False)
                with act.Fori(1, TILES - 2) as t:
                    tile(t, False, True)
                tile(TILES - 2, True, True)
                tile(TILES - 1, True, True)
                square(TILES - 1)

            @block.tensor
            def _(pe):
                def group(t, j, first, last):
                    at = t * PICKS + j * RG
                    for k in range(RG):
                        pe.wait_ge(v_full[k], 16 * (t * GROUPS + j + 1))
                        pe.wait_ge(diag_ready, at + k + 1)
                        for hf in range(2):
                            ins = nc.tensor.matmul(acc[:, hf * HALF:(hf + 1) * HALF], diag[:, k, :],
                                                   v[:, k, hf * HALF:(hf + 1) * HALF],
                                                   start=first and k == 0, stop=last and k == RG - 1)
                        ins.then_inc(v_free, 1)

                def tile(t):
                    group(t, 0, True, False)
                    with pe.Fori(1, GROUPS - 1) as j:
                        group(t, j, False, False)
                    group(t, GROUPS - 1, False, True)

                tile(0)
                with pe.Fori(1, TILES) as t:
                    pe.wait_ge(y_ready, t)
                    tile(t)


def len_of_tile():
    return 6 + 5 + (10 + 2 + 2 * 3 + 2 + 3)


def build(nc, x, norm1_g, w_in, sb_out_g, swa_out_g, swa_sinks, w_out, norm2_g, peer_w_q, peer_keys1, peer_keys2,
          peer_u, peer_v, final_g, out):
    x1_dram = nc.dram_tensor("x1_scratch", (SEQ, D), F32, kind="Internal").ap()
    x2_dram = nc.dram_tensor("x2_scratch", (SEQ, D), F32, kind="Internal").ap()
    score_dram = nc.dram_tensor("score_scratch", (SEQ, SIDES * NK), F32, kind="Internal").ap()
    with ExitStack() as ctx:
        def sem(name):
            return ctx.enter_context(nc.semaphore(name))

        ident, tri, ones, bias, minus_half = constants(nc, ctx, sem)
        with ExitStack() as held:
            mixed = held.enter_context(nc.sbuf_tensor("mixed", [P, TILES, D], F32))
            with ExitStack() as heads:
                def hb(name, shape):
                    return heads.enter_context(nc.sbuf_tensor(name, shape, F32))

                qk_t = hb("qk_t", [P, HEADS, SEQ])
                sb_v = hb("sb_v", [P, TILES, D_SB])
                wq_t = hb("wq_t", [P, HEADS // 2, SEQ])
                wk_t = hb("wk_t", [P, KV, SEQ])
                sw_v = hb("sw_v", [P, TILES, KV * DH])
                project(nc, sem, x, norm1_g, w_in, ident, minus_half, qk_t, sb_v, wq_t, wk_t, sw_v)
                stick(nc, sem, tri, ones, qk_t, sb_v, mixed)
                window(nc, sem, swa_sinks, ident, bias, wq_t, wk_t, sw_v, mixed)
            x2_t = held.enter_context(nc.sbuf_tensor("x2_t", [P, CH, SEQ], F32))
            mix(nc, sem, x, sb_out_g, swa_out_g, w_out, norm2_g, ident, minus_half, mixed, x1_dram, x2_dram, x2_t)
            key_scores(nc, sem, peer_w_q, peer_keys1, peer_keys2, ident, x2_t, score_dram)
        experts(nc, sem, ident, score_dram, x1_dram, x2_dram, peer_u, peer_v, final_g, out)


_INS = ["x", "norm1_g", "w_in", "sb_out_g", "swa_out_g", "swa_sinks", "w_out", "norm2_g", "peer_w_q", "peer_keys1",
        "peer_keys2", "peer_u", "peer_v", "final_g"]


def kernel(**inputs):
    import numpy as _np
    import concourse.bacc as _bacc
    from concourse import mybir as _mybir
    from concourse.bass_utils import run_bass_kernel_spmd as _run

    nc = _bacc.Bacc("TRN2", target_bir_lowering=False, num_devices=1)
    arrays, args = {}, []
    for name in _INS:
        a = _np.ascontiguousarray(inputs[name])
        if name != "final_g":
            a = a[0]
        arrays[f"in_{name}"] = a
        args.append(nc.dram_tensor(f"in_{name}", a.shape, _mybir.dt.from_np(a.dtype), kind="ExternalInput").ap())
    result = nc.dram_tensor("out_0", (SEQ, D), _mybir.dt.float32, kind="ExternalOutput").ap()
    build(nc, *args, result)
    r = _run(nc, [arrays], core_ids=[0])
    return r.results[0]["out_0"].reshape(1, SEQ, D)
```

```python
from contextlib import ExitStack

import concourse.bass as bass
from concourse import mybir

F32 = mybir.dt.float32
I32 = mybir.dt.int32
U32 = mybir.dt.uint32
ALU = mybir.AluOpType
ACT = mybir.ActivationFunctionType
AX = mybir.AxisListType.X

P = 128
SEQ = 1024
D = 1024
TILES = SEQ // P
CH = D // P
HALF = 512
DH = 64
HEADS = 8
D_SB = HEADS * DH
KV = 2
GRP = HEADS // KV
D_IN = 3 * D_SB + HEADS * DH + 2 * KV * DH
COLS = 256
PH = 8
NK = 128
TOPK = 16
PICKS = PH * TOPK
SIDES = 2 * PH
EPS = 1e-6
LOW = -1.0e30
EARLY = 2
LOWEST = -3.0e38
GELU_C = 0.7978845608028654
GELU_A = 0.044715


def place(h):
    return (h % 2) * (HEADS // 2) + h // 2


def place4(g):
    return (g % 2) * (GRP // 2) + g // 2


def bcast(ap, shape):
    return ap.to_broadcast(shape)


def constants(nc, ctx, sem):
    def sb(name, shape, dt=F32):
        return ctx.enter_context(nc.sbuf_tensor(name, shape, dt))

    ident = sb("ident", [P, P])
    tri = sb("tri", [P, P])
    ones = sb("ones", [P, P])
    bias = sb("bias", [P, HEADS, 2 * P])
    minus_half = sb("minus_half", [P, 2 * HEADS])
    dist_i = sb("dist_i", [P, 2 * P], I32)
    dist = sb("dist", [P, 2 * P])
    blank = sem("blank")
    made = sem("made")
    dist_ready = sem("dist_ready")
    slope_done = sem("slope_done")
    cut = sem("cut")

    with nc.Block() as block:
        @block.gpsimd
        def _(pool):
            nc.gpsimd.memset(ident[:], 0.0).then_inc(blank, 1)
            nc.gpsimd.memset(tri[:], 1.0).then_inc(blank, 1)
            nc.gpsimd.memset(ones[:], 1.0).then_inc(blank, 1)
            nc.gpsimd.memset(minus_half[:], -0.5).then_inc(blank, 1)
            nc.gpsimd.iota(dist_i[:], pattern=[[-1, 2 * P]], base=P, channel_multiplier=1).then_inc(dist_ready, 1)
            pool.wait_ge(blank, 4)
            nc.gpsimd.affine_select(out=ident[:], in_=ident[:], compare_op=ALU.not_equal, fill=1.0, base=0,
                                    pattern=[[-1, P]], channel_multiplier=1).then_inc(made, 1)
            nc.gpsimd.affine_select(out=tri[:], in_=tri[:], compare_op=ALU.is_ge, fill=0.0, base=0,
                                    pattern=[[-1, P]], channel_multiplier=1).then_inc(made, 1)
            pool.wait_ge(slope_done, HEADS)
            nc.gpsimd.affine_select(out=bias[:], in_=bias[:], compare_op=ALU.is_ge, fill=LOW, base=P,
                                    pattern=[[0, HEADS], [-1, 2 * P]], channel_multiplier=1).then_inc(cut, 1)
            pool.wait_ge(cut, 1)
            nc.gpsimd.affine_select(out=bias[:], in_=bias[:], compare_op=ALU.is_ge, fill=LOW, base=-1,
                                    pattern=[[0, HEADS], [1, 2 * P]], channel_multiplier=-1).then_inc(cut, 1)

        @block.vector
        def _(dve):
            dve.wait_ge(dist_ready, 1)
            nc.vector.tensor_copy(dist[:], dist_i[:]).then_inc(dist_ready, 1)
            dve.wait_ge(dist_ready, 2)
            for h in range(HEADS):
                at = h // GRP * GRP + place4(h % GRP)
                nc.vector.tensor_scalar(bias[:, at, :], dist[:], -(2.0 ** -(8.0 * (h + 1) / HEADS)), None,
                                        ALU.mult).then_inc(slope_done, 1)
    return ident, tri, ones, bias, minus_half


def project(nc, sem, x, norm1_g, w_in, ident, minus_half, h_t, mixed, qk_t, sb_v, wq_t, wk_t, sw_v):
    groups = D_IN // COLS
    ring = 4
    XR = 4
    w_view = w_in.rearrange("(c p) n -> p c n", p=P)
    with ExitStack() as ctx:
        xs, xn = mixed[:, 0:XR, :], mixed[:, XR:XR + 2, :]
        w = ctx.enter_context(nc.sbuf_tensor("pj_w", [P, ring, CH, COLS], F32))
        g_t = ctx.enter_context(nc.sbuf_tensor("pj_g", [P, CH], F32))
        ss = ctx.enter_context(nc.sbuf_tensor("pj_ss", [P, TILES], F32))
        ms = ctx.enter_context(nc.sbuf_tensor("pj_ms", [P, TILES], F32))
        rstd = ctx.enter_context(nc.sbuf_tensor("pj_rstd", [P, TILES], F32))
        tp = ctx.enter_context(nc.psum_tensor("pj_tp", [P, 2, CH, P], F32))
        acc = ctx.enter_context(nc.psum_tensor("pj_acc", [P, 4, HALF], F32))

        x_in = [sem(f"pj_x_in{t}") for t in range(TILES)]
        w_loaded = [sem(f"pj_w_in{s}") for s in range(ring)]
        g_in = sem("pj_g_in")
        squared = sem("pj_squared")
        mean_done = sem("pj_mean")
        rstd_done = sem("pj_rstd_done")
        normed = sem("pj_normed")
        turned = sem("pj_turned")
        ht_ready = sem("pj_ht_ready")
        acc_full = sem("pj_acc_full")
        acc_read = sem("pj_acc_read")

        units = []
        for g in range(groups):
            for j in range(2):
                col = g * COLS + j * P
                if col < 2 * D_SB:
                    units += [(g, "t", j * P, hf, qk_t[:, col // P, hf * HALF:(hf + 1) * HALF],
                               DH ** -0.5 if col < D_SB else 1.0) for hf in range(2)]
                elif 3 * D_SB <= col < 3 * D_SB + HEADS * DH:
                    b = (col - 3 * D_SB) // P
                    units += [(g, "t", j * P, hf, wq_t[:, b, hf * HALF:(hf + 1) * HALF], DH ** -0.5)
                              for hf in range(2)]
            if 2 * D_SB <= g * COLS < 3 * D_SB:
                c0 = g * COLS - 2 * D_SB
                units += [(g, "v", (0, COLS), t, sb_v[:, t, c0:c0 + COLS], 1.0) for t in range(TILES)]
            if g == groups - 1:
                units += [(g, "k", kv * DH, hf, wk_t[:, kv, hf * HALF:(hf + 1) * HALF], 1.0)
                          for kv in range(KV) for hf in range(2)]
                units += [(g, "v", (P, P), t, sw_v[:, t, :], 1.0) for t in range(TILES)]

        ends = [1 + max(n for n, unit in enumerate(units) if unit[0] == g) for g in range(groups)]

        with nc.Block() as block:
            @block.sync
            def _(sp):
                with nc.allow_non_contiguous_dma(reason="one gain per feature, 4 KB in all"):
                    sp.dma_start(g_t[:], norm1_g.rearrange("(c p) -> p c", p=P)).then_inc(g_in, 16)
                for t in range(TILES):
                    if t >= XR:
                        sp.wait_ge(normed, t - XR + 1)
                    sp.dma_start(xs[:, t % XR, :], x[t * P:(t + 1) * P, :]).then_inc(x_in[t], 16)
                for g in range(groups):
                    if g >= ring:
                        sp.wait_ge(acc_full, ends[g - ring])
                    sp.dma_start(w[:, g % ring, :, :], w_view[:, :, g * COLS:(g + 1) * COLS]).then_inc(
                        w_loaded[g % ring], 16)

            @block.scalar
            def _(act):
                for t in range(TILES):
                    act.wait_ge(x_in[t], 16)
                    if t >= 2:
                        act.wait_ge(turned, t - 1)
                    nc.scalar.activation(xn[:, t % 2, :], xs[:, t % XR, :], ACT.Square,
                                         accum_out=ss[:, t:t + 1]).then_inc(squared, 1)
                for n, (_, _, _, _, dest, scale) in enumerate(units):
                    act.wait_ge(acc_full, n + 1)
                    width = dest.shape[-1]
                    nc.scalar.activation(dest, acc[:, n % 4, 0:width], ACT.Copy, scale=scale).then_inc(acc_read, 1)

            @block.gpsimd
            def _(pool):
                for t in range(TILES):
                    pool.wait_ge(mean_done, t + 1)
                    nc.gpsimd.tensor_tensor(rstd[:, t:t + 1], ms[:, t:t + 1], minus_half[:, 0:1], ALU.pow).then_inc(rstd_done, 1)

            @block.vector
            def _(dve):
                def evacuate(t):
                    dve.wait_ge(turned, t + 1)
                    nc.vector.tensor_tensor(h_t[:, :, t * P:(t + 1) * P], tp[:, t % 2, :, :],
                                            bcast(g_t[:, :].unsqueeze(2), [P, CH, P]), ALU.mult).then_inc(ht_ready, 1)

                dve.wait_ge(g_in, 16)
                for t in range(TILES):
                    dve.wait_ge(squared, t + 1)
                    nc.vector.tensor_scalar(ms[:, t:t + 1], ss[:, t:t + 1], 1.0 / D, EPS, ALU.mult,
                                            ALU.add).then_inc(mean_done, 1)
                    dve.wait_ge(rstd_done, t + 1)
                    nc.vector.tensor_scalar(xn[:, t % 2, :], xs[:, t % XR, :], rstd[:, t:t + 1], None,
                                            ALU.mult).then_inc(normed, 1)
                    if t >= 1:
                        evacuate(t - 1)
                evacuate(TILES - 1)

            @block.tensor
            def _(pe):
                for t in range(TILES):
                    pe.wait_ge(normed, t + 1)
                    if t >= 2:
                        pe.wait_ge(ht_ready, t - 1)
                    for c in range(CH):
                        last = nc.tensor.transpose(tp[:, t % 2, c, :], xn[:, t % 2, c * P:(c + 1) * P], ident[:])
                    last.then_inc(turned, 1)
                pe.wait_ge(ht_ready, TILES)
                for n, (g, kind, at, part, dest, _) in enumerate(units):
                    slot = w[:, g % ring, :, :]
                    if n == 0 or units[n - 1][0] != g:
                        pe.wait_ge(w_loaded[g % ring], 16 * (g // ring + 1))
                    if n >= 4:
                        pe.wait_ge(acc_read, n - 3)
                    for c in range(CH):
                        st = dict(start=c == 0, stop=c == CH - 1)
                        if kind == "v":
                            last = nc.tensor.matmul(acc[:, n % 4, 0:at[1]], h_t[:, c, part * P:(part + 1) * P],
                                                    slot[:, c, at[0]:at[0] + at[1]], **st)
                        elif kind == "t":
                            last = nc.tensor.matmul(acc[:, n % 4, :], slot[:, c, at:at + P],
                                                    h_t[:, c, part * HALF:(part + 1) * HALF], **st)
                        else:
                            for lo in (0, DH):
                                last = nc.tensor.matmul(acc[lo:lo + DH, n % 4, :], slot[:, c, at:at + DH],
                                                        h_t[:, c, part * HALF:(part + 1) * HALF], **st)
                    last.then_inc(acc_full, 1)


def stick(nc, sem, ident, tri, ones, spare, qk_t, sb_v, mixed):
    steps = [(i, kb) for i in range(TILES) for kb in range(i, -1, -1)]
    W = HEADS * P
    with ExitStack() as ctx:
        lsp, a = spare[:, 0:2, :], spare[:, 2:4, :]
        zs = ctx.enter_context(nc.sbuf_tensor("st_zs", [P, 4, W], F32))
        soft = ctx.enter_context(nc.sbuf_tensor("st_sp", [P, 3, W], F32))
        later = ctx.enter_context(nc.sbuf_tensor("st_s", [P, 3, W], F32))
        o_sb = ctx.enter_context(nc.sbuf_tensor("st_o_sb", [P, D_SB], F32))
        z = ctx.enter_context(nc.psum_tensor("st_z", [P, 2, W], F32))
        csum = ctx.enter_context(nc.psum_tensor("st_c", [P, W], F32))
        o = ctx.enter_context(nc.psum_tensor("st_o", [P, 2, D_SB], F32))

        z_ready = sem("st_z_ready")
        z_copied = sem("st_z_copied")
        abs_done = sem("st_abs")
        exp_done = sem("st_exp")
        log_done = sem("st_log")
        soft_done = sem("st_soft")
        soft_cut = sem("st_soft_cut")
        later_done = sem("st_later")
        sum_done = sem("st_sum")
        diff_done = sem("st_diff")
        diff_cut = sem("st_diff_cut")
        a_ready = sem("st_a_ready")
        pv_done = sem("st_pv")
        o_copied = sem("st_o_copied")
        o_turned = sem("st_o_turned")
        o_read = sem("st_o_read")

        def is_sum(n):
            return steps[n][1] < steps[n][0] - 1

        sums = [sum(is_sum(m) for m in range(n + 1)) for n in range(len(steps))]

        def carry_of(n):
            return later[:, n % 3, :] if is_sum(n) else soft[:, (n - 1) % 3, :]

        with nc.Block() as block:
            @block.tensor
            def _(pe):
                def scores(n):
                    i, kb = steps[n]
                    if n >= 2:
                        pe.wait_ge(z_copied, n - 1)
                    for h in range(HEADS):
                        lo = DH * (h % 2)
                        last = nc.tensor.matmul(z[:, n % 2, place(h) * P:(place(h) + 1) * P],
                                                qk_t[lo:lo + DH, HEADS // 2 + h // 2, kb * P:(kb + 1) * P],
                                                qk_t[lo:lo + DH, h // 2, i * P:(i + 1) * P], start=True, stop=True)
                    last.then_inc(z_ready, 1)

                def suffix(n):
                    i, kb = steps[n]
                    if n >= 1:
                        pe.wait_ge(diff_done, n)
                    if kb == i:
                        pe.wait_ge(soft_cut, i + 1)
                    else:
                        pe.wait_ge(soft_done, n + 1)
                        if is_sum(n):
                            pe.wait_ge(later_done, sums[n])
                    for hf in range(2):
                        cols = slice(hf * HALF, (hf + 1) * HALF)
                        last = nc.tensor.matmul(csum[:, cols], tri[:], soft[:, n % 3, cols], start=True, stop=kb == i)
                        if kb < i:
                            last = nc.tensor.matmul(csum[:, cols], ones[:], carry_of(n)[:, cols], start=False, stop=True)
                    last.then_inc(sum_done, 1)

                def values(n):
                    i, kb = steps[n]
                    pe.wait_ge(a_ready, n + 1)
                    if kb == i and i >= 2:
                        pe.wait_ge(o_read, i - 1)
                    for h in range(HEADS):
                        lo = DH * (h % 2)
                        last = nc.tensor.matmul(o[lo:lo + DH, i % 2, (h // 2) * P:(h // 2 + 1) * P],
                                                sb_v[:, kb, h * DH:(h + 1) * DH],
                                                a[:, n % 2, place(h) * P:(place(h) + 1) * P],
                                                start=kb == i and h < 2, stop=kb == 0,
                                                skip_group_check=True)
                    last.then_inc(pv_done, 1)

                def turn_output(i):
                    pe.wait_ge(o_copied, i + 1)
                    for b in range(HEADS // 2):
                        last = nc.tensor.transpose(o[:, i % 2, b * P:(b + 1) * P], o_sb[:, b * P:(b + 1) * P], ident[:])
                    last.then_inc(o_turned, 1)

                for n in range(3):
                    scores(n)
                for n in range(len(steps)):
                    if n + 3 < len(steps):
                        scores(n + 3)
                    suffix(n)
                    if n >= 1:
                        values(n - 1)
                    if n >= 2 and steps[n - 2][1] == 0:
                        turn_output(steps[n - 2][0])
                values(len(steps) - 1)
                turn_output(TILES - 1)

            @block.scalar
            def _(act):
                def copy(n):
                    act.wait_ge(z_ready, n + 1)
                    if n >= 4:
                        act.wait_ge(diff_done, n - 3)
                    nc.scalar.activation(zs[:, n % 4, :], z[:, n % 2, :], ACT.Copy).then_inc(z_copied, 1)

                def log_terms(n):
                    act.wait_ge(abs_done, n + 1)
                    nc.scalar.activation(lsp[:, n % 2, :], lsp[:, n % 2, :], ACT.Exp, scale=-1.0).then_inc(exp_done, 1)
                    act.wait_ge(exp_done, n + 1)
                    nc.scalar.activation(lsp[:, n % 2, :], lsp[:, n % 2, :], ACT.Ln, bias=1.0).then_inc(log_done, 1)

                def weights(n):
                    i, kb = steps[n]
                    act.wait_ge(diff_done, n + 1)
                    if kb == i:
                        act.wait_ge(diff_cut, i + 1)
                    nc.scalar.activation(a[:, n % 2, :], a[:, n % 2, :], ACT.Exp).then_inc(a_ready, 1)

                nc.scalar.preload_act_table_set("natural_log_exp_and_others")
                for n in range(3):
                    copy(n)
                log_terms(0)
                log_terms(1)
                for n in range(len(steps)):
                    if n + 3 < len(steps):
                        copy(n + 3)
                    if n + 2 < len(steps):
                        log_terms(n + 2)
                    weights(n)

            @block.vector
            def _(dve):
                def copy_output(i):
                    dve.wait_ge(pv_done, (i + 1) * (i + 2) // 2)
                    if i >= 1:
                        dve.wait_ge(o_turned, i)
                    nc.vector.tensor_copy(o_sb[:], o[:, i % 2, :]).then_inc(o_copied, 1)

                def read_out(i):
                    dve.wait_ge(o_turned, i + 1)
                    nc.vector.tensor_copy(mixed[:, i, 0:D_SB], o[:, i % 2, :]).then_inc(o_read, 1)

                def magnitude(n):
                    dve.wait_ge(z_copied, n + 1)
                    if n >= 2:
                        dve.wait_ge(soft_done, n - 1)
                    nc.vector.scalar_tensor_tensor(out=lsp[:, n % 2, :], in0=zs[:, n % 4, :], scalar=-1.0,
                                                   in1=zs[:, n % 4, :], op0=ALU.mult, op1=ALU.max).then_inc(abs_done, 1)

                def softplus(n):
                    dve.wait_ge(log_done, n + 1)
                    if n >= 3:
                        dve.wait_ge(sum_done, n - 1)
                    nc.vector.scalar_tensor_tensor(out=soft[:, n % 3, :], in0=zs[:, n % 4, :], scalar=0.0,
                                                   in1=lsp[:, n % 2, :], op0=ALU.max, op1=ALU.add).then_inc(soft_done, 1)

                def carry(n):
                    dve.wait_ge(soft_done, n)
                    if is_sum(n - 1):
                        dve.wait_ge(later_done, sums[n - 1])
                    else:
                        dve.wait_ge(soft_cut, steps[n][0] + 1)
                    if n >= 3:
                        dve.wait_ge(sum_done, n - 2)
                    nc.vector.tensor_tensor(later[:, n % 3, :], carry_of(n - 1), soft[:, (n - 1) % 3, :],
                                            ALU.add).then_inc(later_done, 1)

                def difference(n):
                    dve.wait_ge(sum_done, n + 1)
                    if n >= 2:
                        dve.wait_ge(pv_done, n - 1)
                    nc.vector.tensor_tensor(a[:, n % 2, :], zs[:, n % 4, :], csum[:, :], ALU.subtract).then_inc(diff_done, 1)

                magnitude(0)
                magnitude(1)
                softplus(0)
                magnitude(2)
                for n, (i, kb) in enumerate(steps):
                    if n + 1 < len(steps):
                        softplus(n + 1)
                    if n + 2 < len(steps) and is_sum(n + 2):
                        carry(n + 2)
                    if n + 3 < len(steps):
                        magnitude(n + 3)
                    if n >= 2 and steps[n - 2][1] == 0:
                        copy_output(steps[n - 2][0])
                    if n >= 3 and steps[n - 3][1] == 0:
                        read_out(steps[n - 3][0])
                    difference(n)
                copy_output(TILES - 1)
                read_out(TILES - 1)

            @block.gpsimd
            def _(pool):
                for n, (i, kb) in enumerate(steps):
                    if kb == i:
                        pool.wait_ge(soft_done, n + 1)
                        cut = soft[:, n % 3, :].rearrange("p (h q) -> p h q", h=HEADS)
                        nc.gpsimd.affine_select(out=cut, in_=cut, compare_op=ALU.is_gt, fill=0.0, base=0,
                                                pattern=[[0, HEADS], [1, P]], channel_multiplier=-1).then_inc(soft_cut, 1)
                        pool.wait_ge(diff_done, n + 1)
                        cut = a[:, n % 2, :].rearrange("p (h q) -> p h q", h=HEADS)
                        nc.gpsimd.affine_select(out=cut, in_=cut, compare_op=ALU.is_gt, fill=LOW, base=0,
                                                pattern=[[0, HEADS], [1, P]], channel_multiplier=-1).then_inc(diff_cut, 1)


def window(nc, sem, sinks, ident, bias, wq_t, wk_t, sw_v, mixed):
    steps = [(i, kv) for i in range(TILES) for kv in range(KV)]
    with ExitStack() as ctx:
        sink_row = ctx.enter_context(nc.sbuf_tensor("wd_sink_row", [P, HEADS], F32))
        sink = ctx.enter_context(nc.sbuf_tensor("wd_sink", [P, HEADS], F32))
        p = ctx.enter_context(nc.sbuf_tensor("wd_p", [P, 2, GRP, 2 * P], F32))
        p_t = ctx.enter_context(nc.sbuf_tensor("wd_pt", [P, 2, GRP, 2, P], F32))
        top = ctx.enter_context(nc.sbuf_tensor("wd_top", [P, 4, GRP], F32))
        peak = ctx.enter_context(nc.sbuf_tensor("wd_peak", [P, 4, GRP], F32))
        neg = ctx.enter_context(nc.sbuf_tensor("wd_neg", [P, 4, GRP], F32))
        sd = ctx.enter_context(nc.sbuf_tensor("wd_sd", [P, 4, GRP], F32))
        es = ctx.enter_context(nc.sbuf_tensor("wd_es", [P, 4, GRP], F32))
        rs = ctx.enter_context(nc.sbuf_tensor("wd_rs", [P, 4, GRP], F32))
        den = ctx.enter_context(nc.sbuf_tensor("wd_den", [P, 4, GRP], F32))
        rden = ctx.enter_context(nc.sbuf_tensor("wd_rden", [P, 4, GRP], F32))
        s = ctx.enter_context(nc.psum_tensor("wd_s", [P, 2, GRP, 2 * P], F32))
        tp = ctx.enter_context(nc.psum_tensor("wd_tp", [P, GRP, 2, P], F32))
        o = ctx.enter_context(nc.psum_tensor("wd_o", [P, 2, HALF], F32))

        sink_in = sem("wd_sink_in")
        s_ready = sem("wd_s_ready")
        biased = sem("wd_biased")
        top_done = sem("wd_top_done")
        peak_done = sem("wd_peak_done")
        neg_done = sem("wd_neg_done")
        p_ready = sem("wd_p_ready")
        turned = sem("wd_turned")
        pt_ready = sem("wd_pt_ready")
        pv_done = sem("wd_pv")
        den_done = sem("wd_den_done")
        rden_done = sem("wd_rden_done")
        o_read = sem("wd_o_read")

        def first_key(i):
            return P if i == 0 else 0

        with nc.Block() as block:
            @block.sync
            def _(sp):
                sp.dma_start(sink_row[:], sinks.partition_broadcast(P)).then_inc(sink_in, 16)

            @block.tensor
            def _(pe):
                def scores(n):
                    i, kv = steps[n]
                    k0 = first_key(i)
                    if n >= 2:
                        pe.wait_ge(biased, n - 1)
                    for g in range(GRP):
                        h = kv * GRP + g
                        lo = DH * (h % 2)
                        last = nc.tensor.matmul(s[:, n % 2, place4(g), k0:2 * P], wq_t[lo:lo + DH, h // 2, i * P:(i + 1) * P],
                                                wk_t[lo:lo + DH, kv, (i - 1) * P + k0:(i + 1) * P], start=True, stop=True)
                    last.then_inc(s_ready, 1)

                def turn(n):
                    i, kv = steps[n]
                    pe.wait_ge(p_ready, n + 1)
                    if n >= 1:
                        pe.wait_ge(pt_ready, n)
                    for g in range(GRP):
                        for kb in range(first_key(i) // P, 2):
                            last = nc.tensor.transpose(tp[:, g, kb, :], p[:, n % 2, g, kb * P:(kb + 1) * P], ident[:])
                    last.then_inc(turned, 1)

                def values(n):
                    i, kv = steps[n]
                    pe.wait_ge(pt_ready, n + 1)
                    if n >= 2:
                        pe.wait_ge(o_read, n - 1)
                    for g in range(GRP):
                        k0 = first_key(i) // P
                        for kb in range(k0, 2):
                            last = nc.tensor.matmul(o[:, n % 2, g * DH:(g + 1) * DH], p_t[:, n % 2, g, kb, :],
                                                    sw_v[:, i - 1 + kb, kv * DH:(kv + 1) * DH],
                                                    start=kb == k0, stop=kb == 1)
                    last.then_inc(pv_done, 1)

                scores(0)
                for n in range(len(steps)):
                    if n + 1 < len(steps):
                        scores(n + 1)
                    turn(n)
                    if n >= 1:
                        values(n - 1)
                values(len(steps) - 1)

            @block.vector
            def _(dve):
                def soften(n):
                    i, kv = steps[n]
                    k0 = first_key(i)
                    b, st = n % 2, n % 4
                    sk = sink[:, kv * GRP:(kv + 1) * GRP]
                    dve.wait_ge(s_ready, n + 1)
                    if n >= 2:
                        dve.wait_ge(turned, n - 1)
                        dve.wait_ge(p_ready, n - 1)
                    nc.vector.tensor_tensor(p[:, b, :, k0:], s[:, b, :, k0:], bias[:, kv * GRP:(kv + 1) * GRP, k0:],
                                            ALU.add).then_inc(biased, 1)
                    dve.wait_ge(biased, n + 1)
                    nc.vector.tensor_reduce(top[:, st, :], p[:, b, :, k0:], AX, ALU.max).then_inc(top_done, 1)
                    dve.wait_ge(top_done, n + 1)
                    nc.vector.tensor_tensor(peak[:, st, :], top[:, st, :], sk, ALU.max).then_inc(peak_done, 1)
                    dve.wait_ge(peak_done, n + 1)
                    nc.vector.tensor_scalar(neg[:, st, :], peak[:, st, :], -1.0, None, ALU.mult).then_inc(neg_done, 1)
                    nc.vector.tensor_tensor(sd[:, st, :], sk, peak[:, st, :], ALU.subtract).then_inc(neg_done, 1)

                def read_t(n):
                    k0 = first_key(steps[n][0]) // P
                    dve.wait_ge(turned, n + 1)
                    if n >= 2:
                        dve.wait_ge(pv_done, n - 1)
                    nc.vector.tensor_copy(p_t[:, n % 2, :, k0:, :], tp[:, :, k0:, :]).then_inc(pt_ready, 1)

                def finish(n):
                    i, kv = steps[n]
                    b, st = n % 2, n % 4
                    dve.wait_ge(p_ready, n + 1)
                    nc.vector.tensor_tensor(den[:, st, :], rs[:, st, :], es[:, st, :], ALU.add).then_inc(den_done, 1)
                    dve.wait_ge(den_done, n + 1)
                    nc.vector.reciprocal(rden[:, st, :], den[:, st, :]).then_inc(rden_done, 1)
                    dve.wait_ge(rden_done, n + 1)
                    dve.wait_ge(pv_done, n + 1)
                    dest = mixed[:, i, D_SB + kv * GRP * DH:D_SB + (kv + 1) * GRP * DH]
                    nc.vector.tensor_tensor(dest.rearrange("p (b a d) -> p a b d", a=2, d=DH),
                                            o[:, b, 0:GRP * DH].rearrange("p (a b d) -> p a b d", a=2, d=DH),
                                            bcast(rden[:, st, :].rearrange("p (a b) -> p a b", a=2).unsqueeze(3),
                                                  [P, 2, GRP // 2, DH]), ALU.mult).then_inc(o_read, 1)

                dve.wait_ge(sink_in, 16)
                nc.vector.tensor_copy(sink[:].rearrange("p (kv a b) -> p kv a b", kv=KV, a=2),
                                      sink_row[:].rearrange("p (kv b a) -> p kv a b", kv=KV, a=2)).then_inc(sink_in, 1)
                dve.wait_ge(sink_in, 17)
                soften(0)
                for n in range(len(steps)):
                    if n + 1 < len(steps):
                        soften(n + 1)
                    read_t(n)
                    if n >= 1:
                        finish(n - 1)
                finish(len(steps) - 1)

            @block.scalar
            def _(act):
                for n, (i, kv) in enumerate(steps):
                    b, st, k0 = n % 2, n % 4, first_key(i)
                    act.wait_ge(neg_done, 2 * (n + 1))
                    if n >= 4:
                        act.wait_ge(den_done, n - 3)
                    for g in range(GRP):
                        nc.scalar.activation(p[:, b, g, k0:], p[:, b, g, k0:], ACT.Exp, bias=neg[:, st, g:g + 1],
                                             accum_out=rs[:, st, g:g + 1])
                    nc.scalar.activation(es[:, st, :], sd[:, st, :], ACT.Exp).then_inc(p_ready, 1)


def mix(nc, sem, x, sb_g, sw_g, w_out, norm2_g, ident, minus_half, mixed, x1_dram, x2_dram, x2_t):
    with ExitStack() as ctx:
        w = ctx.enter_context(nc.sbuf_tensor("mx_w", [P, CH, D], F32))
        g1 = ctx.enter_context(nc.sbuf_tensor("mx_g1", [P, D], F32))
        g2 = ctx.enter_context(nc.sbuf_tensor("mx_g2", [P, D], F32))
        xr = ctx.enter_context(nc.sbuf_tensor("mx_xr", [P, 2, D], F32))
        on = ctx.enter_context(nc.sbuf_tensor("mx_on", [P, 2, D], F32))
        m_t = ctx.enter_context(nc.sbuf_tensor("mx_mt", [P, 2, CH, P], F32))
        x1 = ctx.enter_context(nc.sbuf_tensor("mx_x1", [P, 2, D], F32))
        x2 = ctx.enter_context(nc.sbuf_tensor("mx_x2", [P, 2, D], F32))
        hs = ctx.enter_context(nc.sbuf_tensor("mx_hs", [P, 3, 2 * HEADS], F32))
        rs = ctx.enter_context(nc.sbuf_tensor("mx_rs", [P, 3, TILES], F32))
        tp1 = ctx.enter_context(nc.psum_tensor("mx_tp1", [P, CH, P], F32))
        tp2 = ctx.enter_context(nc.psum_tensor("mx_tp2", [P, CH, P], F32))
        y = ctx.enter_context(nc.psum_tensor("mx_y", [P, 2, D], F32))

        w_in_ = sem("mx_w_in")
        g_in = sem("mx_g_in")
        x_in = [sem(f"mx_x_in{s}") for s in range(2)]
        x1_out = [sem(f"mx_x1_out{s}") for s in range(2)]
        x2_out = [sem(f"mx_x2_out{s}") for s in range(2)]
        squared = sem("mx_squared")
        sums = sem("mx_sums")
        scaled = sem("mx_scaled")
        gained = sem("mx_gained")
        turned = sem("mx_turned")
        mt_ready = sem("mx_mt_ready")
        y_ready = sem("mx_y_ready")
        x1_ready = sem("mx_x1_ready")
        squared2 = sem("mx_squared2")
        head_rstd = sem("mx_head_rstd")
        mean2 = sem("mx_mean2")
        rstd2 = sem("mx_rstd2")
        scaled2 = sem("mx_scaled2")
        gained2 = sem("mx_gained2")
        turned2 = sem("mx_turned2")
        x2t_ready = sem("mx_x2t_ready")
        NH = 2 * HEADS

        with nc.Block() as block:
            def store(sp, t):
                sp.wait_ge(x1_ready, t + 1)
                sp.dma_start(x1_dram[t * P:(t + 1) * P, :], x1[:, t % 2, :]).then_inc(x1_out[t % 2], 16)
                sp.wait_ge(gained2, t + 1)
                sp.dma_start(x2_dram[t * P:(t + 1) * P, :], x2[:, t % 2, :]).then_inc(x2_out[t % 2], 16)

            @block.sync
            def _(sp):
                sp.dma_start(g1[:, 0:D_SB], sb_g.partition_broadcast(P)).then_inc(g_in, 16)
                sp.dma_start(g1[:, D_SB:D], sw_g.partition_broadcast(P)).then_inc(g_in, 16)
                sp.dma_start(g2[:], norm2_g.partition_broadcast(P)).then_inc(g_in, 16)
                sp.dma_start(w[:], w_out.rearrange("(c p) n -> p c n", p=P)).then_inc(w_in_, 16)
                for t in range(TILES):
                    if t >= 2:
                        sp.wait_ge(x1_ready, t - 1)
                    sp.dma_start(xr[:, t % 2, :], x[t * P:(t + 1) * P, :]).then_inc(x_in[t % 2], 16)
                    if t >= 1:
                        store(sp, t - 1)
                store(sp, TILES - 1)
                for s in range(2):
                    sp.wait_ge(x1_out[s], 16 * (TILES // 2))
                    sp.wait_ge(x2_out[s], 16 * (TILES // 2))

            @block.scalar
            def _(act):
                for t in range(-1, TILES + 1):
                    if t + 1 < TILES:
                        n = t + 1
                        if n >= 2:
                            act.wait_ge(turned, n - 1)
                        nc.scalar.activation(on[:, n % 2, :], mixed[:, n, :], ACT.Square).then_inc(squared, 1)
                        act.wait_ge(turned, n + 1)
                        if n >= 2:
                            act.wait_ge(y_ready, n - 1)
                        nc.scalar.activation(m_t[:, n % 2, :, :], tp1[:], ACT.Copy).then_inc(mt_ready, 1)
                    if 0 <= t < TILES:
                        act.wait_ge(x1_ready, t + 1)
                        if t >= 2:
                            act.wait_ge(turned2, t - 1)
                            act.wait_ge(x2_out[t % 2], 16 * (t // 2))
                        nc.scalar.activation(x2[:, t % 2, :], x1[:, t % 2, :], ACT.Square,
                                             accum_out=rs[:, 0, t:t + 1]).then_inc(squared2, 1)
                    if 0 <= t - 1:
                        act.wait_ge(turned2, t)
                        nc.scalar.activation(x2_t[:, :, (t - 1) * P:t * P], tp2[:], ACT.Copy).then_inc(x2t_ready, 1)

            @block.vector
            def _(dve):
                for t in range(-1, TILES):
                    if t + 1 < TILES:
                        n = t + 1
                        o3 = on[:, n % 2, :].rearrange("p (h d) -> p h d", d=DH)
                        dve.wait_ge(squared, n + 1)
                        if n >= 1:
                            dve.wait_ge(scaled, n)
                        nc.vector.tensor_reduce(hs[:, 0, :], o3, AX, ALU.add).then_inc(sums, 1)
                        dve.wait_ge(sums, 2 * n + 1)
                        nc.vector.tensor_scalar(hs[:, 1, :], hs[:, 0, :], 1.0 / DH, EPS, ALU.mult, ALU.add).then_inc(sums, 1)
                        dve.wait_ge(head_rstd, n + 1)
                        nc.vector.tensor_tensor(o3, mixed[:, n, :].rearrange("p (h d) -> p h d", d=DH),
                                                bcast(hs[:, 2, :].unsqueeze(2), [P, NH, DH]), ALU.mult).then_inc(scaled, 1)
                    if t >= 0:
                        dve.wait_ge(y_ready, t + 1)
                        dve.wait_ge(x_in[t % 2], 16 * (t // 2 + 1))
                        if t >= 2:
                            dve.wait_ge(x1_out[t % 2], 16 * (t // 2))
                            dve.wait_ge(scaled2, t - 1)
                        nc.vector.tensor_tensor(x1[:, t % 2, :], y[:, t % 2, :], xr[:, t % 2, :], ALU.add).then_inc(x1_ready, 1)
                        dve.wait_ge(squared2, t + 1)
                        nc.vector.tensor_scalar(rs[:, 1, t:t + 1], rs[:, 0, t:t + 1], 1.0 / D, EPS, ALU.mult,
                                                ALU.add).then_inc(mean2, 1)
                        dve.wait_ge(rstd2, t + 1)
                        nc.vector.tensor_scalar(x2[:, t % 2, :], x1[:, t % 2, :], rs[:, 2, t:t + 1], None,
                                                ALU.mult).then_inc(scaled2, 1)

            @block.gpsimd
            def _(pool):
                pool.wait_ge(g_in, 48)
                for t in range(-1, TILES):
                    if t + 1 < TILES:
                        n = t + 1
                        pool.wait_ge(sums, 2 * n + 2)
                        nc.gpsimd.tensor_tensor(hs[:, 2, :], hs[:, 1, :], minus_half[:], ALU.pow).then_inc(head_rstd, 1)
                        pool.wait_ge(scaled, n + 1)
                        nc.gpsimd.tensor_tensor(on[:, n % 2, :], on[:, n % 2, :], g1[:], ALU.mult).then_inc(gained, 1)
                    if t >= 0:
                        pool.wait_ge(mean2, t + 1)
                        nc.gpsimd.tensor_tensor(rs[:, 2, t:t + 1], rs[:, 1, t:t + 1], minus_half[:, 0:1],
                                                ALU.pow).then_inc(rstd2, 1)
                        pool.wait_ge(scaled2, t + 1)
                        nc.gpsimd.tensor_tensor(x2[:, t % 2, :], x2[:, t % 2, :], g2[:], ALU.mult).then_inc(gained2, 1)

            @block.tensor
            def _(pe):
                for t in range(-1, TILES + 1):
                    if 0 <= t < TILES:
                        pe.wait_ge(mt_ready, t + 1)
                        if t == 0:
                            pe.wait_ge(w_in_, 16)
                        if t >= 2:
                            pe.wait_ge(x1_ready, t - 1)
                        for c in range(CH):
                            for hf in range(2):
                                last = nc.tensor.matmul(y[:, t % 2, hf * HALF:(hf + 1) * HALF], m_t[:, t % 2, c, :],
                                                        w[:, c, hf * HALF:(hf + 1) * HALF],
                                                        start=c == 0, stop=c == CH - 1)
                        last.then_inc(y_ready, 1)
                    if t + 1 < TILES:
                        n = t + 1
                        pe.wait_ge(gained, n + 1)
                        if n >= 1:
                            pe.wait_ge(mt_ready, n)
                        for c in range(CH):
                            last = nc.tensor.transpose(tp1[:, c, :], on[:, n % 2, c * P:(c + 1) * P], ident[:])
                        last.then_inc(turned, 1)
                    if t - 1 >= 0:
                        pe.wait_ge(gained2, t)
                        if t >= 2:
                            pe.wait_ge(x2t_ready, t - 1)
                        for c in range(CH):
                            last = nc.tensor.transpose(tp2[:, c, :], x2[:, (t - 1) % 2, c * P:(c + 1) * P], ident[:])
                        last.then_inc(turned2, 1)


class KeyScores:

    def __init__(self, nc, sem, tag, ctx, spans, w, ring, keys_t, w_q, x2_t, score_dram):
        self.nc, self.w, self.ring, self.keys_t, self.x2_t = nc, w, ring, keys_t, x2_t
        self.q_t = ctx.enter_context(nc.sbuf_tensor(f"{tag}_qt", [P, 2, HALF], F32))
        self.out = ctx.enter_context(nc.sbuf_tensor(f"{tag}_out", [P, 4, 4, NK], F32))
        self.q = ctx.enter_context(nc.psum_tensor(f"{tag}_q", [P, 2, HALF], F32))
        self.s = ctx.enter_context(nc.psum_tensor(f"{tag}_s", [P, 2, 4, NK], F32))
        self.w_loaded = [sem(f"{tag}_w_in{k}") for k in range(ring)]
        self.q_ready = sem(f"{tag}_q_ready")
        self.qt_ready = sem(f"{tag}_qt_ready")
        self.s_ready = sem(f"{tag}_s_ready")
        self.s_read = sem(f"{tag}_s_read")
        self.stored = [sem(f"{tag}_stored{k}") for k in range(4)]
        self.units = [(b, first, tiles) for b in range(SIDES) for first, tiles in spans]
        self.per_group = len(spans) * COLS // P
        self.groups = SIDES * P // COLS
        self.w_view = w_q.rearrange("(c p) n -> p c n", p=P)
        self.score_view = score_dram.rearrange("(t p) (b n) -> p t b n", p=P, n=NK)

    def load(self, sp, g):
        sp.dma_start(self.w[:, g % self.ring, :, :], self.w_view[:, :, g * COLS:(g + 1) * COLS]).then_inc(
            self.w_loaded[g % self.ring], 16)

    def store(self, sp, n):
        b, first, tiles = self.units[n]
        sp.wait_ge(self.s_read, n + 1)
        sp.dma_start(self.score_view[:, first:first + tiles, b, :], self.out[:, n % 4, 0:tiles, :]).then_inc(
            self.stored[n % 4], 16)
        g = n // self.per_group + self.ring
        if n % self.per_group == self.per_group - 1 and g < self.groups:
            sp.wait_ge(self.s_ready, n + 1)
            self.load(sp, g)

    def all_stored(self, sp):
        for k in range(4):
            sp.wait_ge(self.stored[k], 16 * (len(self.units) // 4))

    def copy_queries(self, act, n):
        width = self.units[n][2] * P
        act.wait_ge(self.q_ready, n + 1)
        if n >= 2:
            act.wait_ge(self.s_ready, n - 1)
        self.nc.scalar.activation(self.q_t[:, n % 2, 0:width], self.q[:, n % 2, 0:width], ACT.Copy).then_inc(self.qt_ready, 1)

    def read_scores(self, act, n):
        tiles = self.units[n][2]
        act.wait_ge(self.s_ready, n + 1)
        if n >= 4:
            act.wait_ge(self.stored[n % 4], 16 * (n // 4))
        self.nc.scalar.activation(self.out[:, n % 4, 0:tiles, :], self.s[:, n % 2, 0:tiles, :], ACT.Copy).then_inc(self.s_read, 1)

    def evacuate(self, act, n):
        if n == 0:
            self.copy_queries(act, 0)
        if n + 1 < len(self.units):
            self.copy_queries(act, n + 1)
        self.read_scores(act, n)

    def query(self, pe, n):
        b, first, tiles = self.units[n]
        g = n // self.per_group
        if n % self.per_group == 0:
            pe.wait_ge(self.w_loaded[g % self.ring], 16 * (g // self.ring + 1))
        if n >= 2:
            pe.wait_ge(self.qt_ready, n - 1)
        for c in range(CH):
            last = self.nc.tensor.matmul(self.q[:, n % 2, 0:tiles * P], self.w[:, g % self.ring, c, (b % 2) * P:(b % 2 + 1) * P],
                                         self.x2_t[:, c, first * P:(first + tiles) * P], start=c == 0, stop=c == CH - 1)
        last.then_inc(self.q_ready, 1)

    def score(self, pe, n):
        b, first, tiles = self.units[n]
        pe.wait_ge(self.qt_ready, n + 1)
        if n >= 2:
            pe.wait_ge(self.s_read, n - 1)
        for j in range(tiles):
            last = self.nc.tensor.matmul(self.s[:, n % 2, j, :], self.q_t[:, n % 2, j * P:(j + 1) * P], self.keys_t[:, b, :],
                                         start=True, stop=True)
        last.then_inc(self.s_ready, 1)

    def multiply(self, pe):
        self.query(pe, 0)
        for n in range(len(self.units)):
            if n + 1 < len(self.units):
                self.query(pe, n + 1)
            self.score(pe, n)


def key_scores(nc, sem, w_q, keys1, keys2, ident, x2_t, keys_t, score_dram):
    ring = 3
    with ExitStack() as ctx:
        keys = ctx.enter_context(nc.sbuf_tensor("ks_keys", [P, SIDES, P], F32))
        w = ctx.enter_context(nc.sbuf_tensor("ks_w", [P, ring, CH, COLS], F32))
        tp = ctx.enter_context(nc.psum_tensor("ks_tp", [P, 2, 4, P], F32))
        part = KeyScores(nc, sem, "ks", ctx, [(0, EARLY)], w, ring, keys_t, w_q, x2_t, score_dram)
        keys_in = sem("ks_keys_in")
        turned = sem("ks_turned")
        keys_ready = sem("ks_keys_ready")
        side_view = keys[:, :, :].rearrange("n (h s) d -> n h s d", s=2)

        with nc.Block() as block:
            @block.sync
            def _(sp):
                sp.dma_start(side_view[:, :, 0, :], keys1.rearrange("h n d -> n h d")).then_inc(keys_in, 16)
                sp.dma_start(side_view[:, :, 1, :], keys2.rearrange("h n d -> n h d")).then_inc(keys_in, 16)
                for g in range(ring):
                    part.load(sp, g)
                for n in range(len(part.units)):
                    part.store(sp, n)
                part.all_stored(sp)

            @block.scalar
            def _(act):
                for n in range(len(part.units)):
                    part.evacuate(act, n)

            @block.vector
            def _(dve):
                for k in range(SIDES // 4):
                    dve.wait_ge(turned, k + 1)
                    nc.vector.tensor_copy(keys_t[:, 4 * k:4 * k + 4, :], tp[:, k % 2, :, :]).then_inc(keys_ready, 1)

            @block.tensor
            def _(pe):
                pe.wait_ge(keys_in, 32)
                for k in range(SIDES // 4):
                    if k >= 2:
                        pe.wait_ge(keys_ready, k - 1)
                    for j in range(4):
                        last = nc.tensor.transpose(tp[:, k % 2, j, :], keys[:, 4 * k + j, :], ident[:])
                    last.then_inc(turned, 1)
                pe.wait_ge(keys_ready, SIDES // 4)
                part.multiply(pe)


def experts(nc, sem, ident, keys_t, w_q, x2_t, score_dram, x1_dram, x2_dram, peer_u, peer_v, final_g, out):
    RG = 8
    GROUPS = PICKS // RG
    score_t = score_dram.rearrange("(t p) n -> t p n", p=P)
    x1_v = x1_dram.rearrange("(t p) n -> t p n", p=P)
    x2_v = x2_dram.rearrange("(t p) n -> t p n", p=P)
    out_v = out.rearrange("(t p) n -> t p n", p=P)
    with ExitStack() as ctx:
        def sb(name, shape, dt=F32):
            return ctx.enter_context(nc.sbuf_tensor(name, shape, dt))

        u = sb("ex_u", [P, RG, D])
        v = sb("ex_v", [P, RG, D])
        diag = sb("ex_diag", [P, RG, P])
        sc = sb("ex_sc", [P, SIDES, NK])
        left = sb("ex_left", [P, SIDES, NK])
        cand = sb("ex_cand", [P, PH, TOPK, TOPK])
        cleft = sb("ex_cleft", [P, PH, TOPK, TOPK])
        half_v = sb("ex_half_v", [P, SIDES, TOPK])
        half_i = sb("ex_half_i", [P, SIDES, TOPK], U32)
        half_f = sb("ex_half_f", [P, SIDES, TOPK])
        best = sb("ex_best", [P, PH, TOPK])
        pos = sb("ex_pos", [P, PH, TOPK], U32)
        part_i = sb("ex_part_i", [P, 2, PICKS], U32)
        part_f = sb("ex_part_f", [P, 2, PICKS])
        hit = sb("ex_hit", [P, PICKS, TOPK])
        row = sb("ex_row", [P, 2, PICKS])
        index_f = sb("ex_index_f", [P, PICKS])
        index = sb("ex_index", [P, PICKS], I32)
        index_ut = sb("ex_index_ut", [P, PICKS], I32)
        index_vt = sb("ex_index_vt", [P, PICKS], I32)
        gate_e = sb("ex_gate_e", [P, PICKS])
        gates = sb("ex_gates", [P, 2, PICKS])
        gsum = sb("ex_gsum", [P, 2, PH])
        ramp_i = sb("ex_ramp_i", [P, TOPK], I32)
        ramp = sb("ex_ramp", [P, TOPK])
        index_u = sb("ex_index_u", [P, 2, RG], I32)
        index_v = sb("ex_index_v", [P, 2, RG], I32)
        zero_i = sb("ex_zero_i", [P, PICKS], I32)
        x2 = sb("ex_x2", [P, D])
        prod = sb("ex_prod", [P, D])
        dots = sb("ex_dots", [P, RG])
        hid = sb("ex_hid", [P, PICKS])
        ga = sb("ex_ga", [P, 4, PICKS])
        wt = sb("ex_wt", [P, PICKS])
        x1 = sb("ex_x1", [P, D])
        y = sb("ex_y", [P, D])
        gf = sb("ex_gf", [P, D])
        fs = sb("ex_fs", [P, 8])
        acc = ctx.enter_context(nc.psum_tensor("ex_acc", [P, D], F32))
        ysq = ctx.enter_context(nc.psum_tensor("ex_ysq", [P, D], F32))
        key_ring = RG * D // (CH * COLS)
        rest = KeyScores(nc, sem, "kl", ctx, [(EARLY, 4), (EARLY + 4, TILES - EARLY - 4)],
                         v[:].rearrange("p r (h n) -> p (r h) n", n=COLS).rearrange("p (g c) n -> p g c n", c=CH),
                         key_ring, keys_t, w_q, x2_t, score_dram)

        setup = sem("ex_setup")
        gf_in = sem("ex_gf_in")
        sc_in = sem("ex_sc_in")
        x1_in = sem("ex_x1_in")
        x2_in = sem("ex_x2_in")
        stored = sem("ex_stored")
        u_full = [sem(f"ex_u_full{k}") for k in range(RG)]
        v_full = [sem(f"ex_v_full{k}") for k in range(RG)]
        u_free = sem("ex_u_free")
        v_free = sem("ex_v_free")
        iu_ready = sem("ex_iu_ready")
        iv_ready = sem("ex_iv_ready")
        picked = sem("ex_picked")
        index_moved = sem("ex_index_moved")
        chain = sem("ex_chain")
        dot_done = sem("ex_dot")
        hid_ready = sem("ex_hid_ready")
        act_done = sem("ex_act")
        exp_asked = sem("ex_exp_asked")
        gelu_asked = sem("ex_gelu_asked")
        gelu_done = sem("ex_gelu_done")
        wt_ready = sem("ex_wt_ready")
        diag_ready = sem("ex_diag_ready")
        y_ready = sem("ex_y_ready")
        y_squared = sem("ex_y_squared")
        root_asked = sem("ex_root_asked")
        root_done = sem("ex_root_done")
        y_free = sem("ex_y_free")
        y_done = sem("ex_y_done")
        tick = sem("ex_tick")

        def hold(engine, signal, value):
            engine.wait_ge(signal, value)
            engine.sem_inc(tick, 1)

        with nc.Block() as block:
            @block.sync
            def _(sp):
                sp.sem_inc(y_free, 1)
                sp.dma_start(gf[:], final_g.partition_broadcast(P)).then_inc(gf_in, 16)
                sp.dma_start(sc[:].rearrange("p b n -> p (b n)"), score_t[0]).then_inc(sc_in, 16)
                sp.dma_start(x2[:], x2_v[0]).then_inc(x2_in, 16)
                sp.dma_start(x1[:], x1_v[0]).then_inc(x1_in, 16)

                def load_scores(t):
                    sp.wait_ge(picked, t)
                    sp.dma_start(sc[:].rearrange("p b n -> p (b n)"), score_t[bass.ds(t, 1)].squeeze(0)).then_inc(sc_in, 16)

                def load_x2(t):
                    sp.wait_ge(hid_ready, t)
                    sp.dma_start(x2[:], x2_v[bass.ds(t, 1)].squeeze(0)).then_inc(x2_in, 16)

                def turn_over(t):
                    sp.wait_ge(y_done, t)
                    sp.dma_start(out_v[bass.ds(t - 1, 1)].squeeze(0), y[:]).then_inc(stored, 16)
                    sp.dma_start(x1[:], x1_v[bass.ds(t, 1)].squeeze(0)).then_inc(x1_in, 16)
                    sp.wait_ge(stored, 16 * t)
                    sp.sem_inc(y_free, 1)

                for g in range(key_ring):
                    rest.load(sp, g)
                for n in range(len(rest.units)):
                    rest.store(sp, n)
                    if n == 10:
                        load_scores(1)
                rest.all_stored(sp)
                load_scores(2)
                load_x2(1)
                with sp.Fori(1, TILES - 2) as t:
                    load_scores(t + 2)
                    load_x2(t + 1)
                    turn_over(t)
                load_x2(TILES - 1)
                turn_over(TILES - 2)
                turn_over(TILES - 1)
                sp.wait_ge(y_done, TILES)
                sp.dma_start(out_v[TILES - 1], y[:]).then_inc(stored, 16)
                sp.wait_ge(stored, 16 * TILES)

            @block.gpsimd
            def _(pool):
                nc.gpsimd.iota(ramp_i[:], pattern=[[1, TOPK]], base=0, channel_multiplier=0).then_inc(setup, 1)
                nc.gpsimd.memset(zero_i[:], 0).then_inc(setup, 1)
                pool.sem_inc(u_free, RG)
                pool.wait_ge(setup, 2)

                def gathers(t, j, half, table, ring, tile_index, stage, full, free, ready):
                    at = t * PICKS + j * RG
                    pool.wait_ge(free, at + 1)
                    nc.gpsimd.tensor_tensor(stage[:, half, :], tile_index[:, bass.ds(j * RG, RG)],
                                            zero_i[:, 0:RG], ALU.add).then_inc(ready, 1)
                    hold(pool, ready, t * GROUPS + j + 1)
                    for k in range(RG):
                        if k >= 1:
                            hold(pool, free, at + k + 1)
                        nc.gpsimd.indirect_dma_start(
                            out=ring[:, k, :], out_offset=None, in_=table,
                            in_offset=bass.IndirectOffsetOnAxis(ap=stage[:, half, k:k + 1], axis=0)).then_inc(full[k], 16)

                def copy_index(dest, source, value):
                    nc.gpsimd.tensor_tensor(dest[:], source[:], zero_i[:], ALU.add).then_inc(index_moved, 1)
                    hold(pool, index_moved, value)

                pool.wait_ge(picked, 1)
                copy_index(index_ut, index, 1)
                with pool.Fori(0, GROUPS // 2) as pair:
                    for half in range(2):
                        gathers(0, 2 * pair + half, half, peer_u, u, index_ut, index_u, u_full, u_free, iu_ready)
                with pool.Fori(0, TILES - 1) as t:
                    copy_index(index_vt, index_ut, 2 * t + 2)
                    hold(pool, picked, t + 2)
                    copy_index(index_ut, index, 2 * t + 3)
                    with pool.Fori(0, GROUPS // 2) as pair:
                        for half in range(2):
                            gathers(t, 2 * pair + half, half, peer_v, v, index_vt, index_v, v_full, v_free, iv_ready)
                            gathers(t + 1, 2 * pair + half, half, peer_u, u, index_ut, index_u, u_full, u_free, iu_ready)
                copy_index(index_vt, index_ut, 2 * TILES)
                with pool.Fori(0, GROUPS // 2) as pair:
                    for half in range(2):
                        gathers(TILES - 1, 2 * pair + half, half, peer_v, v, index_vt, index_v, v_full, v_free, iv_ready)

            @block.vector
            def _(dve):
                steps = [0]

                def link(ins, base):
                    steps[0] += 1
                    ins.then_inc(chain, 1)
                    hold(dve, chain, base + steps[0])

                def pick_half_first(t, base):
                    hold(dve, sc_in, 16 * (t + 1))
                    for b in range(SIDES):
                        nc.vector.max(half_v[:, b, 0:8], sc[:, b, :])
                    link(nc.vector.drain(), base)
                    for b in range(SIDES):
                        nc.vector.max_index(half_i[:, b, 0:8], half_v[:, b, 0:8], sc[:, b, :])
                        last = nc.vector.match_replace(left[:, b, :], half_v[:, b, 0:8], sc[:, b, :], LOWEST)
                    link(last, base)

                def pick_half_second(t, base):
                    for b in range(SIDES):
                        last = nc.vector.max(half_v[:, b, 8:16], left[:, b, :])
                    link(last, base)
                    for b in range(SIDES):
                        last = nc.vector.max_index(half_i[:, b, 8:16], half_v[:, b, 8:16], left[:, b, :])
                    link(last, base)
                    link(nc.vector.tensor_copy(half_f[:], half_i[:]), base)
                    for h in range(PH):
                        last = nc.vector.tensor_tensor(
                            cand[:, h, :, :], bcast(half_v[:, 2 * h, :].unsqueeze(2), [P, TOPK, TOPK]),
                            bcast(half_v[:, 2 * h + 1, :].unsqueeze(1), [P, TOPK, TOPK]), ALU.add)
                    link(last, base)

                flat = [cand[:, h, :, :].rearrange("p a b -> p (a b)") for h in range(PH)]
                g3 = gate_e[:].rearrange("p (h k) -> p h k", h=PH)
                flat2 = [cleft[:, h, :, :].rearrange("p a b -> p (a b)") for h in range(PH)]

                def pick_first(t, base):
                    for h in range(PH):
                        last = nc.vector.max(best[:, h, 0:8], flat[h])
                    link(last, base)
                    for h in range(PH):
                        nc.vector.max_index(pos[:, h, 0:8], best[:, h, 0:8], flat[h])
                        last = nc.vector.match_replace(flat2[h], best[:, h, 0:8], flat[h], LOWEST)
                    link(last, base)

                def pick_second(t, base):
                    for h in range(PH):
                        last = nc.vector.max(best[:, h, 8:16], flat2[h])
                    link(last, base)
                    for h in range(PH):
                        last = nc.vector.max_index(pos[:, h, 8:16], best[:, h, 8:16], flat2[h])
                    link(last, base)
                    pos_flat = pos[:].rearrange("p h k -> p (h k)")
                    nc.vector.tensor_scalar(part_i[:, 0, :], pos_flat, 4, None, ALU.logical_shift_right)
                    link(nc.vector.tensor_scalar(part_i[:, 1, :], pos_flat, 15, None, ALU.bitwise_and), base)
                    link(nc.vector.tensor_copy(part_f[:], part_i[:]), base)

                    nc.vector.tensor_tensor(g3, best[:], bcast(best[:, :, 0:1], [P, PH, TOPK]),
                                            ALU.subtract).then_inc(exp_asked, 1)

                def pick_rows(side, base):
                    halves = half_f[:].rearrange("p (h s) k -> p s h k", s=2)
                    link(nc.vector.tensor_tensor(hit[:], bcast(part_f[:, side, :].unsqueeze(2), [P, PICKS, TOPK]),
                                                 bcast(ramp[:].unsqueeze(1), [P, PICKS, TOPK]), ALU.is_equal), base)
                    for h in range(PH):
                        hh = hit[:, h * TOPK:(h + 1) * TOPK, :]
                        last = nc.vector.tensor_tensor(hh, hh, bcast(halves[:, side, h, :].unsqueeze(1),
                                                                     [P, TOPK, TOPK]), ALU.mult)
                    link(last, base)
                    link(nc.vector.tensor_reduce(row[:, side, :], hit[:], AX, ALU.add), base)

                def pick_gates(t, base):
                    link(nc.vector.scalar_tensor_tensor(out=index_f[:], in0=row[:, 0, :], scalar=float(NK),
                                                        in1=row[:, 1, :], op0=ALU.mult, op1=ALU.add), base)
                    if not isinstance(t, int):
                        hold(dve, index_moved, 2 * t - 1)
                    elif t >= 1:
                        dve.wait_ge(index_moved, 2 * t - 1)
                    link(nc.vector.tensor_copy(index[:], index_f[:]), base)
                    hold(dve, act_done, t + 1)
                    link(nc.vector.tensor_reduce(gsum[:, 0, :], g3, AX, ALU.add), base)
                    link(nc.vector.reciprocal(gsum[:, 1, :], gsum[:, 0, :]), base)
                    link(nc.vector.tensor_tensor(
                        gates[:, bass.ds(t % 2, 1), :].rearrange("p one (h k) -> p (one h) k", h=PH), g3,
                        bcast(gsum[:, 1, :].unsqueeze(2), [P, PH, TOPK]), ALU.mult), base)
                    dve.sem_inc(picked, 1)

                def dot_group(t, j):
                    at = t * PICKS + j * RG
                    for k in range(RG):
                        dve.wait_ge(u_full[k], 16 * (t * GROUPS + j + 1))
                        nc.vector.tensor_tensor_reduce(out=prod[:], in0=u[:, k, :], in1=x2[:], scale=1.0, scalar=0.0,
                                                       op0=ALU.mult, op1=ALU.add,
                                                       accum_out=dots[:, k:k + 1]).then_inc(u_free, 1)
                        dve.wait_ge(u_free, at + RG + k + 1)
                    nc.vector.tensor_copy(hid[:, bass.ds(j * RG, RG)], dots[:]).then_inc(dot_done, 1)
                    hold(dve, dot_done, t * GROUPS + j + 1)

                def weigh(t, base, has_prev):
                    nc.vector.tensor_tensor(ga[:, 0, :], hid[:], hid[:], ALU.mult).then_inc(hid_ready, 1)
                    dve.wait_ge(hid_ready, t + 1)
                    link(nc.vector.tensor_scalar(ga[:, 1, :], ga[:, 0, :], GELU_A, 1.0, ALU.mult, ALU.add), base)
                    link(nc.vector.tensor_tensor(ga[:, 0, :], ga[:, 1, :], hid[:], ALU.mult), base)
                    nc.vector.tensor_scalar(ga[:, 2, :], ga[:, 0, :], -50.0, None, ALU.max).then_inc(gelu_asked, 1)
                    dve.wait_ge(gelu_done, t + 1)
                    link(nc.vector.tensor_scalar(ga[:, 1, :], ga[:, 3, :], 1.0, None, ALU.add), base)
                    link(nc.vector.reciprocal(ga[:, 0, :], ga[:, 1, :]), base)
                    link(nc.vector.tensor_tensor(ga[:, 1, :], ga[:, 0, :], hid[:], ALU.mult), base)
                    if has_prev:
                        hold(dve, diag_ready, t * PICKS)
                    link(nc.vector.tensor_tensor(wt[:], ga[:, 1, :], gates[:, bass.ds(t % 2, 1), :].squeeze(1), ALU.mult), base)
                    dve.sem_inc(wt_ready, 1)

                def finish(t, base):
                    dve.wait_ge(v_free, (t + 1) * PICKS + RG)
                    dve.wait_ge(x1_in, 16 * (t + 1))
                    dve.wait_ge(y_free, t + 1)
                    nc.vector.tensor_tensor(y[:], acc[:], x1[:], ALU.add).then_inc(y_ready, 1)
                    dve.wait_ge(y_squared, t + 1)
                    nc.vector.tensor_scalar(fs[:, 1:2], fs[:, 0:1], 1.0 / D, EPS, ALU.mult, ALU.add).then_inc(root_asked, 1)
                    dve.wait_ge(root_done, 2 * (t + 1))
                    link(nc.vector.tensor_tensor(fs[:, 4:5], fs[:, 3:4], fs[:, 1:2], ALU.mult), base)
                    link(nc.vector.tensor_tensor(fs[:, 5:6], fs[:, 4:5], fs[:, 3:4], ALU.mult), base)
                    link(nc.vector.tensor_scalar(fs[:, 6:7], fs[:, 5:6], -0.5, 1.5, ALU.mult, ALU.add), base)
                    link(nc.vector.tensor_tensor(fs[:, 7:8], fs[:, 6:7], fs[:, 3:4], ALU.mult), base)
                    link(nc.vector.tensor_scalar(y[:], y[:], fs[:, 7:8], None, ALU.mult), base)
                    nc.vector.tensor_tensor(y[:], y[:], gf[:], ALU.mult).then_inc(y_done, 1)

                dve.wait_ge(setup, 2)
                nc.vector.tensor_copy(ramp[:], ramp_i[:]).then_inc(setup, 1)
                dve.wait_ge(setup, 3)
                dve.wait_ge(gf_in, 16)

                def dot_pair(t, pair):
                    for half in range(2):
                        dot_group(t, 2 * pair + half)

                def tile(t, base, last_tile, has_prev):
                    hold(dve, x2_in, 16 * (t + 1))
                    if last_tile:
                        with dve.Fori(0, GROUPS // 2) as pair:
                            dot_pair(t, pair)
                    else:
                        dot_pair(t, 0)
                        pick_half_first(t + 1, base)
                        dot_pair(t, 1)
                        pick_half_second(t + 1, base)
                        dot_pair(t, 2)
                        pick_first(t + 1, base)
                        dot_pair(t, 3)
                        pick_second(t + 1, base)
                        dot_pair(t, 4)
                        pick_rows(0, base)
                        dot_pair(t, 5)
                        pick_rows(1, base)
                        dot_pair(t, 6)
                        pick_gates(t + 1, base)
                        dot_pair(t, 7)
                    weigh(t, base, has_prev)
                    if has_prev:
                        finish(t - 1, base)

                pick_half_first(0, 0)
                pick_half_second(0, 0)
                pick_first(0, 0)
                pick_second(0, 0)
                pick_rows(0, 0)
                pick_rows(1, 0)
                pick_gates(0, 0)
                tile(0, 0, False, False)
                after_first = steps[0]
                steps[0] = 0
                probe = len_of_tile()
                with dve.Fori(1, TILES - 1) as t:
                    tile(t, (t - 1) * probe + after_first, False, True)
                assert steps[0] == probe
                steps[0] = 0
                base = after_first + (TILES - 2) * probe
                tile(TILES - 1, base, True, True)
                finish(TILES - 1, base)

            @block.scalar
            def _(act):
                def gate_exp(t):
                    act.wait_ge(exp_asked, t + 1)
                    nc.scalar.activation(gate_e[:], gate_e[:], ACT.Exp).then_inc(act_done, 1)

                def gelu_exp(t):
                    act.wait_ge(gelu_asked, t + 1)
                    nc.scalar.activation(ga[:, 3, :], ga[:, 2, :], ACT.Exp, scale=-2.0 * GELU_C).then_inc(gelu_done, 1)

                def square(t):
                    act.wait_ge(y_ready, t + 1)
                    nc.scalar.activation(ysq[:], y[:], ACT.Square, accum_out=fs[:, 0:1]).then_inc(y_squared, 1)
                    act.wait_ge(root_asked, t + 1)
                    nc.scalar.activation(fs[:, 2:3], fs[:, 1:2], ACT.Ln).then_inc(root_done, 1)
                    act.wait_ge(root_done, 2 * t + 1)
                    nc.scalar.activation(fs[:, 3:4], fs[:, 2:3], ACT.Exp, scale=-0.5).then_inc(root_done, 1)

                def diagonals(t, first, last):
                    with act.Fori(first, last) as j:
                        at = t * PICKS + j * RG
                        for k in range(RG):
                            act.wait_ge(v_free, at + k + 1)
                            nc.scalar.activation(diag[:, k, :], ident[:], ACT.Copy,
                                                 scale=wt[:, bass.ds(j * RG + k, 1)]).then_inc(diag_ready, 1)

                def tile(t, last_pick, has_prev):
                    gelu_exp(t)
                    if has_prev:
                        square(t - 1)
                    act.wait_ge(wt_ready, t + 1)
                    diagonals(t, 0, ASKED)
                    if not last_pick:
                        gate_exp(t + 2)
                    diagonals(t, ASKED, GROUPS)

                ASKED = GROUPS // 2 + 2
                for n in range(len(rest.units)):
                    rest.evacuate(act, n)
                    if n == 6:
                        gate_exp(0)
                gate_exp(1)
                tile(0, False, False)
                with act.Fori(1, TILES - 2) as t:
                    tile(t, False, True)
                tile(TILES - 2, True, True)
                tile(TILES - 1, True, True)
                square(TILES - 1)

            @block.tensor
            def _(pe):
                def group(t, j, first, last):
                    at = t * PICKS + j * RG
                    for k in range(RG):
                        pe.wait_ge(v_full[k], 16 * (t * GROUPS + j + 1))
                        pe.wait_ge(diag_ready, at + k + 1)
                        for hf in range(2):
                            ins = nc.tensor.matmul(acc[:, hf * HALF:(hf + 1) * HALF], diag[:, k, :],
                                                   v[:, k, hf * HALF:(hf + 1) * HALF],
                                                   start=first and k == 0, stop=last and k == RG - 1)
                        ins.then_inc(v_free, 1)

                def tile(t):
                    group(t, 0, True, False)
                    with pe.Fori(1, GROUPS - 1) as j:
                        group(t, j, False, False)
                    group(t, GROUPS - 1, False, True)

                rest.multiply(pe)
                pe.wait_ge(rest.s_ready, len(rest.units))
                pe.sem_inc(v_free, RG)
                tile(0)
                with pe.Fori(1, TILES) as t:
                    pe.wait_ge(y_ready, t)
                    tile(t)


def len_of_tile():
    return 6 + 5 + (10 + 2 + 2 * 3 + 2 + 3)


def build(nc, x, norm1_g, w_in, sb_out_g, swa_out_g, swa_sinks, w_out, norm2_g, peer_w_q, peer_keys1, peer_keys2,
          peer_u, peer_v, final_g, out):
    x1_dram = nc.dram_tensor("x1_scratch", (SEQ, D), F32, kind="Internal").ap()
    x2_dram = nc.dram_tensor("x2_scratch", (SEQ, D), F32, kind="Internal").ap()
    score_dram = nc.dram_tensor("score_scratch", (SEQ, SIDES * NK), F32, kind="Internal").ap()
    with ExitStack() as ctx:
        def sem(name):
            return ctx.enter_context(nc.semaphore(name))

        ident, tri, ones, bias, minus_half = constants(nc, ctx, sem)
        x2_t = ctx.enter_context(nc.sbuf_tensor("x2_t", [P, CH, SEQ], F32))
        keys_t = ctx.enter_context(nc.sbuf_tensor("keys_t", [P, SIDES, NK], F32))
        with ExitStack() as held:
            mixed = held.enter_context(nc.sbuf_tensor("mixed", [P, TILES, D], F32))
            with ExitStack() as heads:
                def hb(name, shape):
                    return heads.enter_context(nc.sbuf_tensor(name, shape, F32))

                qk_t = hb("qk_t", [P, HEADS, SEQ])
                sb_v = hb("sb_v", [P, TILES, D_SB])
                wq_t = hb("wq_t", [P, HEADS // 2, SEQ])
                wk_t = hb("wk_t", [P, KV, SEQ])
                sw_v = hb("sw_v", [P, TILES, KV * DH])
                project(nc, sem, x, norm1_g, w_in, ident, minus_half, x2_t, mixed, qk_t, sb_v, wq_t, wk_t, sw_v)
                stick(nc, sem, ident, tri, ones, x2_t, qk_t, sb_v, mixed)
                window(nc, sem, swa_sinks, ident, bias, wq_t, wk_t, sw_v, mixed)
            mix(nc, sem, x, sb_out_g, swa_out_g, w_out, norm2_g, ident, minus_half, mixed, x1_dram, x2_dram, x2_t)
        key_scores(nc, sem, peer_w_q, peer_keys1, peer_keys2, ident, x2_t, keys_t, score_dram)
        experts(nc, sem, ident, keys_t, peer_w_q, x2_t, score_dram, x1_dram, x2_dram, peer_u, peer_v, final_g, out)


_INS = ["x", "norm1_g", "w_in", "sb_out_g", "swa_out_g", "swa_sinks", "w_out", "norm2_g", "peer_w_q", "peer_keys1",
        "peer_keys2", "peer_u", "peer_v", "final_g"]


def kernel(**inputs):
    import numpy as _np
    import concourse.bacc as _bacc
    from concourse import mybir as _mybir
    from concourse.bass_utils import run_bass_kernel_spmd as _run

    nc = _bacc.Bacc("TRN2", target_bir_lowering=False, num_devices=1)
    arrays, args = {}, []
    for name in _INS:
        a = _np.ascontiguousarray(inputs[name])
        if name != "final_g":
            a = a[0]
        arrays[f"in_{name}"] = a
        args.append(nc.dram_tensor(f"in_{name}", a.shape, _mybir.dt.from_np(a.dtype), kind="ExternalInput").ap())
    result = nc.dram_tensor("out_0", (SEQ, D), _mybir.dt.float32, kind="ExternalOutput").ap()
    build(nc, *args, result)
    r = _run(nc, [arrays], core_ids=[0])
    return r.results[0]["out_0"].reshape(1, SEQ, D)
```

```python
from contextlib import ExitStack

import concourse.bass as bass
from concourse import mybir

F32 = mybir.dt.float32
I32 = mybir.dt.int32
U32 = mybir.dt.uint32
ALU = mybir.AluOpType
ACT = mybir.ActivationFunctionType
AX = mybir.AxisListType.X

P = 128
SEQ = 1024
D = 1024
TILES = SEQ // P
CH = D // P
HALF = 512
DH = 64
HEADS = 8
D_SB = HEADS * DH
KV = 2
GRP = HEADS // KV
D_IN = 3 * D_SB + HEADS * DH + 2 * KV * DH
COLS = 256
PH = 8
NK = 128
TOPK = 16
PICKS = PH * TOPK
SIDES = 2 * PH
EPS = 1e-6
LOW = -1.0e30
EARLY = 2
LOWEST = -3.0e38
GELU_C = 0.7978845608028654
GELU_A = 0.044715


def place(h):
    return (h % 2) * (HEADS // 2) + h // 2


def place4(g):
    return (g % 2) * (GRP // 2) + g // 2


def bcast(ap, shape):
    return ap.to_broadcast(shape)


def constants(nc, ctx, sem):
    def sb(name, shape, dt=F32):
        return ctx.enter_context(nc.sbuf_tensor(name, shape, dt))

    ident = sb("ident", [P, P])
    tri = sb("tri", [P, P])
    ones = sb("ones", [P, P])
    bias = sb("bias", [P, HEADS, 2 * P])
    minus_half = sb("minus_half", [P, 2 * HEADS])
    dist_i = sb("dist_i", [P, 2 * P], I32)
    dist = sb("dist", [P, 2 * P])
    blank = sem("blank")
    made = sem("made")
    dist_ready = sem("dist_ready")
    slope_done = sem("slope_done")

    with nc.Block() as block:
        @block.gpsimd
        def _(pool):
            nc.gpsimd.memset(ident[:], 0.0).then_inc(blank, 1)
            nc.gpsimd.memset(tri[:], 1.0).then_inc(blank, 1)
            nc.gpsimd.memset(ones[:], 1.0).then_inc(blank, 1)
            nc.gpsimd.memset(minus_half[:], -0.5).then_inc(blank, 1)
            nc.gpsimd.iota(dist_i[:], pattern=[[-1, 2 * P]], base=P, channel_multiplier=1).then_inc(dist_ready, 1)
            pool.wait_ge(blank, 4)
            nc.gpsimd.affine_select(out=ident[:], in_=ident[:], compare_op=ALU.not_equal, fill=1.0, base=0,
                                    pattern=[[-1, P]], channel_multiplier=1).then_inc(made, 1)
            nc.gpsimd.affine_select(out=tri[:], in_=tri[:], compare_op=ALU.is_ge, fill=0.0, base=0,
                                    pattern=[[-1, P]], channel_multiplier=1).then_inc(made, 1)

        @block.vector
        def _(dve):
            dve.wait_ge(dist_ready, 1)
            nc.vector.tensor_copy(dist[:], dist_i[:]).then_inc(dist_ready, 1)
            dve.wait_ge(dist_ready, 2)
            for h in range(HEADS):
                at = h // GRP * GRP + place4(h % GRP)
                nc.vector.tensor_scalar(bias[:, at, :], dist[:], -(2.0 ** -(8.0 * (h + 1) / HEADS)), None,
                                        ALU.mult).then_inc(slope_done, 1)
    return ident, tri, ones, bias, minus_half


def project(nc, sem, x, norm1_g, w_in, ident, minus_half, bias, h_t, mixed, qk_t, sb_v, wq_t, wk_t, sw_v):
    groups = D_IN // COLS
    ring = 4
    XR = 4
    w_view = w_in.rearrange("(c p) n -> p c n", p=P)
    with ExitStack() as ctx:
        xs, xn = mixed[:, 0:XR, :], mixed[:, XR:XR + 2, :]
        w = ctx.enter_context(nc.sbuf_tensor("pj_w", [P, ring, CH, COLS], F32))
        w_twice = ctx.enter_context(nc.sbuf_tensor("pj_w_twice", [P, KV, CH, 2, DH], F32))
        g_t = ctx.enter_context(nc.sbuf_tensor("pj_g", [P, CH], F32))
        ss = ctx.enter_context(nc.sbuf_tensor("pj_ss", [P, TILES], F32))
        ms = ctx.enter_context(nc.sbuf_tensor("pj_ms", [P, TILES], F32))
        rstd = ctx.enter_context(nc.sbuf_tensor("pj_rstd", [P, TILES], F32))
        tp = ctx.enter_context(nc.psum_tensor("pj_tp", [P, 2, CH, P], F32))
        acc = ctx.enter_context(nc.psum_tensor("pj_acc", [P, 4, HALF], F32))

        x_in = [sem(f"pj_x_in{t}") for t in range(TILES)]
        w_loaded = [sem(f"pj_w_in{s}") for s in range(ring)]
        g_in = sem("pj_g_in")
        squared = sem("pj_squared")
        mean_done = sem("pj_mean")
        rstd_done = sem("pj_rstd_done")
        normed = sem("pj_normed")
        turned = sem("pj_turned")
        ht_ready = sem("pj_ht_ready")
        twice_ready = sem("pj_twice_ready")
        bias_cut = sem("pj_bias_cut")
        acc_full = sem("pj_acc_full")
        acc_read = sem("pj_acc_read")

        units = []
        for g in range(groups):
            for j in range(2):
                col = g * COLS + j * P
                if col < 2 * D_SB:
                    units += [(g, "t", j * P, hf, qk_t[:, col // P, hf * HALF:(hf + 1) * HALF],
                               DH ** -0.5 if col < D_SB else 1.0) for hf in range(2)]
                elif 3 * D_SB <= col < 3 * D_SB + HEADS * DH:
                    b = (col - 3 * D_SB) // P
                    units += [(g, "t", j * P, hf, wq_t[:, b, hf * HALF:(hf + 1) * HALF], DH ** -0.5)
                              for hf in range(2)]
            if 2 * D_SB <= g * COLS < 3 * D_SB:
                c0 = g * COLS - 2 * D_SB
                units += [(g, "v", (0, COLS), t, sb_v[:, t, c0:c0 + COLS], 1.0) for t in range(TILES)]
            if g == groups - 1:
                units += [(g, "k", kv, hf, wk_t[:, kv, hf * HALF:(hf + 1) * HALF], 1.0)
                          for kv in range(KV) for hf in range(2)]
                units += [(g, "v", (P, P), t, sw_v[:, t, :], 1.0) for t in range(TILES)]

        ends = [1 + max(n for n, unit in enumerate(units) if unit[0] == g) for g in range(groups)]

        with nc.Block() as block:
            @block.sync
            def _(sp):
                with nc.allow_non_contiguous_dma(reason="one gain per feature, 4 KB in all"):
                    sp.dma_start(g_t[:], norm1_g.rearrange("(c p) -> p c", p=P)).then_inc(g_in, 16)
                for t in range(TILES):
                    if t >= XR:
                        sp.wait_ge(normed, t - XR + 1)
                    sp.dma_start(xs[:, t % XR, :], x[t * P:(t + 1) * P, :]).then_inc(x_in[t], 16)
                for g in range(groups):
                    if g >= ring:
                        sp.wait_ge(acc_full, ends[g - ring])
                    sp.dma_start(w[:, g % ring, :, :], w_view[:, :, g * COLS:(g + 1) * COLS]).then_inc(
                        w_loaded[g % ring], 16)

            @block.scalar
            def _(act):
                for t in range(TILES):
                    act.wait_ge(x_in[t], 16)
                    if t >= 2:
                        act.wait_ge(turned, t - 1)
                    nc.scalar.activation(xn[:, t % 2, :], xs[:, t % XR, :], ACT.Square,
                                         accum_out=ss[:, t:t + 1]).then_inc(squared, 1)
                for n, (_, _, _, _, dest, scale) in enumerate(units):
                    act.wait_ge(acc_full, n + 1)
                    width = dest.shape[-1]
                    nc.scalar.activation(dest, acc[:, n % 4, 0:width], ACT.Copy, scale=scale).then_inc(acc_read, 1)

            @block.gpsimd
            def _(pool):
                for t in range(TILES):
                    pool.wait_ge(mean_done, t + 1)
                    nc.gpsimd.tensor_tensor(rstd[:, t:t + 1], ms[:, t:t + 1], minus_half[:, 0:1], ALU.pow).then_inc(rstd_done, 1)
                nc.gpsimd.affine_select(out=bias[:], in_=bias[:], compare_op=ALU.is_ge, fill=LOW, base=P,
                                        pattern=[[0, HEADS], [-1, 2 * P]], channel_multiplier=1).then_inc(bias_cut, 1)
                pool.wait_ge(bias_cut, 1)
                nc.gpsimd.affine_select(out=bias[:], in_=bias[:], compare_op=ALU.is_ge, fill=LOW, base=-1,
                                        pattern=[[0, HEADS], [1, 2 * P]], channel_multiplier=-1).then_inc(bias_cut, 1)

            @block.vector
            def _(dve):
                def evacuate(t):
                    dve.wait_ge(turned, t + 1)
                    nc.vector.tensor_tensor(h_t[:, :, t * P:(t + 1) * P], tp[:, t % 2, :, :],
                                            bcast(g_t[:, :].unsqueeze(2), [P, CH, P]), ALU.mult).then_inc(ht_ready, 1)

                dve.wait_ge(g_in, 16)
                for t in range(TILES):
                    dve.wait_ge(squared, t + 1)
                    nc.vector.tensor_scalar(ms[:, t:t + 1], ss[:, t:t + 1], 1.0 / D, EPS, ALU.mult,
                                            ALU.add).then_inc(mean_done, 1)
                    dve.wait_ge(rstd_done, t + 1)
                    nc.vector.tensor_scalar(xn[:, t % 2, :], xs[:, t % XR, :], rstd[:, t:t + 1], None,
                                            ALU.mult).then_inc(normed, 1)
                    if t >= 1:
                        evacuate(t - 1)
                evacuate(TILES - 1)
                g = groups - 1
                dve.wait_ge(w_loaded[g % ring], 16 * (g // ring + 1))
                for kv in range(KV):
                    nc.vector.tensor_copy(w_twice[:, kv, :, :, :],
                                          bcast(w[:, g % ring, :, kv * DH:(kv + 1) * DH].unsqueeze(2),
                                                [P, CH, 2, DH])).then_inc(twice_ready, 1)

            @block.tensor
            def _(pe):
                for t in range(TILES):
                    pe.wait_ge(normed, t + 1)
                    if t >= 2:
                        pe.wait_ge(ht_ready, t - 1)
                    for c in range(CH):
                        last = nc.tensor.transpose(tp[:, t % 2, c, :], xn[:, t % 2, c * P:(c + 1) * P], ident[:])
                    last.then_inc(turned, 1)
                pe.wait_ge(ht_ready, TILES)
                for n, (g, kind, at, part, dest, _) in enumerate(units):
                    slot = w[:, g % ring, :, :]
                    if n == 0 or units[n - 1][0] != g:
                        pe.wait_ge(w_loaded[g % ring], 16 * (g // ring + 1))
                    if kind == "k":
                        pe.wait_ge(twice_ready, KV)
                    if n >= 4:
                        pe.wait_ge(acc_read, n - 3)
                    for c in range(CH):
                        st = dict(start=c == 0, stop=c == CH - 1)
                        if kind == "v":
                            last = nc.tensor.matmul(acc[:, n % 4, 0:at[1]], h_t[:, c, part * P:(part + 1) * P],
                                                    slot[:, c, at[0]:at[0] + at[1]], **st)
                        elif kind == "t":
                            last = nc.tensor.matmul(acc[:, n % 4, :], slot[:, c, at:at + P],
                                                    h_t[:, c, part * HALF:(part + 1) * HALF], **st)
                        else:
                            last = nc.tensor.matmul(acc[:, n % 4, :], w_twice[:, at, c, :, :].rearrange("p r d -> p (r d)"),
                                                    h_t[:, c, part * HALF:(part + 1) * HALF], **st)
                    last.then_inc(acc_full, 1)


def stick(nc, sem, ident, tri, ones, spare, qk_t, sb_v, mixed):
    steps = [(i, kb) for i in range(TILES) for kb in range(i, -1, -1)]
    W = HEADS * P
    with ExitStack() as ctx:
        lsp, a = spare[:, 0:2, :], spare[:, 2:4, :]
        zs = ctx.enter_context(nc.sbuf_tensor("st_zs", [P, 4, W], F32))
        soft = ctx.enter_context(nc.sbuf_tensor("st_sp", [P, 3, W], F32))
        later = ctx.enter_context(nc.sbuf_tensor("st_s", [P, 3, W], F32))
        o_sb = ctx.enter_context(nc.sbuf_tensor("st_o_sb", [P, D_SB], F32))
        z = ctx.enter_context(nc.psum_tensor("st_z", [P, 2, W], F32))
        csum = ctx.enter_context(nc.psum_tensor("st_c", [P, W], F32))
        o = ctx.enter_context(nc.psum_tensor("st_o", [P, 2, D_SB], F32))

        z_ready = sem("st_z_ready")
        z_copied = sem("st_z_copied")
        abs_done = sem("st_abs")
        exp_done = sem("st_exp")
        log_done = sem("st_log")
        soft_done = sem("st_soft")
        soft_cut = sem("st_soft_cut")
        later_done = sem("st_later")
        sum_done = sem("st_sum")
        diff_done = sem("st_diff")
        diff_cut = sem("st_diff_cut")
        a_ready = sem("st_a_ready")
        pv_done = sem("st_pv")
        o_copied = sem("st_o_copied")
        o_turned = sem("st_o_turned")
        o_read = sem("st_o_read")

        def is_sum(n):
            return steps[n][1] < steps[n][0] - 1

        sums = [sum(is_sum(m) for m in range(n + 1)) for n in range(len(steps))]

        def carry_of(n):
            return later[:, n % 3, :] if is_sum(n) else soft[:, (n - 1) % 3, :]

        with nc.Block() as block:
            @block.tensor
            def _(pe):
                def scores(n):
                    i, kb = steps[n]
                    if n >= 2:
                        pe.wait_ge(z_copied, n - 1)
                    for h in range(HEADS):
                        lo = DH * (h % 2)
                        last = nc.tensor.matmul(z[:, n % 2, place(h) * P:(place(h) + 1) * P],
                                                qk_t[lo:lo + DH, HEADS // 2 + h // 2, kb * P:(kb + 1) * P],
                                                qk_t[lo:lo + DH, h // 2, i * P:(i + 1) * P], start=True, stop=True)
                    last.then_inc(z_ready, 1)

                def suffix(n):
                    i, kb = steps[n]
                    if n >= 1:
                        pe.wait_ge(diff_done, n)
                    if kb == i:
                        pe.wait_ge(soft_cut, i + 1)
                    else:
                        pe.wait_ge(soft_done, n + 1)
                        if is_sum(n):
                            pe.wait_ge(later_done, sums[n])
                    for hf in range(2):
                        cols = slice(hf * HALF, (hf + 1) * HALF)
                        last = nc.tensor.matmul(csum[:, cols], tri[:], soft[:, n % 3, cols], start=True, stop=kb == i)
                        if kb < i:
                            last = nc.tensor.matmul(csum[:, cols], ones[:], carry_of(n)[:, cols], start=False, stop=True)
                    last.then_inc(sum_done, 1)

                def values(n):
                    i, kb = steps[n]
                    pe.wait_ge(a_ready, n + 1)
                    if kb == i and i >= 2:
                        pe.wait_ge(o_read, i - 1)
                    for h in range(HEADS):
                        lo = DH * (h % 2)
                        last = nc.tensor.matmul(o[lo:lo + DH, i % 2, (h // 2) * P:(h // 2 + 1) * P],
                                                sb_v[:, kb, h * DH:(h + 1) * DH],
                                                a[:, n % 2, place(h) * P:(place(h) + 1) * P],
                                                start=kb == i and h < 2, stop=kb == 0,
                                                skip_group_check=True)
                    last.then_inc(pv_done, 1)

                def turn_output(i):
                    pe.wait_ge(o_copied, i + 1)
                    for b in range(HEADS // 2):
                        last = nc.tensor.transpose(o[:, i % 2, b * P:(b + 1) * P], o_sb[:, b * P:(b + 1) * P], ident[:])
                    last.then_inc(o_turned, 1)

                for n in range(3):
                    scores(n)
                for n in range(len(steps)):
                    if n + 3 < len(steps):
                        scores(n + 3)
                    suffix(n)
                    if n >= 1:
                        values(n - 1)
                    if n >= 2 and steps[n - 2][1] == 0:
                        turn_output(steps[n - 2][0])
                values(len(steps) - 1)
                turn_output(TILES - 1)

            @block.scalar
            def _(act):
                def copy(n):
                    act.wait_ge(z_ready, n + 1)
                    if n >= 4:
                        act.wait_ge(diff_done, n - 3)
                    nc.scalar.activation(zs[:, n % 4, :], z[:, n % 2, :], ACT.Copy).then_inc(z_copied, 1)

                def log_terms(n):
                    act.wait_ge(abs_done, n + 1)
                    nc.scalar.activation(lsp[:, n % 2, :], lsp[:, n % 2, :], ACT.Exp, scale=-1.0).then_inc(exp_done, 1)
                    act.wait_ge(exp_done, n + 1)
                    nc.scalar.activation(lsp[:, n % 2, :], lsp[:, n % 2, :], ACT.Ln, bias=1.0).then_inc(log_done, 1)

                def weights(n):
                    i, kb = steps[n]
                    act.wait_ge(diff_done, n + 1)
                    if kb == i:
                        act.wait_ge(diff_cut, i + 1)
                    nc.scalar.activation(a[:, n % 2, :], a[:, n % 2, :], ACT.Exp).then_inc(a_ready, 1)

                nc.scalar.preload_act_table_set("natural_log_exp_and_others")
                for n in range(3):
                    copy(n)
                log_terms(0)
                log_terms(1)
                for n in range(len(steps)):
                    if n + 3 < len(steps):
                        copy(n + 3)
                    if n + 2 < len(steps):
                        log_terms(n + 2)
                    weights(n)

            @block.vector
            def _(dve):
                def copy_output(i):
                    dve.wait_ge(pv_done, (i + 1) * (i + 2) // 2)
                    if i >= 1:
                        dve.wait_ge(o_turned, i)
                    nc.vector.tensor_copy(o_sb[:], o[:, i % 2, :]).then_inc(o_copied, 1)

                def read_out(i):
                    dve.wait_ge(o_turned, i + 1)
                    nc.vector.tensor_copy(mixed[:, i, 0:D_SB], o[:, i % 2, :]).then_inc(o_read, 1)

                def magnitude(n):
                    dve.wait_ge(z_copied, n + 1)
                    if n >= 2:
                        dve.wait_ge(soft_done, n - 1)
                    nc.vector.scalar_tensor_tensor(out=lsp[:, n % 2, :], in0=zs[:, n % 4, :], scalar=-1.0,
                                                   in1=zs[:, n % 4, :], op0=ALU.mult, op1=ALU.max).then_inc(abs_done, 1)

                def softplus(n):
                    dve.wait_ge(log_done, n + 1)
                    if n >= 3:
                        dve.wait_ge(sum_done, n - 1)
                    nc.vector.scalar_tensor_tensor(out=soft[:, n % 3, :], in0=zs[:, n % 4, :], scalar=0.0,
                                                   in1=lsp[:, n % 2, :], op0=ALU.max, op1=ALU.add).then_inc(soft_done, 1)

                def carry(n):
                    dve.wait_ge(soft_done, n)
                    if is_sum(n - 1):
                        dve.wait_ge(later_done, sums[n - 1])
                    else:
                        dve.wait_ge(soft_cut, steps[n][0] + 1)
                    if n >= 3:
                        dve.wait_ge(sum_done, n - 2)
                    nc.vector.tensor_tensor(later[:, n % 3, :], carry_of(n - 1), soft[:, (n - 1) % 3, :],
                                            ALU.add).then_inc(later_done, 1)

                def difference(n):
                    dve.wait_ge(sum_done, n + 1)
                    if n >= 2:
                        dve.wait_ge(pv_done, n - 1)
                    nc.vector.tensor_tensor(a[:, n % 2, :], zs[:, n % 4, :], csum[:, :], ALU.subtract).then_inc(diff_done, 1)

                magnitude(0)
                magnitude(1)
                softplus(0)
                magnitude(2)
                for n, (i, kb) in enumerate(steps):
                    if n + 1 < len(steps):
                        softplus(n + 1)
                    if n + 2 < len(steps) and is_sum(n + 2):
                        carry(n + 2)
                    if n + 3 < len(steps):
                        magnitude(n + 3)
                    if n >= 2 and steps[n - 2][1] == 0:
                        copy_output(steps[n - 2][0])
                    if n >= 3 and steps[n - 3][1] == 0:
                        read_out(steps[n - 3][0])
                    difference(n)
                copy_output(TILES - 1)
                read_out(TILES - 1)

            @block.gpsimd
            def _(pool):
                for n, (i, kb) in enumerate(steps):
                    if kb == i:
                        pool.wait_ge(soft_done, n + 1)
                        cut = soft[:, n % 3, :].rearrange("p (h q) -> p h q", h=HEADS)
                        nc.gpsimd.affine_select(out=cut, in_=cut, compare_op=ALU.is_gt, fill=0.0, base=0,
                                                pattern=[[0, HEADS], [1, P]], channel_multiplier=-1).then_inc(soft_cut, 1)
                        pool.wait_ge(diff_done, n + 1)
                        cut = a[:, n % 2, :].rearrange("p (h q) -> p h q", h=HEADS)
                        nc.gpsimd.affine_select(out=cut, in_=cut, compare_op=ALU.is_gt, fill=LOW, base=0,
                                                pattern=[[0, HEADS], [1, P]], channel_multiplier=-1).then_inc(diff_cut, 1)


def window(nc, sem, sinks, ident, bias, wq_t, wk_t, sw_v, mixed, w_out, w_dest, w_out_in):
    steps = [(i, kv) for i in range(TILES) for kv in range(KV)]
    with ExitStack() as ctx:
        sink_row = ctx.enter_context(nc.sbuf_tensor("wd_sink_row", [P, HEADS], F32))
        sink = ctx.enter_context(nc.sbuf_tensor("wd_sink", [P, HEADS], F32))
        p = ctx.enter_context(nc.sbuf_tensor("wd_p", [P, 2, GRP, 2 * P], F32))
        p_t = ctx.enter_context(nc.sbuf_tensor("wd_pt", [P, 2, GRP, 2, P], F32))
        top = ctx.enter_context(nc.sbuf_tensor("wd_top", [P, 4, GRP], F32))
        peak = ctx.enter_context(nc.sbuf_tensor("wd_peak", [P, 4, GRP], F32))
        neg = ctx.enter_context(nc.sbuf_tensor("wd_neg", [P, 4, GRP], F32))
        sd = ctx.enter_context(nc.sbuf_tensor("wd_sd", [P, 4, GRP], F32))
        es = ctx.enter_context(nc.sbuf_tensor("wd_es", [P, 4, GRP], F32))
        rs = ctx.enter_context(nc.sbuf_tensor("wd_rs", [P, 4, GRP], F32))
        den = ctx.enter_context(nc.sbuf_tensor("wd_den", [P, 4, GRP], F32))
        rden = ctx.enter_context(nc.sbuf_tensor("wd_rden", [P, 4, GRP], F32))
        s = ctx.enter_context(nc.psum_tensor("wd_s", [P, 2, GRP, 2 * P], F32))
        tp = ctx.enter_context(nc.psum_tensor("wd_tp", [P, GRP, 2, P], F32))
        o = ctx.enter_context(nc.psum_tensor("wd_o", [P, 2, HALF], F32))

        sink_in = sem("wd_sink_in")
        s_ready = sem("wd_s_ready")
        biased = sem("wd_biased")
        top_done = sem("wd_top_done")
        peak_done = sem("wd_peak_done")
        neg_done = sem("wd_neg_done")
        p_ready = sem("wd_p_ready")
        turned = sem("wd_turned")
        pt_ready = sem("wd_pt_ready")
        pv_done = sem("wd_pv")
        den_done = sem("wd_den_done")
        rden_done = sem("wd_rden_done")
        o_read = sem("wd_o_read")

        def first_key(i):
            return P if i == 0 else 0

        with nc.Block() as block:
            @block.sync
            def _(sp):
                sp.dma_start(sink_row[:], sinks.partition_broadcast(P)).then_inc(sink_in, 16)
                sp.dma_start(w_dest[:], w_out.rearrange("(c p) n -> p c n", p=P)).then_inc(w_out_in, 16)

            @block.tensor
            def _(pe):
                def scores(n):
                    i, kv = steps[n]
                    k0 = first_key(i)
                    if n >= 2:
                        pe.wait_ge(biased, n - 1)
                    for g in range(GRP):
                        h = kv * GRP + g
                        lo = DH * (h % 2)
                        last = nc.tensor.matmul(s[:, n % 2, place4(g), k0:2 * P], wq_t[lo:lo + DH, h // 2, i * P:(i + 1) * P],
                                                wk_t[lo:lo + DH, kv, (i - 1) * P + k0:(i + 1) * P], start=True, stop=True)
                    last.then_inc(s_ready, 1)

                def turn(n):
                    i, kv = steps[n]
                    pe.wait_ge(p_ready, n + 1)
                    if n >= 1:
                        pe.wait_ge(pt_ready, n)
                    for g in range(GRP):
                        for kb in range(first_key(i) // P, 2):
                            last = nc.tensor.transpose(tp[:, g, kb, :], p[:, n % 2, g, kb * P:(kb + 1) * P], ident[:])
                    last.then_inc(turned, 1)

                def values(n):
                    i, kv = steps[n]
                    pe.wait_ge(pt_ready, n + 1)
                    if n >= 2:
                        pe.wait_ge(o_read, n - 1)
                    for g in range(GRP):
                        k0 = first_key(i) // P
                        for kb in range(k0, 2):
                            last = nc.tensor.matmul(o[:, n % 2, g * DH:(g + 1) * DH], p_t[:, n % 2, g, kb, :],
                                                    sw_v[:, i - 1 + kb, kv * DH:(kv + 1) * DH],
                                                    start=kb == k0, stop=kb == 1)
                    last.then_inc(pv_done, 1)

                scores(0)
                for n in range(len(steps)):
                    if n + 1 < len(steps):
                        scores(n + 1)
                    turn(n)
                    if n >= 1:
                        values(n - 1)
                values(len(steps) - 1)

            @block.vector
            def _(dve):
                def soften(n):
                    i, kv = steps[n]
                    k0 = first_key(i)
                    b, st = n % 2, n % 4
                    sk = sink[:, kv * GRP:(kv + 1) * GRP]
                    dve.wait_ge(s_ready, n + 1)
                    if n >= 2:
                        dve.wait_ge(turned, n - 1)
                        dve.wait_ge(p_ready, n - 1)
                    nc.vector.tensor_tensor(p[:, b, :, k0:], s[:, b, :, k0:], bias[:, kv * GRP:(kv + 1) * GRP, k0:],
                                            ALU.add).then_inc(biased, 1)
                    dve.wait_ge(biased, n + 1)
                    nc.vector.tensor_reduce(top[:, st, :], p[:, b, :, k0:], AX, ALU.max).then_inc(top_done, 1)
                    dve.wait_ge(top_done, n + 1)
                    nc.vector.tensor_tensor(peak[:, st, :], top[:, st, :], sk, ALU.max).then_inc(peak_done, 1)
                    dve.wait_ge(peak_done, n + 1)
                    nc.vector.tensor_scalar(neg[:, st, :], peak[:, st, :], -1.0, None, ALU.mult).then_inc(neg_done, 1)
                    nc.vector.tensor_tensor(sd[:, st, :], sk, peak[:, st, :], ALU.subtract).then_inc(neg_done, 1)

                def read_t(n):
                    k0 = first_key(steps[n][0]) // P
                    dve.wait_ge(turned, n + 1)
                    if n >= 2:
                        dve.wait_ge(pv_done, n - 1)
                    nc.vector.tensor_copy(p_t[:, n % 2, :, k0:, :], tp[:, :, k0:, :]).then_inc(pt_ready, 1)

                def finish(n):
                    i, kv = steps[n]
                    b, st = n % 2, n % 4
                    dve.wait_ge(p_ready, n + 1)
                    nc.vector.tensor_tensor(den[:, st, :], rs[:, st, :], es[:, st, :], ALU.add).then_inc(den_done, 1)
                    dve.wait_ge(den_done, n + 1)
                    nc.vector.reciprocal(rden[:, st, :], den[:, st, :]).then_inc(rden_done, 1)
                    dve.wait_ge(rden_done, n + 1)
                    dve.wait_ge(pv_done, n + 1)
                    dest = mixed[:, i, D_SB + kv * GRP * DH:D_SB + (kv + 1) * GRP * DH]
                    nc.vector.tensor_tensor(dest.rearrange("p (b a d) -> p a b d", a=2, d=DH),
                                            o[:, b, 0:GRP * DH].rearrange("p (a b d) -> p a b d", a=2, d=DH),
                                            bcast(rden[:, st, :].rearrange("p (a b) -> p a b", a=2).unsqueeze(3),
                                                  [P, 2, GRP // 2, DH]), ALU.mult).then_inc(o_read, 1)

                dve.wait_ge(sink_in, 16)
                nc.vector.tensor_copy(sink[:].rearrange("p (kv a b) -> p kv a b", kv=KV, a=2),
                                      sink_row[:].rearrange("p (kv b a) -> p kv a b", kv=KV, a=2)).then_inc(sink_in, 1)
                dve.wait_ge(sink_in, 17)
                soften(0)
                for n in range(len(steps)):
                    if n + 1 < len(steps):
                        soften(n + 1)
                    read_t(n)
                    if n >= 1:
                        finish(n - 1)
                finish(len(steps) - 1)

            @block.scalar
            def _(act):
                for n, (i, kv) in enumerate(steps):
                    b, st, k0 = n % 2, n % 4, first_key(i)
                    act.wait_ge(neg_done, 2 * (n + 1))
                    if n >= 4:
                        act.wait_ge(den_done, n - 3)
                    for g in range(GRP):
                        nc.scalar.activation(p[:, b, g, k0:], p[:, b, g, k0:], ACT.Exp, bias=neg[:, st, g:g + 1],
                                             accum_out=rs[:, st, g:g + 1])
                    nc.scalar.activation(es[:, st, :], sd[:, st, :], ACT.Exp).then_inc(p_ready, 1)


def mix(nc, sem, x, sb_g, sw_g, w, w_out_in, norm2_g, ident, minus_half, mixed, x1_dram, x2_dram, x2_t):
    with ExitStack() as ctx:
        g1 = ctx.enter_context(nc.sbuf_tensor("mx_g1", [P, D], F32))
        g2 = ctx.enter_context(nc.sbuf_tensor("mx_g2", [P, D], F32))
        xr = ctx.enter_context(nc.sbuf_tensor("mx_xr", [P, 2, D], F32))
        on = ctx.enter_context(nc.sbuf_tensor("mx_on", [P, 2, D], F32))
        m_t = ctx.enter_context(nc.sbuf_tensor("mx_mt", [P, 2, CH, P], F32))
        x1 = ctx.enter_context(nc.sbuf_tensor("mx_x1", [P, 2, D], F32))
        x2 = ctx.enter_context(nc.sbuf_tensor("mx_x2", [P, 2, D], F32))
        hs = ctx.enter_context(nc.sbuf_tensor("mx_hs", [P, 3, 2 * HEADS], F32))
        rs = ctx.enter_context(nc.sbuf_tensor("mx_rs", [P, 3, TILES], F32))
        tp1 = ctx.enter_context(nc.psum_tensor("mx_tp1", [P, CH, P], F32))
        tp2 = ctx.enter_context(nc.psum_tensor("mx_tp2", [P, CH, P], F32))
        y = ctx.enter_context(nc.psum_tensor("mx_y", [P, 2, D], F32))

        g_in = sem("mx_g_in")
        x_in = [sem(f"mx_x_in{s}") for s in range(2)]
        x1_out = [sem(f"mx_x1_out{s}") for s in range(2)]
        x2_out = [sem(f"mx_x2_out{s}") for s in range(2)]
        squared = sem("mx_squared")
        sums = sem("mx_sums")
        scaled = sem("mx_scaled")
        gained = sem("mx_gained")
        turned = sem("mx_turned")
        mt_ready = sem("mx_mt_ready")
        y_ready = sem("mx_y_ready")
        x1_ready = sem("mx_x1_ready")
        squared2 = sem("mx_squared2")
        head_rstd = sem("mx_head_rstd")
        mean2 = sem("mx_mean2")
        rstd2 = sem("mx_rstd2")
        scaled2 = sem("mx_scaled2")
        gained2 = sem("mx_gained2")
        turned2 = sem("mx_turned2")
        x2t_ready = sem("mx_x2t_ready")
        NH = 2 * HEADS

        with nc.Block() as block:
            def store(sp, t):
                sp.wait_ge(x1_ready, t + 1)
                sp.dma_start(x1_dram[t * P:(t + 1) * P, :], x1[:, t % 2, :]).then_inc(x1_out[t % 2], 16)
                sp.wait_ge(gained2, t + 1)
                sp.dma_start(x2_dram[t * P:(t + 1) * P, :], x2[:, t % 2, :]).then_inc(x2_out[t % 2], 16)

            @block.sync
            def _(sp):
                sp.dma_start(g1[:, 0:D_SB], sb_g.partition_broadcast(P)).then_inc(g_in, 16)
                sp.dma_start(g1[:, D_SB:D], sw_g.partition_broadcast(P)).then_inc(g_in, 16)
                sp.dma_start(g2[:], norm2_g.partition_broadcast(P)).then_inc(g_in, 16)
                for t in range(TILES):
                    if t >= 2:
                        sp.wait_ge(x1_ready, t - 1)
                    sp.dma_start(xr[:, t % 2, :], x[t * P:(t + 1) * P, :]).then_inc(x_in[t % 2], 16)
                    if t >= 1:
                        store(sp, t - 1)
                store(sp, TILES - 1)
                for s in range(2):
                    sp.wait_ge(x1_out[s], 16 * (TILES // 2))
                    sp.wait_ge(x2_out[s], 16 * (TILES // 2))

            @block.scalar
            def _(act):
                for t in range(-1, TILES + 1):
                    if t + 1 < TILES:
                        n = t + 1
                        if n >= 2:
                            act.wait_ge(turned, n - 1)
                        nc.scalar.activation(on[:, n % 2, :], mixed[:, n, :], ACT.Square).then_inc(squared, 1)
                        act.wait_ge(turned, n + 1)
                        if n >= 2:
                            act.wait_ge(y_ready, n - 1)
                        nc.scalar.activation(m_t[:, n % 2, :, :], tp1[:], ACT.Copy).then_inc(mt_ready, 1)
                    if 0 <= t < TILES:
                        act.wait_ge(x1_ready, t + 1)
                        if t >= 2:
                            act.wait_ge(turned2, t - 1)
                            act.wait_ge(x2_out[t % 2], 16 * (t // 2))
                        nc.scalar.activation(x2[:, t % 2, :], x1[:, t % 2, :], ACT.Square,
                                             accum_out=rs[:, 0, t:t + 1]).then_inc(squared2, 1)
                    if 0 <= t - 1:
                        act.wait_ge(turned2, t)
                        nc.scalar.activation(x2_t[:, :, (t - 1) * P:t * P], tp2[:], ACT.Copy).then_inc(x2t_ready, 1)

            @block.vector
            def _(dve):
                for t in range(-1, TILES):
                    if t + 1 < TILES:
                        n = t + 1
                        o3 = on[:, n % 2, :].rearrange("p (h d) -> p h d", d=DH)
                        dve.wait_ge(squared, n + 1)
                        if n >= 1:
                            dve.wait_ge(scaled, n)
                        nc.vector.tensor_reduce(hs[:, 0, :], o3, AX, ALU.add).then_inc(sums, 1)
                        dve.wait_ge(sums, 2 * n + 1)
                        nc.vector.tensor_scalar(hs[:, 1, :], hs[:, 0, :], 1.0 / DH, EPS, ALU.mult, ALU.add).then_inc(sums, 1)
                        dve.wait_ge(head_rstd, n + 1)
                        nc.vector.tensor_tensor(o3, mixed[:, n, :].rearrange("p (h d) -> p h d", d=DH),
                                                bcast(hs[:, 2, :].unsqueeze(2), [P, NH, DH]), ALU.mult).then_inc(scaled, 1)
                    if t >= 0:
                        dve.wait_ge(y_ready, t + 1)
                        dve.wait_ge(x_in[t % 2], 16 * (t // 2 + 1))
                        if t >= 2:
                            dve.wait_ge(x1_out[t % 2], 16 * (t // 2))
                            dve.wait_ge(scaled2, t - 1)
                        nc.vector.tensor_tensor(x1[:, t % 2, :], y[:, t % 2, :], xr[:, t % 2, :], ALU.add).then_inc(x1_ready, 1)
                        dve.wait_ge(squared2, t + 1)
                        nc.vector.tensor_scalar(rs[:, 1, t:t + 1], rs[:, 0, t:t + 1], 1.0 / D, EPS, ALU.mult,
                                                ALU.add).then_inc(mean2, 1)
                        dve.wait_ge(rstd2, t + 1)
                        nc.vector.tensor_scalar(x2[:, t % 2, :], x1[:, t % 2, :], rs[:, 2, t:t + 1], None,
                                                ALU.mult).then_inc(scaled2, 1)

            @block.gpsimd
            def _(pool):
                pool.wait_ge(g_in, 48)
                for t in range(-1, TILES):
                    if t + 1 < TILES:
                        n = t + 1
                        pool.wait_ge(sums, 2 * n + 2)
                        nc.gpsimd.tensor_tensor(hs[:, 2, :], hs[:, 1, :], minus_half[:], ALU.pow).then_inc(head_rstd, 1)
                        pool.wait_ge(scaled, n + 1)
                        nc.gpsimd.tensor_tensor(on[:, n % 2, :], on[:, n % 2, :], g1[:], ALU.mult).then_inc(gained, 1)
                    if t >= 0:
                        pool.wait_ge(mean2, t + 1)
                        nc.gpsimd.tensor_tensor(rs[:, 2, t:t + 1], rs[:, 1, t:t + 1], minus_half[:, 0:1],
                                                ALU.pow).then_inc(rstd2, 1)
                        pool.wait_ge(scaled2, t + 1)
                        nc.gpsimd.tensor_tensor(x2[:, t % 2, :], x2[:, t % 2, :], g2[:], ALU.mult).then_inc(gained2, 1)

            @block.tensor
            def _(pe):
                for t in range(-1, TILES + 1):
                    if 0 <= t < TILES:
                        pe.wait_ge(mt_ready, t + 1)
                        if t == 0:
                            pe.wait_ge(w_out_in, 16)
                        if t >= 2:
                            pe.wait_ge(x1_ready, t - 1)
                        for c in range(CH):
                            for hf in range(2):
                                last = nc.tensor.matmul(y[:, t % 2, hf * HALF:(hf + 1) * HALF], m_t[:, t % 2, c, :],
                                                        w[:, c, hf * HALF:(hf + 1) * HALF],
                                                        start=c == 0, stop=c == CH - 1)
                        last.then_inc(y_ready, 1)
                    if t + 1 < TILES:
                        n = t + 1
                        pe.wait_ge(gained, n + 1)
                        if n >= 1:
                            pe.wait_ge(mt_ready, n)
                        for c in range(CH):
                            last = nc.tensor.transpose(tp1[:, c, :], on[:, n % 2, c * P:(c + 1) * P], ident[:])
                        last.then_inc(turned, 1)
                    if t - 1 >= 0:
                        pe.wait_ge(gained2, t)
                        if t >= 2:
                            pe.wait_ge(x2t_ready, t - 1)
                        for c in range(CH):
                            last = nc.tensor.transpose(tp2[:, c, :], x2[:, (t - 1) % 2, c * P:(c + 1) * P], ident[:])
                        last.then_inc(turned2, 1)


class KeyScores:

    def __init__(self, nc, sem, tag, ctx, passes, w, ring, keys_t, w_q, x2_t, score_dram, sc):
        self.sc, self.sc_ready = sc, sem(f"{tag}_sc_ready")
        self.nc, self.w, self.ring, self.keys_t, self.x2_t = nc, w, ring, keys_t, x2_t
        self.q_t = ctx.enter_context(nc.sbuf_tensor(f"{tag}_qt", [P, 2, HALF], F32))
        self.out = ctx.enter_context(nc.sbuf_tensor(f"{tag}_out", [P, 4, 4, NK], F32))
        self.q = ctx.enter_context(nc.psum_tensor(f"{tag}_q", [P, 2, HALF], F32))
        self.s = ctx.enter_context(nc.psum_tensor(f"{tag}_s", [P, 2, 4, NK], F32))
        self.w_loaded = [sem(f"{tag}_w_in{k}") for k in range(ring)]
        self.q_ready = sem(f"{tag}_q_ready")
        self.qt_ready = sem(f"{tag}_qt_ready")
        self.s_ready = sem(f"{tag}_s_ready")
        self.s_read = sem(f"{tag}_s_read")
        self.stored = [sem(f"{tag}_stored{k}") for k in range(4)]
        self.units = [(b, first, tiles) for spans in passes for b in range(SIDES) for first, tiles in spans]
        self.columns = SIDES * P // COLS
        self.groups = len(passes) * self.columns
        self.group = [k * self.columns + b * P // COLS for k, spans in enumerate(passes) for b in range(SIDES) for _ in spans]
        self.w_view = w_q.rearrange("(c p) n -> p c n", p=P)
        self.score_view = score_dram.rearrange("(t p) (b n) -> p t b n", p=P, n=NK)

    def load(self, sp, g):
        at = g % self.columns * COLS
        sp.dma_start(self.w[:, g % self.ring, :, :], self.w_view[:, :, at:at + COLS]).then_inc(
            self.w_loaded[g % self.ring], 16)

    def store(self, sp, n):
        b, first, tiles = self.units[n]
        sp.wait_ge(self.s_read, n + 1)
        sp.dma_start(self.score_view[:, first:first + tiles, b, :], self.out[:, n % 4, 0:tiles, :]).then_inc(
            self.stored[n % 4], 16)
        g = self.group[n] + self.ring
        if g < self.groups and self.group[n] != self.group[n + 1]:
            sp.wait_ge(self.s_ready, n + 1)
            self.load(sp, g)

    def all_stored(self, sp):
        for k in range(4):
            sp.wait_ge(self.stored[k], 16 * (len(self.units) // 4))

    def copy_queries(self, act, n):
        width = self.units[n][2] * P
        act.wait_ge(self.q_ready, n + 1)
        if n >= 2:
            act.wait_ge(self.s_ready, n - 1)
        self.nc.scalar.activation(self.q_t[:, n % 2, 0:width], self.q[:, n % 2, 0:width], ACT.Copy).then_inc(self.qt_ready, 1)

    def read_scores(self, act, n):
        tiles = self.units[n][2]
        act.wait_ge(self.s_ready, n + 1)
        if n < SIDES:
            self.nc.scalar.activation(self.sc[:, self.units[n][0], :], self.s[:, n % 2, 0, :], ACT.Copy).then_inc(self.sc_ready, 1)
        if n >= 4:
            act.wait_ge(self.stored[n % 4], 16 * (n // 4))
        self.nc.scalar.activation(self.out[:, n % 4, 0:tiles, :], self.s[:, n % 2, 0:tiles, :], ACT.Copy).then_inc(self.s_read, 1)

    def evacuate(self, act, n):
        if n == 0:
            self.copy_queries(act, 0)
        if n + 1 < len(self.units):
            self.copy_queries(act, n + 1)
        self.read_scores(act, n)

    def query(self, pe, n):
        b, first, tiles = self.units[n]
        g = self.group[n]
        if n == 0 or self.group[n - 1] != g:
            pe.wait_ge(self.w_loaded[g % self.ring], 16 * (g // self.ring + 1))
        if n >= 2:
            pe.wait_ge(self.qt_ready, n - 1)
        for c in range(CH):
            last = self.nc.tensor.matmul(self.q[:, n % 2, 0:tiles * P], self.w[:, g % self.ring, c, (b % 2) * P:(b % 2 + 1) * P],
                                         self.x2_t[:, c, first * P:(first + tiles) * P], start=c == 0, stop=c == CH - 1)
        last.then_inc(self.q_ready, 1)

    def score(self, pe, n):
        b, first, tiles = self.units[n]
        pe.wait_ge(self.qt_ready, n + 1)
        if n >= 2:
            pe.wait_ge(self.s_read, n - 1)
        for j in range(tiles):
            last = self.nc.tensor.matmul(self.s[:, n % 2, j, :], self.q_t[:, n % 2, j * P:(j + 1) * P], self.keys_t[:, b, :],
                                         start=True, stop=True)
        last.then_inc(self.s_ready, 1)

    def multiply(self, pe):
        self.query(pe, 0)
        for n in range(len(self.units)):
            if n + 1 < len(self.units):
                self.query(pe, n + 1)
            self.score(pe, n)


def experts(nc, sem, ident, spare, keys_t, keys1, keys2, w_q, x2_t, score_dram, x1_dram, x2_dram, peer_u, peer_v, final_g, out):
    RG = 8
    GROUPS = PICKS // RG
    score_t = score_dram.rearrange("(t p) n -> t p n", p=P)
    x1_v = x1_dram.rearrange("(t p) n -> t p n", p=P)
    x2_v = x2_dram.rearrange("(t p) n -> t p n", p=P)
    out_v = out.rearrange("(t p) n -> t p n", p=P)
    with ExitStack() as ctx:
        def sb(name, shape, dt=F32):
            return ctx.enter_context(nc.sbuf_tensor(name, shape, dt))

        u = sb("ex_u", [P, RG, D])
        v = sb("ex_v", [P, RG, D])
        diag = sb("ex_diag", [P, RG, P])
        sc = sb("ex_sc", [P, SIDES, NK])
        left = sb("ex_left", [P, SIDES, NK])
        cand = sb("ex_cand", [P, PH, TOPK, TOPK])
        cleft = sb("ex_cleft", [P, PH, TOPK, TOPK])
        half_v = sb("ex_half_v", [P, SIDES, TOPK])
        half_i = sb("ex_half_i", [P, SIDES, TOPK], U32)
        half_f = sb("ex_half_f", [P, SIDES, TOPK])
        best = sb("ex_best", [P, PH, TOPK])
        pos = sb("ex_pos", [P, PH, TOPK], U32)
        part_i = sb("ex_part_i", [P, 2, PICKS], U32)
        part_f = sb("ex_part_f", [P, 2, PICKS])
        hit = sb("ex_hit", [P, PICKS, TOPK])
        row = sb("ex_row", [P, 2, PICKS])
        index_f = sb("ex_index_f", [P, PICKS])
        index = sb("ex_index", [P, PICKS], I32)
        index_ut = sb("ex_index_ut", [P, PICKS], I32)
        index_vt = sb("ex_index_vt", [P, PICKS], I32)
        gate_e = sb("ex_gate_e", [P, PICKS])
        gates = sb("ex_gates", [P, 2, PICKS])
        gsum = sb("ex_gsum", [P, 2, PH])
        ramp_i = sb("ex_ramp_i", [P, TOPK], I32)
        ramp = sb("ex_ramp", [P, TOPK])
        index_u = sb("ex_index_u", [P, 2, RG], I32)
        index_v = sb("ex_index_v", [P, 2, RG], I32)
        zero_i = sb("ex_zero_i", [P, PICKS], I32)
        x2 = sb("ex_x2", [P, D])
        prod = [sb("ex_prod", [P, D]), spare]
        dots = sb("ex_dots", [P, RG])
        hid = sb("ex_hid", [P, PICKS])
        ga = sb("ex_ga", [P, 4, PICKS])
        wt = sb("ex_wt", [P, PICKS])
        x1 = sb("ex_x1", [P, D])
        y = sb("ex_y", [P, D])
        gf = sb("ex_gf", [P, D])
        fs = sb("ex_fs", [P, 8])
        acc = ctx.enter_context(nc.psum_tensor("ex_acc", [P, D], F32))
        ysq = ctx.enter_context(nc.psum_tensor("ex_ysq", [P, D], F32))
        key_ring = RG * D // (CH * COLS)
        keys = u[:].rearrange("p r (b n) -> p (r b) n", n=P)[:, 0:SIDES, :]
        turn = acc[:].rearrange("p (k j n) -> p k j n", k=2, n=P)
        keys_in = sem("ex_keys_in")
        keys_turned = sem("ex_keys_turned")
        keys_ready = sem("ex_keys_ready")
        ks = KeyScores(nc, sem, "kl", ctx, [[(0, EARLY)], [(EARLY, 4), (EARLY + 4, TILES - EARLY - 4)]],
                         v[:].rearrange("p r (h n) -> p (r h) n", n=COLS).rearrange("p (g c) n -> p g c n", c=CH),
                         key_ring, keys_t, w_q, x2_t, score_dram, sc)

        setup = sem("ex_setup")
        gf_in = sem("ex_gf_in")
        sc_in = sem("ex_sc_in")
        x1_in = sem("ex_x1_in")
        x2_in = sem("ex_x2_in")
        stored = sem("ex_stored")
        u_full = [sem(f"ex_u_full{k}") for k in range(RG)]
        v_full = [sem(f"ex_v_full{k}") for k in range(RG)]
        u_free = sem("ex_u_free")
        v_free = sem("ex_v_free")
        iu_ready = sem("ex_iu_ready")
        iv_ready = sem("ex_iv_ready")
        picked = sem("ex_picked")
        index_moved = sem("ex_index_moved")
        chain = sem("ex_chain")
        dot_done = sem("ex_dot")
        hid_ready = sem("ex_hid_ready")
        act_done = sem("ex_act")
        exp_asked = sem("ex_exp_asked")
        gelu_asked = sem("ex_gelu_asked")
        gelu_done = sem("ex_gelu_done")
        wt_ready = sem("ex_wt_ready")
        diag_ready = sem("ex_diag_ready")
        extra_used = sem("ex_extra_used")
        y_ready = sem("ex_y_ready")
        y_squared = sem("ex_y_squared")
        root_asked = sem("ex_root_asked")
        root_done = sem("ex_root_done")
        y_free = sem("ex_y_free")
        y_done = sem("ex_y_done")
        tick = sem("ex_tick")

        def hold(engine, signal, value):
            engine.wait_ge(signal, value)
            engine.sem_inc(tick, 1)

        with nc.Block() as block:
            @block.sync
            def _(sp):
                sp.sem_inc(y_free, 1)
                side_view = keys.rearrange("n (h s) d -> n h s d", s=2)
                sp.dma_start(side_view[:, :, 0, :], keys1.rearrange("h n d -> n h d")).then_inc(keys_in, 16)
                sp.dma_start(side_view[:, :, 1, :], keys2.rearrange("h n d -> n h d")).then_inc(keys_in, 16)
                for g in range(key_ring):
                    ks.load(sp, g)
                sp.dma_start(gf[:], final_g.partition_broadcast(P)).then_inc(gf_in, 16)
                sp.dma_start(x2[:], x2_v[0]).then_inc(x2_in, 16)
                sp.dma_start(x1[:], x1_v[0]).then_inc(x1_in, 16)

                def load_scores(t):
                    sp.wait_ge(picked, t)
                    sp.dma_start(sc[:].rearrange("p b n -> p (b n)"), score_t[bass.ds(t, 1)].squeeze(0)).then_inc(sc_in, 16)

                def load_x2(t):
                    sp.wait_ge(hid_ready, t)
                    sp.dma_start(x2[:], x2_v[bass.ds(t, 1)].squeeze(0)).then_inc(x2_in, 16)

                def turn_over(t):
                    sp.wait_ge(y_done, t)
                    sp.dma_start(out_v[bass.ds(t - 1, 1)].squeeze(0), y[:]).then_inc(stored, 16)
                    sp.dma_start(x1[:], x1_v[bass.ds(t, 1)].squeeze(0)).then_inc(x1_in, 16)
                    sp.wait_ge(stored, 16 * t)
                    sp.sem_inc(y_free, 1)

                for n in range(len(ks.units)):
                    ks.store(sp, n)
                    if n == SIDES + 8:
                        load_scores(1)
                ks.all_stored(sp)
                load_scores(2)
                load_x2(1)
                with sp.Fori(1, TILES - 2) as t:
                    load_scores(t + 2)
                    load_x2(t + 1)
                    turn_over(t)
                load_x2(TILES - 1)
                turn_over(TILES - 2)
                turn_over(TILES - 1)
                sp.wait_ge(y_done, TILES)
                sp.dma_start(out_v[TILES - 1], y[:]).then_inc(stored, 16)
                sp.wait_ge(stored, 16 * TILES)

            @block.gpsimd
            def _(pool):
                nc.gpsimd.iota(ramp_i[:], pattern=[[1, TOPK]], base=0, channel_multiplier=0).then_inc(setup, 1)
                nc.gpsimd.memset(zero_i[:], 0).then_inc(setup, 1)
                pool.sem_inc(u_free, RG)
                pool.wait_ge(setup, 2)

                def gathers(t, j, half, table, ring, tile_index, stage, full, free, ready, slots=RG):
                    at = t * PICKS + j * slots + RG - slots
                    pool.wait_ge(free, at + 1)
                    nc.gpsimd.tensor_tensor(stage[:, half, :], tile_index[:, bass.ds(j * RG, RG)],
                                            zero_i[:, 0:RG], ALU.add).then_inc(ready, 1)
                    hold(pool, ready, t * GROUPS + j + 1)
                    for k in range(RG):
                        if k >= slots:
                            hold(pool, extra_used, j + 1)
                        elif k >= 1:
                            hold(pool, free, at + k + 1)
                        nc.gpsimd.indirect_dma_start(
                            out=ring[:, k, :], out_offset=None, in_=table,
                            in_offset=bass.IndirectOffsetOnAxis(ap=stage[:, half, k:k + 1], axis=0)).then_inc(full[k], 16)

                def copy_index(dest, source, value):
                    nc.gpsimd.tensor_tensor(dest[:], source[:], zero_i[:], ALU.add).then_inc(index_moved, 1)
                    hold(pool, index_moved, value)

                pool.wait_ge(picked, 1)
                copy_index(index_ut, index, 1)
                with pool.Fori(0, GROUPS // 2) as pair:
                    for half in range(2):
                        gathers(0, 2 * pair + half, half, peer_u, u, index_ut, index_u, u_full, u_free, iu_ready)
                with pool.Fori(0, TILES - 1) as t:
                    copy_index(index_vt, index_ut, 2 * t + 2)
                    hold(pool, picked, t + 2)
                    copy_index(index_ut, index, 2 * t + 3)
                    with pool.Fori(0, GROUPS // 2) as pair:
                        for half in range(2):
                            gathers(t, 2 * pair + half, half, peer_v, v, index_vt, index_v, v_full, v_free, iv_ready)
                            gathers(t + 1, 2 * pair + half, half, peer_u, u, index_ut, index_u, u_full, u_free, iu_ready)
                copy_index(index_vt, index_ut, 2 * TILES)
                with pool.Fori(0, GROUPS // 2) as pair:
                    for half in range(2):
                        gathers(TILES - 1, 2 * pair + half, half, peer_v, v, index_vt, index_v, v_full, v_free, iv_ready,
                                RG - 1)

            @block.vector
            def _(dve):
                steps = [0]

                def link(ins, base):
                    steps[0] += 1
                    ins.then_inc(chain, 1)
                    hold(dve, chain, base + steps[0])

                def pick_half_first(t, base, sides=range(SIDES)):
                    if not isinstance(t, int):
                        hold(dve, sc_in, 16 * t)
                    elif t >= 1:
                        dve.wait_ge(sc_in, 16 * t)
                    else:
                        dve.wait_ge(ks.sc_ready, sides[-1] + 1)
                    for b in sides:
                        nc.vector.max(half_v[:, b, 0:8], sc[:, b, :])
                    link(nc.vector.drain(), base)
                    for b in sides:
                        nc.vector.max_index(half_i[:, b, 0:8], half_v[:, b, 0:8], sc[:, b, :])
                        last = nc.vector.match_replace(left[:, b, :], half_v[:, b, 0:8], sc[:, b, :], LOWEST)
                    link(last, base)

                def pick_half_second(base, sides=range(SIDES)):
                    for b in sides:
                        last = nc.vector.max(half_v[:, b, 8:16], left[:, b, :])
                    link(last, base)
                    for b in sides:
                        last = nc.vector.max_index(half_i[:, b, 8:16], half_v[:, b, 8:16], left[:, b, :])
                    link(last, base)

                def pick_table(base):
                    link(nc.vector.tensor_copy(half_f[:], half_i[:]), base)
                    for h in range(PH):
                        last = nc.vector.tensor_tensor(
                            cand[:, h, :, :], bcast(half_v[:, 2 * h, :].unsqueeze(2), [P, TOPK, TOPK]),
                            bcast(half_v[:, 2 * h + 1, :].unsqueeze(1), [P, TOPK, TOPK]), ALU.add)
                    link(last, base)

                flat = [cand[:, h, :, :].rearrange("p a b -> p (a b)") for h in range(PH)]
                g3 = gate_e[:].rearrange("p (h k) -> p h k", h=PH)
                flat2 = [cleft[:, h, :, :].rearrange("p a b -> p (a b)") for h in range(PH)]

                def pick_first(base):
                    for h in range(PH):
                        last = nc.vector.max(best[:, h, 0:8], flat[h])
                    link(last, base)
                    for h in range(PH):
                        nc.vector.max_index(pos[:, h, 0:8], best[:, h, 0:8], flat[h])
                        last = nc.vector.match_replace(flat2[h], best[:, h, 0:8], flat[h], LOWEST)
                    link(last, base)

                def pick_second(base):
                    for h in range(PH):
                        last = nc.vector.max(best[:, h, 8:16], flat2[h])
                    link(last, base)
                    for h in range(PH):
                        last = nc.vector.max_index(pos[:, h, 8:16], best[:, h, 8:16], flat2[h])
                    link(last, base)
                    pos_flat = pos[:].rearrange("p h k -> p (h k)")
                    nc.vector.tensor_scalar(part_i[:, 0, :], pos_flat, 4, None, ALU.logical_shift_right)
                    link(nc.vector.tensor_scalar(part_i[:, 1, :], pos_flat, 15, None, ALU.bitwise_and), base)
                    link(nc.vector.tensor_copy(part_f[:], part_i[:]), base)

                    nc.vector.tensor_tensor(g3, best[:], bcast(best[:, :, 0:1], [P, PH, TOPK]),
                                            ALU.subtract).then_inc(exp_asked, 1)

                def pick_rows(side, base):
                    halves = half_f[:].rearrange("p (h s) k -> p s h k", s=2)
                    link(nc.vector.tensor_tensor(hit[:], bcast(part_f[:, side, :].unsqueeze(2), [P, PICKS, TOPK]),
                                                 bcast(ramp[:].unsqueeze(1), [P, PICKS, TOPK]), ALU.is_equal), base)
                    for h in range(PH):
                        hh = hit[:, h * TOPK:(h + 1) * TOPK, :]
                        last = nc.vector.tensor_tensor(hh, hh, bcast(halves[:, side, h, :].unsqueeze(1),
                                                                     [P, TOPK, TOPK]), ALU.mult)
                    link(last, base)
                    link(nc.vector.tensor_reduce(row[:, side, :], hit[:], AX, ALU.add), base)

                def pick_gates(t, base):
                    link(nc.vector.scalar_tensor_tensor(out=index_f[:], in0=row[:, 0, :], scalar=float(NK),
                                                        in1=row[:, 1, :], op0=ALU.mult, op1=ALU.add), base)
                    if not isinstance(t, int):
                        hold(dve, index_moved, 2 * t - 1)
                    elif t >= 1:
                        dve.wait_ge(index_moved, 2 * t - 1)
                    link(nc.vector.tensor_copy(index[:], index_f[:]), base)
                    hold(dve, act_done, t + 1)
                    link(nc.vector.tensor_reduce(gsum[:, 0, :], g3, AX, ALU.add), base)
                    link(nc.vector.reciprocal(gsum[:, 1, :], gsum[:, 0, :]), base)
                    link(nc.vector.tensor_tensor(
                        gates[:, bass.ds(t % 2, 1), :].rearrange("p one (h k) -> p (one h) k", h=PH), g3,
                        bcast(gsum[:, 1, :].unsqueeze(2), [P, PH, TOPK]), ALU.mult), base)
                    dve.sem_inc(picked, 1)

                def dot_group(t, j):
                    at = t * PICKS + j * RG
                    for k in range(RG):
                        dve.wait_ge(u_full[k], 16 * (t * GROUPS + j + 1))
                        if k >= 2:
                            dve.wait_ge(u_free, at + RG + k - 1)
                        nc.vector.tensor_tensor_reduce(out=prod[k % 2][:], in0=u[:, k, :], in1=x2[:], scale=1.0, scalar=0.0,
                                                       op0=ALU.mult, op1=ALU.add,
                                                       accum_out=dots[:, k:k + 1]).then_inc(u_free, 1)
                    dve.wait_ge(u_free, at + 2 * RG)
                    nc.vector.tensor_copy(hid[:, bass.ds(j * RG, RG)], dots[:]).then_inc(dot_done, 1)
                    hold(dve, dot_done, t * GROUPS + j + 1)

                def weigh(t, base, has_prev):
                    nc.vector.tensor_tensor(ga[:, 0, :], hid[:], hid[:], ALU.mult).then_inc(hid_ready, 1)
                    dve.wait_ge(hid_ready, t + 1)
                    link(nc.vector.tensor_scalar(ga[:, 1, :], ga[:, 0, :], GELU_A, 1.0, ALU.mult, ALU.add), base)
                    link(nc.vector.tensor_tensor(ga[:, 0, :], ga[:, 1, :], hid[:], ALU.mult), base)
                    nc.vector.tensor_scalar(ga[:, 2, :], ga[:, 0, :], -50.0, None, ALU.max).then_inc(gelu_asked, 1)
                    dve.wait_ge(gelu_done, t + 1)
                    link(nc.vector.tensor_scalar(ga[:, 1, :], ga[:, 3, :], 1.0, None, ALU.add), base)
                    link(nc.vector.reciprocal(ga[:, 0, :], ga[:, 1, :]), base)
                    link(nc.vector.tensor_tensor(ga[:, 1, :], ga[:, 0, :], hid[:], ALU.mult), base)
                    if has_prev:
                        hold(dve, diag_ready, t * PICKS)
                    link(nc.vector.tensor_tensor(wt[:], ga[:, 1, :], gates[:, bass.ds(t % 2, 1), :].squeeze(1), ALU.mult), base)
                    dve.sem_inc(wt_ready, 1)

                def extra():
                    dve.wait_ge(x1_in, 16 * TILES)
                    held = x1
                    for j in range(GROUPS):
                        dve.wait_ge(v_full[RG - 1], 16 * ((TILES - 1) * GROUPS + j + 1))
                        nc.vector.scalar_tensor_tensor(out=prod[j % 2][:], in0=v[:, RG - 1, :], scalar=wt[:, (j + 1) * RG - 1:(j + 1) * RG],
                                                       in1=held[:], op0=ALU.mult, op1=ALU.add).then_inc(extra_used, 1)
                        dve.wait_ge(extra_used, j + 2)
                        held = prod[j % 2]
                    return held

                def finish(t, base, rows=x1, products=None):
                    dve.wait_ge(v_free, (t + 1) * PICKS + RG if products is None else products)
                    dve.wait_ge(x1_in, 16 * (t + 1))
                    dve.wait_ge(y_free, t + 1)
                    nc.vector.tensor_tensor(y[:], acc[:], rows[:], ALU.add).then_inc(y_ready, 1)
                    dve.wait_ge(y_squared, t + 1)
                    nc.vector.tensor_scalar(fs[:, 1:2], fs[:, 0:1], 1.0 / D, EPS, ALU.mult, ALU.add).then_inc(root_asked, 1)
                    dve.wait_ge(root_done, 2 * (t + 1))
                    link(nc.vector.tensor_tensor(fs[:, 4:5], fs[:, 3:4], fs[:, 1:2], ALU.mult), base)
                    link(nc.vector.tensor_tensor(fs[:, 5:6], fs[:, 4:5], fs[:, 3:4], ALU.mult), base)
                    link(nc.vector.tensor_scalar(fs[:, 6:7], fs[:, 5:6], -0.5, 1.5, ALU.mult, ALU.add), base)
                    link(nc.vector.tensor_tensor(fs[:, 7:8], fs[:, 6:7], fs[:, 3:4], ALU.mult), base)
                    link(nc.vector.tensor_scalar(y[:], y[:], fs[:, 7:8], None, ALU.mult), base)
                    nc.vector.tensor_tensor(y[:], y[:], gf[:], ALU.mult).then_inc(y_done, 1)

                dve.sem_inc(extra_used, 1)
                for k in range(SIDES // 4):
                    dve.wait_ge(keys_turned, k + 1)
                    nc.vector.tensor_copy(keys_t[:, 4 * k:4 * k + 4, :], turn[:, k % 2, :, :]).then_inc(keys_ready, 1)
                dve.wait_ge(setup, 2)
                nc.vector.tensor_copy(ramp[:], ramp_i[:]).then_inc(setup, 1)
                dve.wait_ge(setup, 3)
                dve.wait_ge(gf_in, 16)

                def dot_pair(t, pair):
                    for half in range(2):
                        dot_group(t, 2 * pair + half)

                def tile(t, base, last_tile, has_prev):
                    hold(dve, x2_in, 16 * (t + 1))
                    if last_tile:
                        with dve.Fori(0, GROUPS // 2) as pair:
                            dot_pair(t, pair)
                    else:
                        dot_pair(t, 0)
                        pick_half_first(t + 1, base)
                        dot_pair(t, 1)
                        pick_half_second(base)
                        pick_table(base)
                        dot_pair(t, 2)
                        pick_first(base)
                        dot_pair(t, 3)
                        pick_second(base)
                        dot_pair(t, 4)
                        pick_rows(0, base)
                        dot_pair(t, 5)
                        pick_rows(1, base)
                        dot_pair(t, 6)
                        pick_gates(t + 1, base)
                        dot_pair(t, 7)
                    weigh(t, base, has_prev)
                    if has_prev:
                        finish(t - 1, base)

                for b in range(0, SIDES, 4):
                    pick_half_first(0, 0, range(b, b + 4))
                    pick_half_second(0, range(b, b + 4))
                pick_table(0)
                pick_first(0)
                pick_second(0)
                pick_rows(0, 0)
                pick_rows(1, 0)
                pick_gates(0, 0)
                tile(0, 0, False, False)
                after_first = steps[0]
                steps[0] = 0
                probe = len_of_tile()
                with dve.Fori(1, TILES - 1) as t:
                    tile(t, (t - 1) * probe + after_first, False, True)
                assert steps[0] == probe
                steps[0] = 0
                base = after_first + (TILES - 2) * probe
                tile(TILES - 1, base, True, True)
                finish(TILES - 1, base, extra(), (TILES - 1) * PICKS + RG + GROUPS * (RG - 1))

            @block.scalar
            def _(act):
                def gate_exp(t):
                    act.wait_ge(exp_asked, t + 1)
                    nc.scalar.activation(gate_e[:], gate_e[:], ACT.Exp).then_inc(act_done, 1)

                def gelu_exp(t):
                    act.wait_ge(gelu_asked, t + 1)
                    nc.scalar.activation(ga[:, 3, :], ga[:, 2, :], ACT.Exp, scale=-2.0 * GELU_C).then_inc(gelu_done, 1)

                def square(t):
                    act.wait_ge(y_ready, t + 1)
                    nc.scalar.activation(ysq[:], y[:], ACT.Square, accum_out=fs[:, 0:1]).then_inc(y_squared, 1)
                    act.wait_ge(root_asked, t + 1)
                    nc.scalar.activation(fs[:, 2:3], fs[:, 1:2], ACT.Ln).then_inc(root_done, 1)
                    act.wait_ge(root_done, 2 * t + 1)
                    nc.scalar.activation(fs[:, 3:4], fs[:, 2:3], ACT.Exp, scale=-0.5).then_inc(root_done, 1)

                def diagonals(t, first, last, slots=RG):
                    with act.Fori(first, last) as j:
                        at = t * PICKS + j * slots + RG - slots
                        for k in range(slots):
                            act.wait_ge(v_free, at + k + 1)
                            nc.scalar.activation(diag[:, k, :], ident[:], ACT.Copy,
                                                 scale=wt[:, bass.ds(j * RG + k, 1)]).then_inc(diag_ready, 1)

                def tile(t, last_pick, has_prev, slots=RG):
                    gelu_exp(t)
                    if has_prev:
                        square(t - 1)
                    act.wait_ge(wt_ready, t + 1)
                    if last_pick:
                        diagonals(t, 0, GROUPS, slots)
                    else:
                        diagonals(t, 0, ASKED)
                        gate_exp(t + 2)
                        diagonals(t, ASKED, GROUPS)

                ASKED = GROUPS // 2 + 2
                for n in range(len(ks.units)):
                    ks.evacuate(act, n)
                    if n == SIDES + 2:
                        gate_exp(0)
                gate_exp(1)
                tile(0, False, False)
                with act.Fori(1, TILES - 2) as t:
                    tile(t, False, True)
                tile(TILES - 2, True, True)
                tile(TILES - 1, True, True, RG - 1)
                square(TILES - 1)

            @block.tensor
            def _(pe):
                def group(t, j, first, last, slots):
                    at = t * PICKS + j * slots
                    for k in range(slots):
                        pe.wait_ge(v_full[k], 16 * (t * GROUPS + j + 1))
                        pe.wait_ge(diag_ready, at + k + 1)
                        for hf in range(2):
                            ins = nc.tensor.matmul(acc[:, hf * HALF:(hf + 1) * HALF], diag[:, k, :],
                                                   v[:, k, hf * HALF:(hf + 1) * HALF],
                                                   start=first and k == 0, stop=last and k == slots - 1)
                        ins.then_inc(v_free, 1)

                def tile(t, slots=RG):
                    group(t, 0, True, False, slots)
                    with pe.Fori(1, GROUPS - 1) as j:
                        group(t, j, False, False, slots)
                    group(t, GROUPS - 1, False, True, slots)

                pe.wait_ge(keys_in, 32)
                for k in range(SIDES // 4):
                    if k >= 2:
                        pe.wait_ge(keys_ready, k - 1)
                    for j in range(4):
                        last = nc.tensor.transpose(turn[:, k % 2, j, :], keys[:, 4 * k + j, :], ident[:])
                    last.then_inc(keys_turned, 1)
                pe.wait_ge(keys_ready, SIDES // 4)
                ks.multiply(pe)
                pe.wait_ge(ks.s_ready, len(ks.units))
                pe.sem_inc(v_free, RG)
                tile(0)
                with pe.Fori(1, TILES - 1) as t:
                    pe.wait_ge(y_ready, t)
                    tile(t)
                pe.wait_ge(y_ready, TILES - 1)
                tile(TILES - 1, RG - 1)


def len_of_tile():
    return 6 + 5 + (10 + 2 + 2 * 3 + 2 + 3)


def build(nc, x, norm1_g, w_in, sb_out_g, swa_out_g, swa_sinks, w_out, norm2_g, peer_w_q, peer_keys1, peer_keys2,
          peer_u, peer_v, final_g, out):
    x1_dram = nc.dram_tensor("x1_scratch", (SEQ, D), F32, kind="Internal").ap()
    x2_dram = nc.dram_tensor("x2_scratch", (SEQ, D), F32, kind="Internal").ap()
    score_dram = nc.dram_tensor("score_scratch", (SEQ, SIDES * NK), F32, kind="Internal").ap()
    with ExitStack() as ctx:
        def sem(name):
            return ctx.enter_context(nc.semaphore(name))

        ident, tri, ones, bias, minus_half = constants(nc, ctx, sem)
        x2_t = ctx.enter_context(nc.sbuf_tensor("x2_t", [P, CH, SEQ], F32))
        keys_t = ctx.enter_context(nc.sbuf_tensor("keys_t", [P, SIDES, NK], F32))
        with ExitStack() as held:
            mixed = held.enter_context(nc.sbuf_tensor("mixed", [P, TILES, D], F32))
            qk_t = held.enter_context(nc.sbuf_tensor("qk_t", [P, HEADS, SEQ], F32))
            w_out_in = sem("w_out_in")
            with ExitStack() as heads:
                def hb(name, shape):
                    return heads.enter_context(nc.sbuf_tensor(name, shape, F32))

                sb_v = hb("sb_v", [P, TILES, D_SB])
                wq_t = hb("wq_t", [P, HEADS // 2, SEQ])
                wk_t = hb("wk_t", [P, KV, SEQ])
                sw_v = hb("sw_v", [P, TILES, KV * DH])
                project(nc, sem, x, norm1_g, w_in, ident, minus_half, bias, x2_t, mixed, qk_t, sb_v, wq_t, wk_t, sw_v)
                stick(nc, sem, ident, tri, ones, x2_t, qk_t, sb_v, mixed)
                window(nc, sem, swa_sinks, ident, bias, wq_t, wk_t, sw_v, mixed, w_out, qk_t, w_out_in)
            mix(nc, sem, x, sb_out_g, swa_out_g, qk_t, w_out_in, norm2_g, ident, minus_half, mixed, x1_dram, x2_dram, x2_t)
        spare = bias[:, 0:HEADS // 2, :].rearrange("p h n -> p (h n)")
        experts(nc, sem, ident, spare, keys_t, peer_keys1, peer_keys2, peer_w_q, x2_t, score_dram, x1_dram, x2_dram, peer_u, peer_v, final_g, out)


_INS = ["x", "norm1_g", "w_in", "sb_out_g", "swa_out_g", "swa_sinks", "w_out", "norm2_g", "peer_w_q", "peer_keys1",
        "peer_keys2", "peer_u", "peer_v", "final_g"]


def kernel(**inputs):
    import numpy as _np
    import concourse.bacc as _bacc
    from concourse import mybir as _mybir
    from concourse.bass_utils import run_bass_kernel_spmd as _run

    nc = _bacc.Bacc("TRN2", target_bir_lowering=False, num_devices=1)
    arrays, args = {}, []
    for name in _INS:
        a = _np.ascontiguousarray(inputs[name])
        if name != "final_g":
            a = a[0]
        arrays[f"in_{name}"] = a
        args.append(nc.dram_tensor(f"in_{name}", a.shape, _mybir.dt.from_np(a.dtype), kind="ExternalInput").ap())
    result = nc.dram_tensor("out_0", (SEQ, D), _mybir.dt.float32, kind="ExternalOutput").ap()
    build(nc, *args, result)
    r = _run(nc, [arrays], core_ids=[0])
    return r.results[0]["out_0"].reshape(1, SEQ, D)
```
